# Optimizing a Trainium2 kernel written in Bass

```python
import jax, jax.numpy as jnp
from jax import lax
import numpy as np

D_MODEL = 1024
BATCH = 1
SEQ = 256
DEPTH = 1

GRID_W = 64
NA_HEADS = 8
NA_HEAD_DIM = 64
NA_WIN_ROWS_MAX = 8
NA_WIN_COLS = 16
NA_WIDTH = NA_HEADS * NA_HEAD_DIM
MLA_HEADS = 8
MLA_Q_RANK = 256
MLA_KV_RANK = 128
MLA_NOPE_DIM = 64
MLA_ROPE_DIM = 32
MLA_V_DIM = 64
MLA_QK_DIM = MLA_NOPE_DIM + MLA_ROPE_DIM
MLA_WIDTH = MLA_HEADS * MLA_V_DIM
ROPE_THETA = 10000.0
ATTN_BLOCK = 128
IN_SPLITS = (NA_WIDTH, NA_WIDTH, NA_WIDTH, MLA_Q_RANK, MLA_KV_RANK, MLA_ROPE_DIM, D_MODEL, D_MODEL)
IN_COLS = 3 * NA_WIDTH + MLA_Q_RANK + MLA_KV_RANK + MLA_ROPE_DIM + 2 * D_MODEL
N_EXPERTS = 64
TOP_K = 8
N_GROUPS = 8
TOPK_GROUPS = 4
EXPERT_FF = 256
SHARED_FF = 256
ROUTED_SCALE = 2.5
MOE_CHUNK = 128
EPS = 1e-6
NEG_BIG = -1e30


def rms_norm(x, g):
    xf = x.astype(jnp.float32)
    y = xf * lax.rsqrt(jnp.mean(xf * xf, axis=-1, keepdims=True) + EPS)
    return (y * g.astype(jnp.float32)).astype(x.dtype)

def apply_rope(x, positions):
    half = x.shape[-1] // 2
    inv_freq = ROPE_THETA ** (-jnp.arange(half, dtype=jnp.float32) / half)
    ang = positions.astype(jnp.float32)[:, :, None, None] * inv_freq
    cos, sin = jnp.cos(ang), jnp.sin(ang)
    xf = x.astype(jnp.float32)
    x1, x2 = xf[..., :half], xf[..., half:]
    return jnp.concatenate([x1 * cos - x2 * sin, x2 * cos + x1 * sin], axis=-1).astype(x.dtype)

def neighbourhood_attention(q, k, v, rpb):
    B, S, H, Dh = q.shape
    R = S // GRID_W
    kh = min(NA_WIN_ROWS_MAX, R)
    to_grid = lambda t: t.reshape(B, R, GRID_W, H, Dh).transpose(0, 3, 1, 2, 4)
    qg, kg, vg = to_grid(q), to_grid(k), to_grid(v)
    rows = jnp.arange(R)
    row_start = jnp.clip(rows - kh // 2, 0, R - kh)
    key_rows = row_start[:, None] + jnp.arange(kh)[None, :]
    kb = kg[:, :, key_rows]
    vb = vg[:, :, key_rows]
    s = jnp.einsum('bhrqd,bhrjkd->bhrqjk', qg, kb).astype(jnp.float32) * (Dh ** -0.5)
    cols = jnp.arange(GRID_W)
    col_start = jnp.clip(cols - NA_WIN_COLS // 2, 0, GRID_W - NA_WIN_COLS)
    in_win = (cols[None, :] >= col_start[:, None]) & (cols[None, :] < col_start[:, None] + NA_WIN_COLS)
    dr = key_rows - rows[:, None]
    dc = jnp.clip(cols[None, :] - cols[:, None], -(NA_WIN_COLS - 1), NA_WIN_COLS - 1)
    bias = rpb[:, dr[:, None, :, None] + (NA_WIN_ROWS_MAX - 1),
               dc[None, :, None, :] + (NA_WIN_COLS - 1)]
    s = s + bias.astype(jnp.float32)[None]
    s = jnp.where(in_win[:, None, :], s, NEG_BIG)
    p = jax.nn.softmax(s.reshape(B, H, R, GRID_W, kh * GRID_W), axis=-1)
    p = p.reshape(B, H, R, GRID_W, kh, GRID_W).astype(v.dtype)
    o = jnp.einsum('bhrqjk,bhrjkd->bhrqd', p, vb)
    return o.transpose(0, 2, 3, 1, 4).reshape(B, S, H * Dh)

def blocked_full_attention(q, k, v):
    B, S, H, Dqk = q.shape
    Dv = v.shape[-1]
    nb = S // ATTN_BLOCK
    qb = q.reshape(B, nb, ATTN_BLOCK, H, Dqk).transpose(1, 0, 2, 3, 4)
    scale = Dqk ** -0.5

    def one_block(q_blk):
        s = jnp.einsum('bqhd,bkhd->bhqk', q_blk, k).astype(jnp.float32) * scale
        p = jax.nn.softmax(s, axis=-1).astype(v.dtype)
        return jnp.einsum('bhqk,bkhd->bqhd', p, v)

    o = lax.map(one_block, qb)
    return o.transpose(1, 0, 2, 3, 4).reshape(B, S, H * Dv)

def moe_ffn(h, w_router, e_bias, w_eg, w_eu, w_ed, w_sg, w_su, w_sd):
    B, S, D = h.shape
    t = h.reshape(-1, D)
    T = t.shape[0]
    scores = jax.nn.sigmoid((t @ w_router).astype(jnp.float32))
    sel = scores + e_bias.astype(jnp.float32)
    grp = sel.reshape(T, N_GROUPS, N_EXPERTS // N_GROUPS)
    grp_score = jnp.sum(lax.top_k(grp, 2)[0], axis=-1)
    _, gidx = lax.top_k(grp_score, TOPK_GROUPS)
    gmask = jnp.sum(jax.nn.one_hot(gidx, N_GROUPS, dtype=jnp.float32), axis=-2)
    emask = jnp.repeat(gmask, N_EXPERTS // N_GROUPS, axis=-1)
    sel = jnp.where(emask > 0, sel, -jnp.inf)
    _, eidx = lax.top_k(sel, TOP_K)
    w = jnp.take_along_axis(scores, eidx, axis=-1)
    w = w / jnp.sum(w, axis=-1, keepdims=True) * ROUTED_SCALE
    gates = jnp.sum(jax.nn.one_hot(eidx, N_EXPERTS, dtype=jnp.float32) * w[..., None], axis=-2)
    tc = t.reshape(-1, MOE_CHUNK, D)
    gc = gates.reshape(-1, MOE_CHUNK, N_EXPERTS).astype(t.dtype)

    def expert_chunk(args):
        xc, gch = args
        hg = jnp.einsum('cd,edf->cef', xc, w_eg)
        hu = jnp.einsum('cd,edf->cef', xc, w_eu)
        a = jax.nn.silu(hg) * hu * gch[..., None]
        return jnp.einsum('cef,efd->cd', a, w_ed)

    routed = lax.map(expert_chunk, (tc, gc)).reshape(T, D)
    shared = (jax.nn.silu(t @ w_sg) * (t @ w_su)) @ w_sd
    return (routed + shared).reshape(B, S, D)

def first_inputs(seed: int = 0) -> dict:
    key = jax.random.key(seed)
    ks = iter(jax.random.split(key, 32))
    f32 = jnp.float32
    nrm = lambda shape, s: jax.random.normal(next(ks), shape, f32) * s
    gain = lambda shape: 1.0 + 0.05 * jax.random.normal(next(ks), shape, f32)
    L, D, E, F = DEPTH, D_MODEL, N_EXPERTS, EXPERT_FF
    x = jax.random.normal(next(ks), (BATCH, SEQ, D), f32)
    c = jax.random.normal(next(ks), (BATCH, D), f32)
    positions = jnp.broadcast_to(jnp.arange(SEQ, dtype=jnp.int32)[None, :], (BATCH, SEQ))
    return {
        "x": x,
        "c": c,
        "positions": positions,
        "w_ada": nrm((L, D, 6 * D), 0.3 * D ** -0.5),
        "b_ada": nrm((L, 6 * D), 0.02),
        "g_norm1": gain((L, D)),
        "w_in": nrm((L, D, IN_COLS), D ** -0.5),
        "g_na_q": gain((L, NA_HEAD_DIM)),
        "g_na_k": gain((L, NA_HEAD_DIM)),
        "na_rpb": nrm((L, NA_HEADS, 2 * NA_WIN_ROWS_MAX - 1, 2 * NA_WIN_COLS - 1), 0.1),
        "g_q_lat": gain((L, MLA_Q_RANK)),
        "w_uq": nrm((L, MLA_Q_RANK, MLA_HEADS * MLA_QK_DIM), MLA_Q_RANK ** -0.5),
        "g_kv_lat": gain((L, MLA_KV_RANK)),
        "w_ukv": nrm((L, MLA_KV_RANK, MLA_HEADS * (MLA_NOPE_DIM + MLA_V_DIM)), MLA_KV_RANK ** -0.5),
        "g_mla_q": gain((L, MLA_QK_DIM)),
        "g_mla_k": gain((L, MLA_QK_DIM)),
        "w_proj_na": nrm((L, NA_WIDTH, D), NA_WIDTH ** -0.5),
        "w_proj_mla": nrm((L, MLA_WIDTH, D), MLA_WIDTH ** -0.5),
        "w_out": nrm((L, D, D), D ** -0.5),
        "g_norm2": gain((L, D)),
        "w_router": nrm((L, D, E), D ** -0.5),
        "e_bias": nrm((L, E), 0.01),
        "w_exp_gate": nrm((L, E, D, F), D ** -0.5),
        "w_exp_up": nrm((L, E, D, F), D ** -0.5),
        "w_exp_down": nrm((L, E, F, D), F ** -0.5),
        "w_sh_gate": nrm((L, D, SHARED_FF), D ** -0.5),
        "w_sh_up": nrm((L, D, SHARED_FF), D ** -0.5),
        "w_sh_down": nrm((L, SHARED_FF, D), SHARED_FF ** -0.5),
    }

def first_block(x, c, positions, w_ada, b_ada, g_norm1, w_in, g_na_q, g_na_k, na_rpb,
              g_q_lat, w_uq, g_kv_lat, w_ukv, g_mla_q, g_mla_k, w_proj_na, w_proj_mla,
              w_out, g_norm2, w_router, e_bias, w_exp_gate, w_exp_up, w_exp_down,
              w_sh_gate, w_sh_up, w_sh_down):
    B, S, D = x.shape
    split_at = list(np.cumsum(IN_SPLITS)[:-1])
    for l in range(DEPTH):
        mod = jax.nn.silu(c) @ w_ada[l] + b_ada[l]
        shift1, scale1, gate1, shift2, scale2, gate2 = jnp.split(mod[:, None, :], 6, axis=-1)

        h = rms_norm(x, g_norm1[l]) * (1.0 + scale1) + shift1
        proj = h @ w_in[l]
        na_q, na_k, na_v, q_lat, kv_lat, k_rot, gate_na, gate_mla = jnp.split(proj, split_at, axis=-1)

        qa = rms_norm(na_q.reshape(B, S, NA_HEADS, NA_HEAD_DIM), g_na_q[l])
        ka = rms_norm(na_k.reshape(B, S, NA_HEADS, NA_HEAD_DIM), g_na_k[l])
        va = na_v.reshape(B, S, NA_HEADS, NA_HEAD_DIM)
        y_na = neighbourhood_attention(qa, ka, va, na_rpb[l])

        qm = (rms_norm(q_lat, g_q_lat[l]) @ w_uq[l]).reshape(B, S, MLA_HEADS, MLA_QK_DIM)
        q_nope, q_rope = qm[..., :MLA_NOPE_DIM], apply_rope(qm[..., MLA_NOPE_DIM:], positions)
        kvm = (rms_norm(kv_lat, g_kv_lat[l]) @ w_ukv[l]).reshape(B, S, MLA_HEADS, MLA_NOPE_DIM + MLA_V_DIM)
        k_nope, vm = kvm[..., :MLA_NOPE_DIM], kvm[..., MLA_NOPE_DIM:]
        k_rope = jnp.broadcast_to(apply_rope(k_rot[:, :, None, :], positions), (B, S, MLA_HEADS, MLA_ROPE_DIM))
        qm = rms_norm(jnp.concatenate([q_nope, q_rope], axis=-1), g_mla_q[l])
        km = rms_norm(jnp.concatenate([k_nope, k_rope], axis=-1), g_mla_k[l])
        y_mla = blocked_full_attention(qm, km, vm)

        merged = (jax.nn.sigmoid(gate_na) * (y_na @ w_proj_na[l])
                  + jax.nn.sigmoid(gate_mla) * (y_mla @ w_proj_mla[l]))
        x = x + gate1 * (merged @ w_out[l])

        h2 = rms_norm(x, g_norm2[l]) * (1.0 + scale2) + shift2
        y_ffn = moe_ffn(h2, w_router[l], e_bias[l], w_exp_gate[l], w_exp_up[l], w_exp_down[l],
                        w_sh_gate[l], w_sh_up[l], w_sh_down[l])
        x = x + gate2 * y_ffn
    return x


DEPTH_2 = 2

CTX_LEN = 256
CHUNK = 128
A_HEADS = 4
A_HEAD_DIM = 128
A_W = A_HEADS * A_HEAD_DIM
B_GROUPS = 4
B_GROUP_DIM = 128
B_W = B_GROUPS * B_GROUP_DIM
AB_IN = 3 * A_W + 2 * B_W
AB_OUT = A_W + B_W
C_HEADS = 16
C_KV_HEADS = 4
C_GROUP = C_HEADS // C_KV_HEADS
C_HEAD_DIM = 64
C_Q_W = C_HEADS * C_HEAD_DIM
C_KV_W = C_KV_HEADS * C_HEAD_DIM
C_IN = 2 * C_Q_W + 2 * C_KV_W
WINDOW = 128
Q_BLOCK = 128
ROPE_BASE = 10000.0
NORM_EPS = 1e-6
NEG_INF = -1e30
N_EVEN = (DEPTH_2 + 1) // 2
N_ODD = DEPTH_2 // 2


def rms_norm_2(x, g):
    xf = x.astype(jnp.float32)
    y = xf * lax.rsqrt(jnp.mean(xf * xf, axis=-1, keepdims=True) + NORM_EPS)
    return (y * g.astype(jnp.float32)).astype(x.dtype)

def layer_norm(x, g):
    xf = x.astype(jnp.float32)
    mu = jnp.mean(xf, axis=-1, keepdims=True)
    xc = xf - mu
    y = xc * lax.rsqrt(jnp.mean(xc * xc, axis=-1, keepdims=True) + NORM_EPS)
    return (y * g.astype(jnp.float32)).astype(x.dtype)

def adaln(cond, w, b):
    m = jax.nn.silu(cond) @ w + b
    return jnp.split(m, 3, axis=-1)

def rope_1d(x, pos):
    nf = x.shape[-1] // 2
    inv = ROPE_BASE ** (-jnp.arange(nf, dtype=jnp.float32) / nf)
    ang = pos.astype(jnp.float32)[:, None] * inv[None, :]
    cos = jnp.cos(ang)[None, :, None, :].astype(x.dtype)
    sin = jnp.sin(ang)[None, :, None, :].astype(x.dtype)
    x1, x2 = x[..., :nf], x[..., nf:]
    return jnp.concatenate([x1 * cos - x2 * sin, x2 * cos + x1 * sin], axis=-1)

def rope_2d(x, row, col):
    half = x.shape[-1] // 2
    return jnp.concatenate([rope_1d(x[..., :half], row), rope_1d(x[..., half:], col)], axis=-1)

def sink_softmax(scores, sink):
    s = jnp.broadcast_to(sink, scores.shape[:-1] + (1,))
    p = jax.nn.softmax(jnp.concatenate([s, scores], axis=-1), axis=-1)
    return p[..., 1:]

def mixer_ab(h, w_in, v_g, s_w, s_b, w_out):
    bsz, L, _ = h.shape
    z = h @ w_in
    u, v, g_a, x_b, g_b = jnp.split(z, [A_W, 2 * A_W, 3 * A_W, 3 * A_W + B_W], axis=-1)
    v = layer_norm(v, v_g).reshape(bsz, L // CHUNK, CHUNK, A_HEADS, A_HEAD_DIM)
    sv = jnp.einsum('bnphc,hqp->bnqhc', v, s_w) + s_b.T[:, :, None]
    y_a = u * sv.reshape(bsz, L, A_W) * jax.nn.silu(g_a)
    xb = x_b.reshape(bsz, L, B_GROUPS, B_GROUP_DIM).astype(jnp.float32)
    f = jnp.real(jnp.fft.fft2(xb, axes=(1, 3), norm='ortho')).astype(h.dtype).reshape(bsz, L, B_W)
    y_b = f * jax.nn.silu(g_b)
    return jnp.concatenate([y_a, y_b], axis=-1) @ w_out

def split_c(z):
    return jnp.split(z, [C_Q_W, C_Q_W + C_KV_W, C_Q_W + 2 * C_KV_W], axis=-1)

def window_attention(q, k, v, k_ctx, v_ctx, sink):
    bsz, S, _, hd = q.shape
    qg = q.reshape(bsz, S, C_KV_HEADS, C_GROUP, hd)
    pad = ((0, 0), (WINDOW, WINDOW), (0, 0), (0, 0))
    kp, vp = jnp.pad(k, pad), jnp.pad(v, pad)
    kb_len = Q_BLOCK + 2 * WINDOW
    scale = hd ** -0.5
    sink_b = sink.reshape(C_KV_HEADS, C_GROUP).astype(jnp.float32)[None, :, :, None, None]

    def one_block(n):
        start = n * Q_BLOCK
        qb = lax.dynamic_slice_in_dim(qg, start, Q_BLOCK, axis=1)
        kb = lax.dynamic_slice_in_dim(kp, start, kb_len, axis=1)
        vb = lax.dynamic_slice_in_dim(vp, start, kb_len, axis=1)
        qpos = start + jnp.arange(Q_BLOCK)
        kpos = start - WINDOW + jnp.arange(kb_len)
        valid = (jnp.abs(qpos[:, None] - kpos[None, :]) <= WINDOW) & (kpos[None, :] >= 0) & (kpos[None, :] < S)
        s_win = jnp.einsum('bqkgd,bjkd->bkgqj', qb, kb).astype(jnp.float32) * scale
        s_win = jnp.where(valid, s_win, NEG_INF)
        s_ctx = jnp.einsum('bqkgd,bjkd->bkgqj', qb, k_ctx).astype(jnp.float32) * scale
        p = sink_softmax(jnp.concatenate([s_ctx, s_win], axis=-1), sink_b)
        vals = jnp.concatenate([v_ctx, vb], axis=1)
        return jnp.einsum('bkgqj,bjkd->bqkgd', p.astype(v.dtype), vals)

    out = lax.map(one_block, jnp.arange(S // Q_BLOCK))
    return jnp.moveaxis(out, 0, 1).reshape(bsz, S, C_Q_W)

def context_attention(q, k, v, sink):
    bsz, L, _, hd = q.shape
    qg = q.reshape(bsz, L, C_KV_HEADS, C_GROUP, hd)
    s = jnp.einsum('bqkgd,bjkd->bkgqj', qg, k).astype(jnp.float32) * hd ** -0.5
    sink_b = sink.reshape(C_KV_HEADS, C_GROUP).astype(jnp.float32)[None, :, :, None, None]
    p = sink_softmax(s, sink_b)
    o = jnp.einsum('bkgqj,bjkd->bqkgd', p.astype(v.dtype), v)
    return o.reshape(bsz, L, C_Q_W)

def second_inputs(seed: int = 0) -> dict:
    key = jax.random.key(seed)
    ks = jax.random.split(key, 16)

    def nrm(k, shape, s):
        return jax.random.normal(k, shape, jnp.float32) * s

    return {
        'x': nrm(ks[0], (BATCH, SEQ, D_MODEL), 1.0),
        'c': nrm(ks[1], (BATCH, D_MODEL), 1.0),
        'ctx': nrm(ks[2], (BATCH, CTX_LEN, D_MODEL), 1.0),
        'c_ctx': nrm(ks[3], (D_MODEL,), 1.0),
        'norm_g': 1.0 + nrm(ks[4], (DEPTH_2, D_MODEL), 0.02),
        'ada_w': nrm(ks[5], (DEPTH_2, D_MODEL, 3 * D_MODEL), 0.5 * D_MODEL ** -0.5),
        'ada_b': nrm(ks[6], (DEPTH_2, 3 * D_MODEL), 0.02),
        'w_in_ab': nrm(ks[7], (N_EVEN, D_MODEL, AB_IN), D_MODEL ** -0.5),
        'v_norm_g': 1.0 + nrm(ks[8], (N_EVEN, A_W), 0.02),
        'spatial_w': nrm(ks[9], (N_EVEN, A_HEADS, CHUNK, CHUNK), CHUNK ** -0.5),
        'spatial_b': 1.0 + nrm(ks[10], (N_EVEN, A_HEADS, CHUNK), 0.02),
        'w_out_ab': nrm(ks[11], (N_EVEN, AB_OUT, D_MODEL), AB_OUT ** -0.5),
        'w_in_c': nrm(ks[12], (N_ODD, D_MODEL, C_IN), D_MODEL ** -0.5),
        'sink_logit': nrm(ks[13], (N_ODD, C_HEADS), 0.5),
        'w_out_c': nrm(ks[14], (N_ODD, C_Q_W, D_MODEL), C_Q_W ** -0.5),
        'final_g': 1.0 + nrm(ks[15], (D_MODEL,), 0.02),
    }

def second_block(x, c, ctx, c_ctx, norm_g, ada_w, ada_b, w_in_ab, v_norm_g, spatial_w, spatial_b,
              w_out_ab, w_in_c, sink_logit, w_out_c, final_g):
    bsz, S, _ = x.shape
    rows = S // GRID_W
    row = jnp.repeat(jnp.arange(rows), GRID_W)
    col = jnp.tile(jnp.arange(GRID_W), rows)

    for layer in range(DEPTH_2):
        need_ctx_out = layer < DEPTH_2 - 1
        shift, scale, gate = adaln(c[:, None, :], ada_w[layer], ada_b[layer])
        shift_c, scale_c, gate_c = adaln(c_ctx, ada_w[layer], ada_b[layer])
        h = rms_norm_2(x, norm_g[layer]) * (1.0 + scale) + shift
        if layer % 2 == 0:
            i = layer // 2
            y = mixer_ab(h, w_in_ab[i], v_norm_g[i], spatial_w[i], spatial_b[i], w_out_ab[i])
            if need_ctx_out:
                hc = rms_norm_2(ctx, norm_g[layer]) * (1.0 + scale_c) + shift_c
                yc = mixer_ab(hc, w_in_ab[i], v_norm_g[i], spatial_w[i], spatial_b[i], w_out_ab[i])
                ctx = ctx + gate_c * yc
            x = x + gate * y
        else:
            i = layer // 2
            w_in = w_in_c[i]
            hc = rms_norm_2(ctx, norm_g[layer]) * (1.0 + scale_c) + shift_c
            q, k, v, g = split_c(h @ w_in)
            q = rope_2d(q.reshape(bsz, S, C_HEADS, C_HEAD_DIM), row, col)
            k = rope_2d(k.reshape(bsz, S, C_KV_HEADS, C_HEAD_DIM), row, col)
            v = v.reshape(bsz, S, C_KV_HEADS, C_HEAD_DIM)
            Lc = ctx.shape[1]
            if need_ctx_out:
                q_c, k_c, v_c, g_c = split_c(hc @ w_in)
            else:
                k_c, v_c = jnp.split(hc @ w_in[:, C_Q_W:C_Q_W + 2 * C_KV_W], 2, axis=-1)
            k_c = k_c.reshape(bsz, Lc, C_KV_HEADS, C_HEAD_DIM)
            v_c = v_c.reshape(bsz, Lc, C_KV_HEADS, C_HEAD_DIM)
            o = window_attention(q, k, v, k_c, v_c, sink_logit[i])
            y = (o * jax.nn.silu(g)) @ w_out_c[i]
            if need_ctx_out:
                o_c = context_attention(q_c.reshape(bsz, Lc, C_HEADS, C_HEAD_DIM), k_c, v_c, sink_logit[i])
                ctx = ctx + gate_c * ((o_c * jax.nn.silu(g_c)) @ w_out_c[i])
            x = x + gate * y

    return rms_norm_2(x, final_g)


def setup_inputs(seed=0):
    out = dict(first_inputs(seed))
    for name, value in second_inputs(seed + 1).items():
        if name != "x":
            out[name + "_2"] = value
    return out


def reference(
    x, c, positions, w_ada, b_ada, g_norm1, w_in, g_na_q, g_na_k, na_rpb, g_q_lat, w_uq,
    g_kv_lat, w_ukv, g_mla_q, g_mla_k, w_proj_na, w_proj_mla, w_out, g_norm2, w_router, e_bias,
    w_exp_gate, w_exp_up, w_exp_down, w_sh_gate, w_sh_up, w_sh_down, c_2, ctx_2, c_ctx_2,
    norm_g_2, ada_w_2, ada_b_2, w_in_ab_2, v_norm_g_2, spatial_w_2, spatial_b_2, w_out_ab_2,
    w_in_c_2, sink_logit_2, w_out_c_2, final_g_2,
):
    x = first_block(
        x, c, positions, w_ada, b_ada, g_norm1, w_in, g_na_q, g_na_k, na_rpb, g_q_lat, w_uq,
        g_kv_lat, w_ukv, g_mla_q, g_mla_k, w_proj_na, w_proj_mla, w_out, g_norm2, w_router,
        e_bias, w_exp_gate, w_exp_up, w_exp_down, w_sh_gate, w_sh_up, w_sh_down,
    )
    return second_block(
        x, c_2, ctx_2, c_ctx_2, norm_g_2, ada_w_2, ada_b_2, w_in_ab_2, v_norm_g_2, spatial_w_2,
        spatial_b_2, w_out_ab_2, w_in_c_2, sink_logit_2, w_out_c_2, final_g_2,
    )


_drawn_inputs = setup_inputs


def setup_inputs(seed=0):
    import zlib

    import numpy as np

    out = dict(_drawn_inputs(seed))
    spreads = {}
    factors = {'g_norm1': 8.0,
     'g_na_q': 8.0,
     'g_na_k': 8.0,
     'na_rpb': 8.0,
     'g_q_lat': 8.0,
     'w_uq': 3.748,
     'g_kv_lat': 8.0,
     'g_mla_q': 8.0,
     'g_mla_k': 8.0,
     'ctx_2': 4.189,
     'norm_g_2': 7.477,
     'ada_b_2': 3.0,
     'v_norm_g_2': 8.0,
     'spatial_b_2': 8.0,
     'sink_logit_2': 8.0,
     'final_g_2': 2.884}
    for name, (base, spread) in spreads.items():
        noise = np.random.default_rng([zlib.crc32(name.encode()), seed]).standard_normal(out[name].shape)
        drawn = base * np.exp(spread * noise) if base else spread * noise
        out[name] = __import__('jax').numpy.asarray(drawn.astype(out[name].dtype))
    for name, factor in factors.items():
        out[name] = (out[name] * factor).astype(out[name].dtype)
    return out
```

```python
from contextlib import ExitStack

import numpy as np
import concourse.bass as bass
from concourse import mybir

ALU = mybir.AluOpType
ACT = mybir.ActivationFunctionType
F32 = mybir.dt.float32
BF16 = mybir.dt.bfloat16
I32 = mybir.dt.int32
U32 = mybir.dt.uint32
AXX = mybir.AxisListType.X

P = 128
D = 1024
KT = D // P
T = 256
TT = T // P
E = 64
TOPK = 8
GROUPS = 8
TOPG = 4
FF = 256
SLOTS = 96
ROUNDS = (T + SLOTS - 1) // SLOTS
SLAB = 2048
RING = 9
PER_E = 3
UN = RING // PER_E
TURNS = E // UN
EPS = 1e-6
NEG = -1e30
TWO_PI = 2 * np.pi
RUN = 5 * 31 + 64

C_WIDTHS = dict(fold=2, ident=P, bones=P, perm96=96, tri=P, iota=SLOTS, namask=64, invf=1, gtri=64, eoff=64)
C2_WIDTHS = dict(perm128=P, dft_c=256, dft_l=4 * 256, cos2=256, sin2=256, wmask=2 * 512)
V_WIDTHS = dict(c=8, c2=16, b_ada=48, g1=8, gq=1, gk=1, gql=2, gkv=1, gmq=1, gmk=1, g2=8, ng2=16,
                b2=48, vg=4, fg=8, ebias=64, sink=16, sb=512)


def offsets(widths):
    at, out = 0, {}
    for k, w in widths.items():
        out[k] = (at, at + w)
        at += w
    return out, at


C_AT, C_W = offsets(C_WIDTHS)
C2_AT, C2_W = offsets(C2_WIDTHS)
V_AT, V_W = offsets(V_WIDTHS)


def build(nc, xT_d, consts_d, consts2_d, vecs_d, pos_d, rpb_d, spat_d, router_d, slabs_d, exp_d, out_d, rows_d, more_d):
    with ExitStack() as ctx:
        def sb(name, shape, dt=F32):
            return ctx.enter_context(nc.sbuf_tensor(name, shape, dt))

        sems = {}

        def S(name):
            if name not in sems:
                sems[name] = ctx.enter_context(nc.semaphore(name))
            return sems[name]

        ring = sb("ring", [P, RING, SLAB])
        xT = sb("resid", [P, KT, 2 * T])
        hT = sb("hT", [P, KT, 2 * T])
        cs = sb("cs", [P, C_W])
        ve = sb("ve", [P, V_W])
        silc = sb("silc", [P, 8, 32])
        silc2 = sb("silc2", [P, 8, 32])
        quarters = sb("quarters", [P, 2, 256])
        mod1 = sb("mod1", [P, 48])
        mod2 = sb("mod2", [P, 48, 2])
        gs = sb("gs", [P, 8, 2])
        ones = sb("ones", [P, P])
        rstd = sb("rstd", [P, 512])
        stat = sb("stat", [P, 512])
        arena = sb("arena", [P, 17632])

        def ar(at, n, *dims, parts=P, lo=0):
            v = arena[lo:lo + parts, at:at + n]
            if len(dims) == 2:
                v = v.rearrange("p (a b) -> p a b", a=dims[0])
            if len(dims) == 3:
                v = v.rearrange("p (a b c) -> p a b c", a=dims[0], b=dims[1])
            return v

        def cc(name, a=0, b=None):
            src, at = (cs, C_AT) if name in C_AT else (cs2, C2_AT)
            lo, hi = at[name]
            return src[:, lo + a:(hi if b is None else lo + b)]

        def vv(name, a=0, b=None):
            lo, hi = V_AT[name]
            return ve[:, lo + a:(hi if b is None else lo + b)]

        qk = ar(0, 2048, 8, 256)
        vna = ar(2048, 1024, 2, 512)
        lat = ar(3072, 1024, 4, 256)
        sgate = ar(4096, 4096, 16, 256)
        qm = ar(8192, 2048, 8, 256)
        km = ar(10240, 2048, 8, 256)
        vm = ar(12288, 1024, 2, 512)
        yT = qk
        merged = qm
        var = hT[:, 4:8, :].rearrange("p a b -> p (a b)")
        sqt = ar(13312, 1024, 2, 512)
        braw = ar(14336, 8 * RUN, 8, RUN)
        bmask = ar(16096, 1024, 2, 512)
        rope_c = ar(17120, 256)
        rope_s = ar(17376, 256)
        pr = sb("pr", [P, 2, 1024])
        pT = sb("pT", [P, 2, 1024])
        att = sb("att", [P, 4, 8])
        small = pT[:, :, :].rearrange("p a b -> p (a b)")
        hbf = arena[:, 0:3072].bitcast(BF16).rearrange("p (q t d) -> p q t d", q=3, t=2)
        htok = ar(3072, 1024, 2, 512)
        xg = ar(4096, 3 * 9 * SLOTS, 3, 9 * SLOTS)
        selb = ar(6688, 3 * SLOTS).bitcast(BF16).rearrange("p (u t s) -> p u t s", u=3, t=2)
        selg = ar(6976, 3 * 2 * SLOTS, 3, 2, SLOTS)
        sgt = ar(7552, 3 * 2 * SLOTS, 3, 2 * SLOTS)
        upt = ar(8128, 3 * 2 * SLOTS, 3, 2 * SLOTS)
        aT = ar(8704, 3 * 2 * SLOTS, 3, 2 * SLOTS)
        yo = ar(9280, 3 * 1024, 3, 1024)
        shg = ar(12352, 512, 2, 256)
        shu = ar(12864, 512, 2, 256)
        gat = ar(4096, 3 * 1024, 3, 1024)
        acc = ar(7168, 2 * 1024, 2, 1024)
        lg = small[:, 0:128].rearrange("p (a b) -> p a b", a=2)
        sel = small[:, 128:256].rearrange("p (a b) -> p a b", a=2)
        m8 = small[:, 256:384].rearrange("p (a g b) -> p a g b", a=2, g=8)
        gsc = small[:, 384:400].rearrange("p (a b) -> p a b", a=2)
        cmpa = small[:, 400:528].rearrange("p (a g b) -> p a g b", a=2, g=8)
        cmpb = small[:, 528:656].rearrange("p (a g b) -> p a g b", a=2, g=8)
        gmk = small[:, 656:672].rearrange("p (a b) -> p a b", a=2)
        gpen = small[:, 672:688].rearrange("p (a b) -> p a b", a=2)
        top = small[:, 688:704].rearrange("p (a b) -> p a b", a=2)
        rep = small[:, 704:832].rearrange("p (a b) -> p a b", a=2)
        mask = small[:, 832:960].rearrange("p (a b) -> p a b", a=2)
        gates = small[:, 960:1092].rearrange("p (a b) -> p a b", a=2)
        posm = small[:, 1092:1224].rearrange("p (a b) -> p a b", a=2)
        pos1 = small[:, 1224:1352].rearrange("p (a b) -> p a b", a=2)
        rowf = small[:, 1352:1480].rearrange("p (a b) -> p a b", a=2)
        den = small[:, 1480:1484]
        ridx = small[:, 1484:1500].bitcast(U32).rearrange("p (a b) -> p a b", a=2)
        rtop = small[:, 1500:1516].rearrange("p (a b) -> p a b", a=2)
        ridx2 = small[:, 1520:1536].bitcast(U32).rearrange("p (a b) -> p a b", a=2)
        near = small[:, 400:528].rearrange("p (a b) -> p a b", a=2)
        flag_f = small[:, 1516:1517]
        flag = small[:, 1517:1518].bitcast(I32)
        wr = sb("wr", [P, 8, 64])
        zrow = sb("zrow", [P, D // P])
        mark = sb("mark", [1, 32])
        zT = ar(0, 8192, 16, 512)
        vtok = ar(8192, 2048, 4, 512)
        fa = ar(10240, 1024, 2, 512)
        smt = ar(11264, 1024, 2, 512)
        cs2 = ar(13376, C2_W)
        spat = ar(13376 + C2_W, 512, 4, 128)
        bn = ar(12800, 64, 4, 16)
        q2 = ar(0, 2048, 8, 256)
        g2s = ar(2048, 2048, 8, 256)
        k2 = ar(4096, 1024, 2, 512)
        v2 = ar(5120, 1024, 4, 256)
        o2 = ar(6144, 2048, 8, 256)
        rt1 = ar(8192, 1024, 4, 256)
        rt2 = ar(9216, 1024, 4, 256)
        outT = ar(0, 2048, 8, 256)

        bank = [ctx.enter_context(nc.psum_tensor(f"bank{b}", [P, 512], F32)) for b in range(8)]
        psum_full = [S(f"psum_full{b}") for b in range(8)]
        psum_done = [S(f"psum_done{b}") for b in range(8)]
        uses = [0] * 8
        place = {}

        def full(eng, name):
            b, n = place[name]
            eng.wait_ge(psum_full[b], n + 1)

        def done(eng, name):
            b, n = place[name]
            eng.wait_ge(psum_done[b], n + 1)

        def bk(name):
            return bank[place[name][0]]

        def emptied(ins, name):
            ins.then_inc(psum_done[place[name][0]], 1)

        slab_in = [S(f"slab_in{k}") for k in range(RING)]
        slabs = []
        slab_end = []

        def na_head(h):
            b = 64 * (h % 2)
            return dict(q=lambda t: qk[b:b + 64, h // 2, t * P:(t + 1) * P], k=[qk[b:b + 64, 4 + h // 2, :]],
                        v=lambda j: vna[:, j, 64 * h:64 * h + 64], o=b)

        def mla_head(h):
            return dict(q=lambda t: qm[0:96, h, t * P:(t + 1) * P], k=[km[0:96, h, :]],
                        v=lambda j: vm[:, j, 64 * h:64 * h + 64], o=64 * (h % 2))

        def c_head(h):
            b, g = 64 * (h % 2), h // 8
            return dict(q=lambda t: q2[b:b + 64, h // 2, t * P:(t + 1) * P], k=[k2[b:b + 64, g, :]],
                        v=lambda j: v2[:, j, 128 * g + b:128 * g + b + 64], o=b)

        KINDS = dict(na=(8, na_head, 256), mla=(8, mla_head, 256), c=(16, c_head, 512))

        def probs(kind, h):
            if kind == "c":
                return ar(9216 + 1024 * (h % 4), 1024)
            return pr[:, (h % 4) // 2, 512 * (h % 2):512 * (h % 2) + 512]

        fillers = [("ada1", j) for j in range(8, 24)] + [("ada2", j) for j in range(24)]
        FILL = {("na", i): fillers[6 * i:6 * i + 6] for i in range(4)}
        FILL.update({("mla", i): fillers[24 + 4 * i:28 + 4 * i] for i in range(4)})

        moe0 = [0] * 8
        MOE_BANKS = dict(G0=0, G1=1, Hg=2, Hu=3, D0=4, D1=5)

        block = ctx.enter_context(nc.Block())

        @block.tensor
        def _(pe):
            mmul = nc.tensor.matmul

            def open_group(name, b):
                if uses[b]:
                    pe.wait_ge(psum_done[b], uses[b])
                place[name] = (b, uses[b])
                uses[b] += 1
                return bank[b]

            def close_group(ins, name):
                ins.then_inc(psum_full[place[name][0]], 1)

            def take_slab(src):
                n = len(slabs)
                slabs.append(src)
                slab_end.append(None)
                pe.wait_ge(slab_in[n % RING], 16 * (n // RING + 1))
                return ring[:, n % RING, :], n

            def ada_slab(which, j):
                w, n = take_slab((which, j))
                w = w.rearrange("p (k c) -> p k c", k=8)
                name = (which, j, "quarters")
                o = open_group(name, 6)
                for kk in range(2):
                    for g in range(4):
                        mm = mmul(o[32 * g:32 * g + 32, 0:256], (silc if which == "ada1" else silc2)[:, 4 * kk + g, :],
                                  w[:, 4 * kk + g, :], start=(kk == 0), stop=(kk == 1))
                close_group(mm, name)
                slab_end[n] = name
                if ada_prev:
                    ada_fold(*ada_prev.pop())
                ada_prev.append((which, j))

            ada_prev = []

            def ada_fold(which, j):
                done(pe, (which, j, "quarters"))
                o = open_group((which, j), 7)
                width = 1 if which == "ada1" else 2
                for t in range(2):
                    mm = mmul(o[:, t * width:(t + 1) * width], quarters[:, j % 2, t * P:(t + 1) * P], cc("fold", 0, width),
                              start=True, stop=True)
                close_group(mm, (which, j))

            def rms_sums(name, b, n_tok, tiles=KT, src=None):
                o = open_group(name, b)
                for k in range(tiles):
                    mm = mmul(o[:, 0:n_tok], ones[:], hT[:, k, 0:n_tok] if src is None else src(k),
                              start=(k == 0), stop=(k == tiles - 1))
                close_group(mm, name)

            def t_tiles(tag, src, n_tiles, b, n_tok, rows=P, lo=0):
                w, n = take_slab(src)
                w = w.rearrange("p (k c) -> p k c", k=8)
                for t in range(n_tiles):
                    name = (tag, t)
                    o = open_group(name, b[t % len(b)])
                    for k in range(KT):
                        mm = mmul(o[:, 0:n_tok], w[:, k, t * P:(t + 1) * P], hT[:, k, 0:n_tok],
                                  start=(k == 0), stop=(k == KT - 1))
                    close_group(mm, name)
                slab_end[n] = name

            def tok_tiles(tag, src, toks, b):
                w, n = take_slab(src)
                w = w.rearrange("p (k c) -> p k c", k=8)
                for t in range(toks):
                    name = (tag, t)
                    o = open_group(name, b[t % len(b)])
                    for k in range(KT):
                        mm = mmul(o[:, 0:256], hT[:, k, t * P:(t + 1) * P], w[:, k, :],
                                  start=(k == 0), stop=(k == KT - 1))
                    close_group(mm, name)
                slab_end[n] = name

            def attention(kind):
                n_heads, head, nk = KINDS[kind]
                per = nk // 256

                def scores(i):
                    for t in range(TT):
                        for h in (2 * i, 2 * i + 1):
                            hd = head(h)
                            if nk == 256:
                                name = (kind, "s", h)
                                if t == 0:
                                    open_group(name, h % 2)
                                mm = mmul(bk(name)[:, 256 * t:256 * t + 256], hd["q"](t), hd["k"][0], start=True, stop=True)
                                if t == 1:
                                    close_group(mm, name)
                            else:
                                name = (kind, "s", h, t)
                                o = open_group(name, (0 if h % 2 == 0 else 6) + t)
                                close_group(mmul(o[:, :], hd["q"](t), hd["k"][0], start=True, stop=True), name)

                def turn(h):
                    pe.wait_ge(S(kind + "_probs"), h + 1)
                    for j in range(per):
                        name = (kind, "t", h, j)
                        o = open_group(name, 2 + (h % 2 if per == 1 else j))
                        for kt in range(2):
                            for t in range(TT):
                                at = t * nk + (2 * j + kt) * P
                                mm = nc.tensor.transpose(o[:, 256 * kt + P * t:256 * kt + P * t + P],
                                                         probs(kind, h)[:, at:at + P], cc("ident"))
                        close_group(mm, name)

                def values(i):
                    name = (kind, "o", i)
                    o = open_group(name, 4 + i % 2)
                    for h in (2 * i, 2 * i + 1):
                        for j in range(per):
                            done(pe, (kind, "t", h, j))
                    for kt in range(2 * per):
                        for h in (2 * i, 2 * i + 1):
                            hd = head(h)
                            mm = mmul(o[hd["o"]:hd["o"] + 64, 0:256], hd["v"](kt), pT[:, h % 2, 256 * kt:256 * kt + 256],
                                      start=(kt == 0), stop=(kt == 2 * per - 1))
                    close_group(mm, name)

                scores(0)
                for i in range(n_heads // 2):
                    if 2 * i + 2 < n_heads:
                        scores(i + 1)
                    for f in FILL.get((kind, i), []):
                        ada_slab(*f)
                    turn(2 * i)
                    turn(2 * i + 1)
                    values(i)

            pe.wait_ge(S("silu_c"), 1)
            pe.wait_ge(S("const_in"), 48)
            for j in range(8):
                ada_slab("ada1", j)
            ada_fold(*ada_prev.pop())
            pe.wait_ge(S("ones_set"), 1)
            pe.wait_ge(S("const_in"), 48)
            pe.wait_ge(S("sq1"), 1)
            rms_sums("sum1", 0, 256)
            pe.wait_ge(S("h1"), 8)
            for s in range(4):
                t_tiles(f"qk{s}", ("in", s), 2, [1, 2], 256)
                for t in range(2):
                    j = 2 * s + t
                    pe.wait_ge(S("sq_qk"), j + 1)
                    o = open_group(("qkn", j), 3 + j % 2)
                    close_group(mmul(o[:, 0:256], cc("bones"), sqt[:, j % 2, 0:256], start=True, stop=True), ("qkn", j))
            for s in range(2):
                tok_tiles(f"vna{s}", ("in", 4 + s), 2, [1, 2])
            t_tiles("ql", ("in", 6), 2, [1, 2], 256)
            w, n = take_slab(("in", 7))
            w = w.rearrange("p (k c) -> p k c", k=8)
            o = open_group("kvl", 3)
            for k in range(KT):
                mm = mmul(o[:, 0:256], w[:, k, 0:P], hT[:, k, 0:256], start=(k == 0), stop=(k == KT - 1))
            close_group(mm, "kvl")
            o = open_group("krot", 4)
            for k in range(KT):
                mm = mmul(o[64:96, 0:256], w[:, k, P:P + 32], hT[:, k, 0:256], start=(k == 0), stop=(k == KT - 1))
            close_group(mm, "krot")
            slab_end[n] = "krot"
            pe.wait_ge(S("sq_ql"), 2)
            rms_sums("sum_ql", 5, 256, tiles=2, src=lambda k: sqt[:, k, 0:256])
            pe.wait_ge(S("sq_kvl"), 1)
            rms_sums("sum_kvl", 6, 256, tiles=1, src=lambda k: sqt[:, k, 256:512])
            for s in range(8):
                t_tiles(f"gt{s}", ("in", 8 + s), 2, [1, 2], 256)
            pe.wait_ge(S("qln"), 2)
            w, n = take_slab(("uq", 0))
            w = w[:, 0:1536].rearrange("p (k c) -> p k c", k=2)
            for g in range(4):
                o = open_group(("uq", g), 1 + g % 2)
                for h in range(2):
                    for k in range(2):
                        mm = mmul(o[0:96, 256 * h:256 * h + 256], w[:, k, 96 * (2 * g + h):96 * (2 * g + h) + 96],
                                  lat[:, k, :], start=(k == 0), stop=(k == 1))
                close_group(mm, ("uq", g))
            slab_end[n] = ("uq", 3)
            pe.wait_ge(S("kvn"), 1)
            w, n = take_slab(("ukv", 0))
            for g in range(4):
                o = open_group(("uk", g), 1 + g % 2)
                for h in range(2):
                    mm = mmul(o[0:64, 256 * h:256 * h + 256], w[:, 64 * (2 * g + h):64 * (2 * g + h) + 64],
                              lat[:, 2, :], start=True, stop=True)
                close_group(mm, ("uk", g))
            for t in range(2):
                o = open_group(("uv", t), 1 + t % 2)
                close_group(mmul(o[:, :], lat[:, 2, t * P:(t + 1) * P], w[:, 512:1024], start=True, stop=True), ("uv", t))
            slab_end[n] = ("uv", 1)
            pe.wait_ge(S("qk_ready"), 8)
            attention("na")
            for g in range(4):
                done(pe, ("uq", g))
                o = open_group(("qsw", g), 1 + g % 2)
                close_group(mmul(o[0:96, :], cs[0:96, C_AT["perm96"][0]:C_AT["perm96"][1]],
                                 qm[0:96, 2 * g:2 * g + 2, :].rearrange("p a b -> p (a b)"), start=True, stop=True), ("qsw", g))
            pe.wait_ge(S("kr_zero"), 1)
            done(pe, "krot")
            o = open_group("ksw", 3)
            close_group(mmul(o[0:96, 0:256], cs[0:96, C_AT["perm96"][0]:C_AT["perm96"][1]], lat[0:96, 3, :],
                             start=True, stop=True), "ksw")
            for g in range(8):
                pe.wait_ge(S("sq_m"), g + 1)
                o = open_group(("msum", g), 1 + g % 2)
                close_group(mmul(o[0:96, :], ones[0:96, 0:96], sqt[0:96, g % 2, :], start=True, stop=True), ("msum", g))
            pe.wait_ge(S("m_ready"), 8)
            attention("mla")
            ada_fold(*ada_prev.pop())
            done(pe, ("na", "o", 3))
            done(pe, ("mla", "o", 3))
            for half in range(2):
                wa, na = take_slab(("pna", half))
                wb, nb = take_slab(("pmla", half))
                for t in range(4):
                    d = 4 * half + t
                    for tag, w, y0, b in (("pn", wa, 0, 0), ("pm", wb, 4, 1)):
                        o = open_group((tag, d), b + 2 * (d % 2))
                        for k in range(4):
                            mm = mmul(o[:, 0:256], w[:, 512 * k + P * t:512 * k + P * t + P], yT[:, y0 + k, :],
                                      start=(k == 0), stop=(k == 3))
                        close_group(mm, (tag, d))
                slab_end[na] = slab_end[nb] = ("pm", d)
            pe.wait_ge(S("merged"), 8)
            for s in range(4):
                w, n = take_slab(("out", s))
                w = w.rearrange("p (k c) -> p k c", k=8)
                for t in range(2):
                    o = open_group(("wo", 2 * s + t), 4 + t)
                    for k in range(KT):
                        mm = mmul(o[:, 0:256], w[:, k, t * P:(t + 1) * P], merged[:, k, :], start=(k == 0), stop=(k == KT - 1))
                    close_group(mm, ("wo", 2 * s + t))
                slab_end[n] = ("wo", 2 * s + 1)
            pe.wait_ge(S("sq2"), 1)
            rms_sums("sum2", 0, 256)
            pe.wait_ge(S("h2"), 8)
            for t in range(TT):
                o = open_group(("rt", t), 6)
                for k in range(KT):
                    mm = mmul(o[:, 0:64], hT[:, k, t * P:(t + 1) * P], wr[:, k, :], start=(k == 0), stop=(k == KT - 1))
                close_group(mm, ("rt", t))
            for g in range(4):
                o = open_group(("tk", g), 1 + g % 2)
                for k in range(4):
                    mm = nc.tensor.transpose(o[:, P * k:P * k + P],
                                             hT[:, 4 * (g % 2) + k, (g // 2) * P:(g // 2) * P + P], cc("ident"))
                close_group(mm, ("tk", g))
            t_tiles("shg", ("shg", 0), 2, [3, 4], 256)
            t_tiles("shu", ("shu", 0), 2, [3, 4], 256)
            pe.wait_ge(S("sh_act"), 1)
            w, n = take_slab(("shd", 0))
            for d in range(8):
                o = open_group(("shd", d), 3 + d % 2)
                for f in range(2):
                    mm = mmul(o[:, 0:256], w[:, 1024 * f + P * d:1024 * f + P * d + P], shu[:, f, :], start=(f == 0), stop=(f == 1))
                close_group(mm, ("shd", d))
            slab_end[n] = ("shd", 7)
            pe.wait_ge(S("mask"), 1)
            o = open_group("pos", 7)
            mmul(o[:, 0:64], cc("tri"), mask[:, 0, :], start=True, stop=True)
            mmul(o[:, 64:128], ones[:], mask[:, 0, :], start=True, stop=False)
            mmul(o[:, 64:128], cc("tri"), mask[:, 1, :], start=False, stop=True)
            mmul(o[:, 128:192], ones[:], mask[:, 0, :], start=True, stop=False)
            mm = mmul(o[:, 128:192], ones[:], mask[:, 1, :], start=False, stop=True)
            close_group(mm, "pos")

            moe_slab0 = len(slabs)
            for b in range(8):
                moe0[b] = uses[b]
            done(pe, ("tk", 3))

            def wait_done(key, e):
                pe.wait_ge(psum_done[MOE_BANKS[key]], e + moe0[MOE_BANKS[key]])

            def gather(e, u):
                pe.wait_ge(S("sel_ready"), e + 1)
                for g, key in enumerate(("G0", "G1")):
                    wait_done(key, e)
                    o = bank[MOE_BANKS[key]]
                    for d in range(4):
                        for t in range(TT):
                            for q in range(3):
                                mm = mmul(o[:, SLOTS * d:SLOTS * d + SLOTS], hbf[:, q, t, P * (4 * g + d):P * (4 * g + d) + P],
                                          selb[:, u, t, :], start=(t == 0 and q == 0), stop=(t == 1 and q == 2))
                    if g == 1:
                        for t in range(TT):
                            mm = mmul(o[:, 4 * SLOTS:5 * SLOTS], ones[:], selg[:, u, t, :], start=(t == 0), stop=(t == 1))
                    mm.then_inc(psum_full[MOE_BANKS[key]], 1)

            def hidden(e, u, arrived):
                pe.wait_ge(psum_done[MOE_BANKS["G0"]], e + moe0[MOE_BANKS["G0"]] + 1)
                pe.wait_ge(psum_done[MOE_BANKS["G1"]], e + moe0[MOE_BANKS["G1"]] + 1)
                for j, key in enumerate(("Hg", "Hu")):
                    wait_done(key, e)
                    w = arrived(j).rearrange("p (k c) -> p k c", k=8)
                    for f in range(2):
                        for k in range(KT):
                            mm = mmul(bank[MOE_BANKS[key]][:, SLOTS * f:SLOTS * f + SLOTS], w[:, k, P * f:P * f + P],
                                      xg[:, u, SLOTS * k:SLOTS * k + SLOTS], start=(k == 0), stop=(k == KT - 1))
                    mm.then_inc(psum_full[MOE_BANKS[key]], 1)

            def down(e, u, arrived):
                pe.wait_ge(S("act_ready"), e + 1)
                w = arrived(2)
                for c, key in enumerate(("D0", "D1")):
                    wait_done(key, e)
                    for f in range(2):
                        mm = mmul(bank[MOE_BANKS[key]][0:SLOTS, :], aT[:, u, SLOTS * f:SLOTS * f + SLOTS],
                                  w[:, 1024 * f + 512 * c:1024 * f + 512 * c + 512], start=(f == 0), stop=(f == 1))
                    mm.then_inc(psum_full[MOE_BANKS[key]], 1)

            def expert(i, u):
                def arrived(j):
                    n = moe_slab0 + PER_E * u + j
                    pe.wait_ge(slab_in[n % RING], 16 * i + 16 * (n // RING + 1))
                    return ring[:, n % RING, :]
                hidden(UN * i + u, u, arrived)
                if not (isinstance(i, int) and UN * i + u == E - 1):
                    gather(UN * i + u + 1, (u + 1) % UN)
                down(UN * i + u, u, arrived)

            gather(0, 0)
            with pe.Fori(0, TURNS) as i:
                for u in range(UN):
                    expert(i, u)
            for u in range(E - UN * TURNS):
                expert(TURNS, u)
            for b in MOE_BANKS.values():
                uses[b] += E
            for e in range(E):
                for j in range(PER_E):
                    slabs.append(("exp", e, j))
                    slab_end.append(("moe", e, j))

            pe.wait_ge(S("flag"), 1)
            many = pe.value_load(flag[0:1, 0:1])
            with pe.If(many > SLOTS):
                for b in MOE_BANKS.values():
                    pe.wait_ge(psum_done[b], uses[b])
                for r in range(1, ROUNDS):
                    with pe.Fori(0, E) as e:
                        n = e + E * (r - 1)
                        pe.wait_ge(S("ov_sel"), n + 1)
                        for g in range(2):
                            o = bank[g]
                            for d in range(4):
                                for t in range(TT):
                                    for q in range(3):
                                        mmul(o[:, SLOTS * d:SLOTS * d + SLOTS], hbf[:, q, t, P * (4 * g + d):P * (4 * g + d) + P],
                                             selb[:, 0, t, :], start=(t == 0 and q == 0), stop=(t == 1 and q == 2))
                        for t in range(TT):
                            mm = mmul(bank[1][:, 4 * SLOTS:5 * SLOTS], ones[:], selg[:, 0, t, :], start=(t == 0), stop=(t == 1))
                        mm.then_inc(S("ov_pe"), 1)
                        pe.wait_ge(S("ov_xg"), n + 1)
                        pe.wait_ge(S("ov_w"), 48 * n + 48)
                        for j in range(2):
                            w = ring[:, j, :].rearrange("p (k c) -> p k c", k=8)
                            for f in range(2):
                                for k in range(KT):
                                    mm = mmul(bank[2 + j][:, SLOTS * f:SLOTS * f + SLOTS], w[:, k, P * f:P * f + P],
                                              xg[:, 0, SLOTS * k:SLOTS * k + SLOTS], start=(k == 0), stop=(k == KT - 1))
                        mm.then_inc(S("ov_pe"), 1)
                        pe.wait_ge(S("ov_act"), n + 1)
                        for c in range(2):
                            for f in range(2):
                                mm = mmul(bank[4 + c][0:SLOTS, :], aT[:, 0, SLOTS * f:SLOTS * f + SLOTS],
                                          ring[:, 2, 1024 * f + 512 * c:1024 * f + 512 * c + 512], start=(f == 0), stop=(f == 1))
                        mm.then_inc(S("ov_pe"), 1)

            for g in range(4):
                pe.wait_ge(S("acc_final"), 1)
                o = open_group(("ac", g), 6 + g % 2)
                for k in range(4):
                    at = 512 * (g % 2) + P * k
                    mm = nc.tensor.transpose(o[:, P * k:P * k + P], acc[:, g // 2, at:at + P], cc("ident"))
                close_group(mm, ("ac", g))

            pe.wait_ge(S("sq3"), 1)
            rms_sums("sum3", 0, 512)
            pe.wait_ge(S("h3"), 16)
            pe.wait_ge(S("const2_in"), 32)
            for s in range(2):
                tok_tiles(f"vab{s}", ("ab", s), 4, [1, 2])
            for s in range(8):
                t_tiles(f"z{s}", ("ab", 2 + s), 2, [3, 4], 512)
            for g in range(4):
                for st in range(2):
                    n = 2 * g + st
                    done(pe, (f"z{g // 2}", g % 2))
                    o = open_group(("fa", n), 5 + n % 2)
                    for t in range(TT):
                        at = 256 * st + P * t
                        mm = mmul(o[:, 256 * t:256 * t + 256], zT[:, 12 + g, at:at + P], cc("dft_c"), start=True, stop=True)
                    close_group(mm, ("fa", n))
                    done(pe, ("fa", n))
                    o = open_group(("fb", n), 0 if n % 2 else 7)
                    for t in range(TT):
                        for c in range(2):
                            mm = mmul(o[:, 0:256], fa[:, n % 2, 256 * t + P * c:256 * t + P * c + P],
                                      cc("dft_l", 512 * t + 256 * c, 512 * t + 256 * c + 256),
                                      start=(t == 0 and c == 0), stop=(t == 1 and c == 1))
                    close_group(mm, ("fb", n))
            pe.wait_ge(S("v_norm"), 4)
            for h in range(4):
                o = open_group(("sp", h), 1 + h % 2)
                for t in range(4):
                    mm = mmul(o[:, P * t:P * t + P], vtok[:, t, P * h:P * h + P], spat[:, h, :], start=True, stop=True)
                close_group(mm, ("sp", h))
            pe.wait_ge(S("y_a"), 4)
            done(pe, ("fb", 7))
            done(pe, ("fb", 6))
            for s in range(4):
                w, n = take_slab(("oab", s))
                w = w.rearrange("p (k c) -> p k c", k=8)
                for t in range(2):
                    o = open_group(("oab", 2 * s + t), 3 + t)
                    for k in range(KT):
                        mm = mmul(o[:, :], w[:, k, t * P:(t + 1) * P], zT[:, k, :], start=(k == 0), stop=(k == KT - 1))
                    close_group(mm, ("oab", 2 * s + t))
                slab_end[n] = ("oab", 2 * s + 1)
            pe.wait_ge(S("sq4"), 1)
            rms_sums("sum4", 0, 512)
            pe.wait_ge(S("h4"), 16)
            t_tiles("k2", ("cin", 0), 2, [1, 2], 512)
            tok_tiles("v2", ("cin", 1), 4, [1, 2])
            for s in range(4):
                t_tiles(f"q2{s}", ("cin", 2 + s), 2, [3, 4], 256)
            for s in range(4):
                t_tiles(f"g2{s}", ("cin", 6 + s), 2, [3, 4], 256)
            for j in range(10):
                done(pe, ("k2", j) if j < 2 else (f"q2{(j - 2) // 2}", j % 2))
                src = k2[:, j, 0:256] if j < 2 else q2[:, j - 2, :]
                o = open_group(("sw", j), 1 + j % 2)
                close_group(mmul(o[:, 0:256], cc("perm128"), src, start=True, stop=True), ("sw", j))
            pe.wait_ge(S("rope2"), 10)
            done(pe, ("v2", 2))
            done(pe, ("v2", 3))
            attention("c")
            done(pe, ("c", "o", 7))
            done(pe, ("c", "o", 6))
            for s in range(4):
                w, n = take_slab(("oc", s))
                w = w.rearrange("p (k c) -> p k c", k=8)
                for t in range(2):
                    o = open_group(("oc", 2 * s + t), t)
                    for k in range(KT):
                        mm = mmul(o[:, 0:256], w[:, k, t * P:(t + 1) * P], o2[:, k, :], start=(k == 0), stop=(k == KT - 1))
                    close_group(mm, ("oc", 2 * s + t))
                slab_end[n] = ("oc", 2 * s + 1)
            pe.wait_ge(S("sq5"), 1)
            rms_sums("sum5", 2, 256)

        exp0 = next(n for n, s in enumerate(slabs) if s[0] == "exp")

        @block.sync
        def _(sp):
            def load(n):
                slot = n % RING
                src = slabs[n]
                w = slabs_d[slabs_at[src[0]] + src[1]]
                sp.dma_start(ring[:, slot, :], w).then_inc(slab_in[slot], 16)

            def slab_read(n):
                end = slab_end[n]
                if end[0] == "moe":
                    b = MOE_BANKS[("Hg", "Hu", "D1")[end[2]]]
                    sp.wait_ge(psum_full[b], moe0[b] + end[1] + 1)
                else:
                    full(sp, end)

            for n in range(exp0):
                if n >= RING:
                    slab_read(n - RING)
                load(n)

            def expert_slabs(i, u):
                e = UN * i + u
                for j in range(PER_E):
                    n = exp0 + PER_E * u + j
                    if isinstance(i, int) and i == 0:
                        slab_read(n - RING)
                    else:
                        b = MOE_BANKS[("Hg", "Hu", "D1")[j]]
                        sp.wait_ge(psum_full[b], e + (moe0[b] + 1 - UN))
                    sp.dma_start(ring[:, n % RING, :], exp_d[e, j]).then_inc(slab_in[n % RING], 16)

            for u in range(UN):
                expert_slabs(0, u)
            with sp.Fori(1, TURNS) as i:
                for u in range(UN):
                    expert_slabs(i, u)
            for u in range(E - UN * TURNS):
                expert_slabs(TURNS, u)

            sp.wait_ge(S("flag"), 1)
            many = sp.value_load(flag[0:1, 0:1])
            with sp.If(many > SLOTS):
                for j in range(RING):
                    slab_read(exp0 + PER_E * E - RING + j)
                for r in range(1, ROUNDS):
                    with sp.Fori(0, E) as e:
                        sp.wait_ge(S("ov_go"), e + 1 + E * (r - 1))
                        for j in range(PER_E):
                            sp.dma_start(ring[:, j, :], exp_d[e, j]).then_inc(S("ov_w"), 16)
                sp.wait_ge(S("ov_pe"), 3 * E * (ROUNDS - 1))
            for n in range(exp0 + PER_E * E, len(slabs)):
                slab_read(n - RING)
                load(n)

        @block.gpsimd
        def _(pool):
            g = nc.gpsimd
            g.memset(silc[:], 0.0).then_inc(S("silc_zero"), 1)
            g.memset(silc2[:], 0.0).then_inc(S("silc_zero"), 1)
            g.memset(ones[:], 1.0).then_inc(S("ones_set"), 1)
            g.memset(lat[0:64, 3, :], 0.0).then_inc(S("kr_zero"), 1)
            pool.wait_ge(S("const_in"), 48)
            pool.wait_ge(S("bias_in"), 32)
            for h in range(8):
                if h >= 2:
                    done(pool, ("na", "s", h - 2))
                for t in range(TT):
                    r = braw[:, h, :]
                    rev = bass.AP(r.tensor, r.offset + 62 * (1 - t) + 63, [list(r.ap[0]), [31, 4], [-1, 64]])
                    m = cc("namask")
                    mb = bass.AP(m.tensor, m.offset, [list(m.ap[0]), [0, 4], [1, 64]])
                    g.tensor_tensor(bmask[:, h % 2, 256 * t:256 * t + 256].rearrange("p (a b) -> p a b", a=4),
                                    rev, mb, ALU.add).then_inc(S("bias_made"), 1)
            pool.wait_ge(S("rope_tab"), 1)
            for gg in range(4):
                full(pool, ("qsw", gg))
                for h in range(2):
                    v = qm[0:96, 2 * gg + h, :]
                    last = g.tensor_tensor(v, v, rope_c[0:96, :], ALU.mult)
                last.then_inc(S("q_cos"), 1)

            pool.wait_ge(S("x1"), 1)
            pool.dma_start(cs2, consts2_d).then_inc(S("const2_in"), 16)
            pool.dma_start(spat, spat_d).then_inc(S("const2_in"), 16)
            g.memset(zrow[:], 0.0).then_inc(S("zero_row"), 1)
            pool.wait_ge(S("zero_row"), 1)
            for dst in (rows_d, more_d):
                pool.dma_start(dst[0:1, :].rearrange("a (p c) -> (a p) c", p=P), zrow[:]).then_inc(S("zero_in"), 16)
            rows_of = rows_d[1:1 + E * SLOTS, :].rearrange("(e s) d -> e s d", e=E)
            more_of = more_d[1:1 + E * SLOTS * (ROUNDS - 1), :].rearrange("(e r s) d -> e r s d", e=E, r=ROUNDS - 1)

            def store(e, u):
                for key in ("D0", "D1"):
                    b = MOE_BANKS[key]
                    pool.wait_ge(psum_done[b], e + (moe0[b] + 1))
                pool.dma_start(rows_of[e], yo[0:SLOTS, u, :]).then_inc(S(f"stored{u}"), 16)

            with pool.Fori(0, TURNS) as i:
                for u in range(UN):
                    store(UN * i + u, u)
            for u in range(E - UN * TURNS):
                store(UN * TURNS + u, u)
            pool.wait_ge(S("flag"), 1)
            many = pool.value_load(flag[0:1, 0:1])
            for u in range(UN):
                pool.wait_ge(S(f"stored{u}"), 16 * (TURNS + (1 if u < E - UN * TURNS else 0)))
            with pool.If(many > SLOTS):
                for r in range(1, ROUNDS):
                    with pool.Fori(0, E) as e:
                        pool.wait_ge(S("ov_y"), e + E * (r - 1) + 1)
                        pool.dma_start(more_of[e, r - 1], yo[0:SLOTS, 0, :]).then_inc(S("ov_stored"), 16)
                pool.wait_ge(S("ov_stored"), 16 * E * (ROUNDS - 1))
            pool.wait_ge(S("ridx"), 1)
            pool.wait_ge(S("zero_in"), 32)
            for t in range(TT):
                for k in range(TOPK):
                    n = TOPK * t + k
                    if n >= 3:
                        pool.wait_ge(S("acc"), n - 2)
                    pool.indirect_dma_start(out=gat[:, n % 3, :], out_offset=None, in_=rows_d,
                                            in_offset=bass.IndirectOffsetOnAxis(ap=ridx[:, t, k:k + 1], axis=0)
                                            ).then_inc(S(f"rows_in{n % 3}"), 16)
            with pool.If(many > SLOTS):
                pool.wait_ge(S("acc"), TT * TOPK)
                pool.wait_ge(S("ov_ridx"), 1)
                for n in range(TT * TOPK):
                    if n:
                        pool.wait_ge(S("ov_acc"), n)
                    pool.indirect_dma_start(out=gat[:, 0, :], out_offset=None, in_=more_d,
                                            in_offset=bass.IndirectOffsetOnAxis(ap=ridx2[:, n // TOPK, n % TOPK:n % TOPK + 1], axis=0)
                                            ).then_inc(S("ov_rows"), 16)

        @block.scalar
        def _(act):
            a = nc.scalar
            steps = [0]

            def link(ins):
                steps[0] += 1
                ins.then_inc(S("act_step"), 1)
                act.wait_ge(S("act_step"), steps[0])

            act.dma_start(ve[:], vecs_d).then_inc(S("vec_in"), 16)
            act.dma_start(xT[:], xT_d).then_inc(S("x_in"), 16)
            act.dma_start(cs[:], consts_d).then_inc(S("const_in"), 16)
            act.dma_start(stat[0:96, 0:256].bitcast(I32), pos_d).then_inc(S("const_in"), 16)
            act.dma_start(wr[:], router_d).then_inc(S("const_in"), 16)
            for r in range(2):
                src = bass.AP(rpb_d.tensor, (5 - r) * 31 - 48, [[1, 64], [15 * 31, 8], [1, RUN]])
                act.dma_start(braw[64 * r:64 * r + 64, :, :], src).then_inc(S("bias_in"), 16)
            act.wait_ge(S("vec_in"), 16)
            act.wait_ge(S("silc_zero"), 2)
            a.activation(silc[:, :, 0], vv("c"), ACT.Silu)
            a.activation(silc2[:, :, 0:2], vv("c2").rearrange("p (a b) -> p a b", a=8), ACT.Silu).then_inc(S("silu_c"), 1)
            act.wait_ge(S("x_in"), 16)
            for k in range(KT):
                last = a.activation(hT[:, k, 0:256], xT[:, k, 0:256], ACT.Square)
            last.then_inc(S("sq1"), 1)

            def ada_quarters(which, j):
                name = (which, j, "quarters")
                full(act, name)
                emptied(a.copy(quarters[:, j % 2, :], bk(name)[:, 0:256]), name)

            for j in range(8):
                ada_quarters("ada1", j)

            def root(n, src, tag, cols, parts=P):
                act.wait_ge(S(tag + "_ms"), n)
                a.activation(src[0:parts, 0:cols], src[0:parts, 0:cols], ACT.Sqrt).then_inc(S(tag + "_rt"), 1)

            def shifts(tag, cols, shift):
                for k in range(KT):
                    for s in range(cols // 256):
                        n = k * (cols // 256) + s
                        act.wait_ge(S(tag + "_scaled"), n + 1)
                        v = hT[:, k, 256 * s:256 * s + 256]
                        a.activation(v, v, ACT.Identity, bias=shift(k, s)).then_inc(S(tag), 1)

            act.wait_ge(S("angle"), 1)
            a.activation(rope_s[0:96, :], sqt[0:96, 0, 0:256], ACT.Sin)
            a.activation(rope_c[0:96, :], sqt[0:96, 1, 0:256], ACT.Sin).then_inc(S("rope_tab"), 1)
            root(1, rstd, "n1", 256)
            shifts("h1", 256, lambda k, s: mod1[:, k:k + 1])
            for s in range(4):
                for t in range(2):
                    j = 2 * s + t
                    full(act, (f"qk{s}", t))
                    if j >= 2:
                        full(act, ("qkn", j - 2))
                    a.activation(sqt[:, j % 2, 0:256], bk((f"qk{s}", t))[:, 0:256], ACT.Square).then_inc(S("sq_qk"), 1)
                    emptied(a.copy(qk[:, j, :], bk((f"qk{s}", t))[:, 0:256]), (f"qk{s}", t))
            for s in range(2):
                for t in range(2):
                    full(act, (f"vna{s}", t))
                    emptied(a.copy(vna[:, t, 256 * s:256 * s + 256], bk((f"vna{s}", t))[:, 0:256]), (f"vna{s}", t))
            for t in range(2):
                full(act, ("ql", t))
                full(act, ("qkn", 6 + t))
                a.activation(sqt[:, t, 0:256], bk(("ql", t))[:, 0:256], ACT.Square).then_inc(S("sq_ql"), 1)
                emptied(a.copy(lat[:, t, :], bk(("ql", t))[:, 0:256]), ("ql", t))
            full(act, "kvl")
            a.activation(sqt[:, 0, 256:512], bk("kvl")[:, 0:256], ACT.Square).then_inc(S("sq_kvl"), 1)
            emptied(a.copy(lat[:, 2, :], bk("kvl")[:, 0:256]), "kvl")
            full(act, "krot")
            emptied(a.copy(lat[64:96, 3, :], bk("krot")[64:96, 0:256]), "krot")
            root(1, pr[:, :, :].rearrange("p a b -> p (a b)"), "qk", 2048)
            root(1, stat, "lt", 512)
            for s in range(8):
                for t in range(2):
                    full(act, (f"gt{s}", t))
                    emptied(a.activation(sgate[:, 2 * s + t, :], bk((f"gt{s}", t))[:, 0:256], ACT.Sigmoid), (f"gt{s}", t))
            for gg in range(4):
                full(act, ("uq", gg))
                emptied(a.copy(qm[0:96, 2 * gg:2 * gg + 2, :].rearrange("p a b -> p (a b)"), bk(("uq", gg))[0:96, :]), ("uq", gg))
            for gg in range(4):
                full(act, ("uk", gg))
                emptied(a.copy(km[0:64, 2 * gg:2 * gg + 2, :].rearrange("p a b -> p (a b)"), bk(("uk", gg))[0:64, :]), ("uk", gg))
            for t in range(2):
                full(act, ("uv", t))
                emptied(a.copy(vm[:, t, :], bk(("uv", t))[:, :]), ("uv", t))

            def attention(kind):
                n_heads, _, nk = KINDS[kind]
                for i in range(n_heads // 2):
                    for h in (2 * i, 2 * i + 1):
                        act.wait_ge(S(kind + "_negmax"), h + 1)
                        if kind == "c":
                            a.activation(att[:, h % 4, 6:8], att[:, h % 4, 0:2], ACT.Exp)
                        if kind == "mla" and h >= 4:
                            full(act, (kind, "t", h - 4, 0))
                        for t in range(TT):
                            o = probs(kind, h)[:, nk * t:nk * t + nk]
                            src = bk((kind, "s", h))[:, 256 * t:256 * t + 256] if kind == "mla" else o
                            ins = a.activation(o, src, ACT.Exp, bias=att[:, h % 4, 2 + t:3 + t],
                                               scale=96 ** -0.5 if kind == "mla" else 1.0,
                                               accum_out=att[:, h % 4, 4 + t:5 + t])
                        if kind == "mla":
                            emptied(ins, (kind, "s", h))
                        else:
                            ins.then_inc(S(kind + "_exp"), 1)
                    for f in FILL.get((kind, i), []):
                        ada_quarters(*f)
                    for h in (2 * i, 2 * i + 1):
                        for j in range(nk // 256):
                            full(act, (kind, "t", h, j))
                            emptied(a.copy(pT[:, h % 2, 512 * j:512 * j + 512], bk((kind, "t", h, j))[:, :]), (kind, "t", h, j))

            attention("na")
            for gg in range(8):
                act.wait_ge(S("m_in"), gg + 1)
                if gg >= 2:
                    full(act, ("msum", gg - 2))
                v = (qm if gg < 4 else km)[0:96, 2 * (gg % 4):2 * (gg % 4) + 2, :].rearrange("p a b -> p (a b)")
                a.activation(sqt[0:96, gg % 2, :], v, ACT.Square).then_inc(S("sq_m"), 1)
            root(1, var, "mq", 2048, 96)
            root(1, pT[:, :, :].rearrange("p a b -> p (a b)"), "mk", 2048, 96)
            attention("mla")
            act.wait_ge(S("x1"), 1)
            for k in range(KT):
                last = a.activation(hT[:, k, 0:256], xT[:, k, 0:256], ACT.Square)
            last.then_inc(S("sq2"), 1)
            root(1, rstd, "n2", 256)
            shifts("h2", 256, lambda k, s: mod1[:, 24 + k:25 + k])
            for t in range(TT):
                full(act, ("rt", t))
                emptied(a.activation(lg[:, t, :], bk(("rt", t))[:, 0:64], ACT.Sigmoid), ("rt", t))
            for gg in range(4):
                w0, t = 512 * (gg % 2), gg // 2
                full(act, ("tk", gg))
                a.copy(hbf[:, 0, t, w0:w0 + 512], bk(("tk", gg))[:, :]).then_inc(S("part_a"), 1)
                act.wait_ge(S("rest_a"), gg + 1)
                a.copy(hbf[:, 1, t, w0:w0 + 512], htok[:, gg % 2, :]).then_inc(S("part_b"), 1)
            for t in range(2):
                full(act, ("shg", t))
                emptied(a.activation(shg[:, t, :], bk(("shg", t))[:, 0:256], ACT.Silu), ("shg", t))

            def moe_full(key, e):
                b = MOE_BANKS[key]
                act.wait_ge(psum_full[b], e + (moe0[b] + 1))

            def gathered(e, u):
                moe_full("G0", e)
                a.copy(xg[:, u, 0:4 * SLOTS], bank[MOE_BANKS["G0"]][:, 0:4 * SLOTS]).then_inc(psum_done[MOE_BANKS["G0"]], 1)

            def expert(i, u):
                e = UN * i + u
                moe_full("Hg", e)
                a.activation(sgt[:, u, :], bank[MOE_BANKS["Hg"]][:, 0:2 * SLOTS], ACT.Silu).then_inc(psum_done[MOE_BANKS["Hg"]], 1)
                if not (isinstance(i, int) and e == E - 1):
                    gathered(e + 1, (u + 1) % UN)
                moe_full("D0", e)
                if not (isinstance(i, int) and i == 0):
                    act.wait_ge(S(f"stored{u}"), 16 * i)
                a.copy(yo[0:SLOTS, u, 0:512], bank[MOE_BANKS["D0"]][0:SLOTS, :]).then_inc(psum_done[MOE_BANKS["D0"]], 1)

            gathered(0, 0)
            for u in range(UN):
                expert(0, u)
            with act.Fori(1, TURNS) as i:
                for u in range(UN):
                    expert(i, u)
            for u in range(E - UN * TURNS):
                expert(TURNS, u)

            act.wait_ge(S("flag"), 1)
            many = act.value_load(flag[0:1, 0:1])
            with act.If(many > SLOTS):
                for r in range(1, ROUNDS):
                    with act.Fori(0, E) as e:
                        act.wait_ge(S("ov_pe"), 3 * e + 3 * E * (r - 1) + 2)
                        a.activation(sgt[:, 0, :], bank[2][:, 0:2 * SLOTS], ACT.Silu).then_inc(S("ov_silu"), 1)

            def squares(ready, n, tag, cols):
                act.wait_ge(S(ready), n)
                for k in range(KT):
                    last = a.activation(hT[:, k, 0:cols], xT[:, k, 0:cols], ACT.Square)
                last.then_inc(S(tag), 1)

            squares("x2", 1, "sq3", 512)
            root(1, rstd, "n3", 512)
            shifts("h3", 512, lambda k, s: mod2[:, k, s:s + 1])
            for s in range(2):
                for t in range(4):
                    full(act, (f"vab{s}", t))
                    emptied(a.copy(vtok[:, t, 256 * s:256 * s + 256], bk((f"vab{s}", t))[:, 0:256]), (f"vab{s}", t))
            root(1, bn[:, :, 13], "v", 4)
            for s in range(8):
                for t in range(2):
                    at = (12, 4, 0, 8)[s // 2] + 2 * (s % 2) + t
                    full(act, (f"z{s}", t))
                    f = (ACT.Copy, ACT.Silu, ACT.Copy, ACT.Silu)[s // 2]
                    emptied(a.activation(zT[:, at, :], bk((f"z{s}", t))[:, :], f), (f"z{s}", t))
            for n in range(8):
                full(act, ("fa", n))
                if n >= 2:
                    full(act, ("fb", n - 2))
                emptied(a.copy(fa[:, n % 2, :], bk(("fa", n))[:, :]), ("fa", n))
            squares("x3", 1, "sq4", 512)
            root(1, rstd, "n4", 512)
            shifts("h4", 512, lambda k, s: mod2[:, 24 + k, s:s + 1])
            for t in range(2):
                full(act, ("k2", t))
                emptied(a.copy(k2[:, t, :], bk(("k2", t))[:, :]), ("k2", t))
            for t in range(4):
                full(act, ("v2", t))
                emptied(a.copy(v2[:, t, :], bk(("v2", t))[:, 0:256]), ("v2", t))
            for s in range(4):
                for t in range(2):
                    full(act, (f"q2{s}", t))
                    emptied(a.copy(q2[:, 2 * s + t, :], bk((f"q2{s}", t))[:, 0:256]), (f"q2{s}", t))
            for s in range(4):
                for t in range(2):
                    full(act, (f"g2{s}", t))
                    emptied(a.activation(g2s[:, 2 * s + t, :], bk((f"g2{s}", t))[:, 0:256], ACT.Silu), (f"g2{s}", t))

            attention("c")
            act.wait_ge(S("x4"), 1)
            for k in range(KT):
                last = a.activation(hT[:, k, 0:256], xT[:, k, 0:256], ACT.Square)
            last.then_inc(S("sq5"), 1)
            root(1, rstd, "n5", 256)
            for k in range(KT):
                act.wait_ge(S("y_out"), k + 1)
                act.dma_start(out_d[:, k, :], outT[:, k, :]).then_inc(S("stored_out"), 16)
            act.wait_ge(S("stored_out"), 16 * KT)

        @block.vector
        def _(dve):
            v = nc.vector
            steps = [0]
            signals = [0]

            def link(ins):
                steps[0] += 1
                ins.then_inc(S("dve_step"), 1)
                dve.wait_ge(S("dve_step"), steps[0])

            def signal(name):
                signals[0] += 1
                v.tensor_copy(mark[0:1, signals[0]:signals[0] + 1], mark[0:1, 0:1]).then_inc(S(name), 1)

            def bc(ap, *dims):
                return bass.AP(ap.tensor, ap.offset, [list(ap.ap[0])] + [list(d) for d in dims])

            def ada(which, j):
                full(dve, (which, j))
                o = bk((which, j))
                if which == "ada1":
                    emptied(v.tensor_tensor(mod1[:, 2 * j:2 * j + 2], o[:, 0:2], vv("b_ada", 2 * j, 2 * j + 2), ALU.add), (which, j))
                else:
                    b = vv("b2", 2 * j, 2 * j + 2)
                    emptied(v.tensor_tensor(mod2[:, 2 * j:2 * j + 2, :], o[:, 0:4].rearrange("p (a b) -> p a b", a=2),
                                            bc(b, [1, 2], [0, 2]), ALU.add), (which, j))

            def rms(tag, name, width, cols, dst, parts=P, last=True):
                full(dve, name)
                emptied(v.tensor_scalar(dst[0:parts, 0:cols], bk(name)[0:parts, 0:cols], 1.0 / width, EPS, ALU.mult, ALU.add), name)
                done(dve, name)
                signal(tag + "_ms")
                dve.wait_ge(S(tag + "_rt"), 1)
                link(v.reciprocal(dst[0:parts, 0:cols], dst[0:parts, 0:cols]))

            def scale_tiles(tag, cols, gain):
                for k in range(KT):
                    for s in range(cols // 256):
                        v.scalar_tensor_tensor(out=hT[:, k, 256 * s:256 * s + 256], in0=xT[:, k, 256 * s:256 * s + 256],
                                               scalar=gain(k, s), in1=rstd[:, 256 * s:256 * s + 256],
                                               op0=ALU.mult, op1=ALU.mult).then_inc(S(tag + "_scaled"), 1)

            link(v.memset(mark[:], 0.0))
            dve.wait_ge(S("const_in"), 48)
            pf, an, tn = pr[0:96, 0, 0:256], pr[0:96, 0, 256:512], pr[0:96, 0, 512:768]
            sn, co = sqt[0:96, 0, 0:256], sqt[0:96, 1, 0:256]
            link(v.tensor_copy(pf, stat[0:96, 0:256].bitcast(I32)))
            link(v.tensor_scalar(an, pf, cc("invf")[0:96, :], None, ALU.mult))
            MAGIC = 12582912.0
            link(v.tensor_scalar(tn, an, 1.0 / TWO_PI, MAGIC, ALU.mult, ALU.add))
            link(v.tensor_scalar(tn, tn, -MAGIC, None, ALU.add))
            C1 = 6.28125
            C2 = float(np.float32(np.round((TWO_PI - C1) * 2 ** 20) / 2 ** 20))
            C3 = float(TWO_PI - C1 - C2)
            for c in (C1, C2, C3):
                link(v.scalar_tensor_tensor(out=an, in0=tn, scalar=-c, in1=an, op0=ALU.mult, op1=ALU.add))
            LIM = 3.1415925
            link(v.tensor_scalar(sn, an, LIM, -LIM, ALU.min, ALU.max))
            link(v.tensor_scalar(an, an, float(np.pi / 2), None, ALU.add))
            link(v.tensor_scalar(tn, an, float(np.pi), -TWO_PI, ALU.is_gt, ALU.mult))
            link(v.tensor_tensor(an, an, tn, ALU.add))
            v.tensor_scalar(co, an, LIM, -LIM, ALU.min, ALU.max).then_inc(S("angle"), 1)

            for j in range(8):
                ada("ada1", j)
            done(dve, ("ada1", 6))
            done(dve, ("ada1", 7))
            link(v.scalar_tensor_tensor(out=gs[:, :, 0], in0=mod1[:, 8:16], scalar=1.0, in1=vv("g1"), op0=ALU.add, op1=ALU.mult))
            rms("n1", "sum1", D, 256, rstd)
            scale_tiles("h1", 256, lambda k, s: gs[:, k, 0:1])
            for j in range(8):
                full(dve, ("qkn", j))
                emptied(v.tensor_scalar(pr[:, j // 4, 256 * (j % 4):256 * (j % 4) + 256], bk(("qkn", j))[:, 0:256],
                                        1.0 / 64, EPS, ALU.mult, ALU.add), ("qkn", j))
            full(dve, "sum_ql")
            emptied(v.tensor_scalar(stat[:, 0:256], bk("sum_ql")[:, 0:256], 1.0 / 256, EPS, ALU.mult, ALU.add), "sum_ql")
            full(dve, "sum_kvl")
            emptied(v.tensor_scalar(stat[:, 256:512], bk("sum_kvl")[:, 0:256], 1.0 / 128, EPS, ALU.mult, ALU.add), "sum_kvl")
            done(dve, "sum_kvl")
            done(dve, "sum_ql")
            signal("lt_ms")
            signal("qk_ms")
            dve.wait_ge(S("qk_rt"), 1)
            prf = pr[:, :, :].rearrange("p a b -> p (a b)")
            link(v.reciprocal(prf, prf))
            for j in range(8):
                done(dve, (f"qk{j // 2}", j % 2))
                g = vv("gq") if j < 4 else vv("gk")
                v.scalar_tensor_tensor(out=qk[:, j, :], in0=qk[:, j, :], scalar=g, in1=prf[:, 256 * j:256 * j + 256],
                                       op0=ALU.mult, op1=ALU.mult).then_inc(S("qk_ready"), 1)
            dve.wait_ge(S("lt_rt"), 1)
            link(v.reciprocal(stat[:, :], stat[:, :]))
            for t in range(2):
                done(dve, ("ql", t))
                v.scalar_tensor_tensor(out=lat[:, t, :], in0=lat[:, t, :], scalar=vv("gql", t, t + 1), in1=stat[:, 0:256],
                                       op0=ALU.mult, op1=ALU.mult).then_inc(S("qln"), 1)
            done(dve, "kvl")
            v.scalar_tensor_tensor(out=lat[:, 2, :], in0=lat[:, 2, :], scalar=vv("gkv"), in1=stat[:, 256:512],
                                   op0=ALU.mult, op1=ALU.mult).then_inc(S("kvn"), 1)

            def normalise(kind, h, nk):
                mx = att[:, h % 4, :]
                link(v.reciprocal(mx[:, 4:6], mx[:, 4:6]))
                for t in range(TT):
                    o = probs(kind, h)[:, nk * t:nk * t + nk]
                    last = v.tensor_scalar(o, o, mx[:, 4 + t:5 + t], None, ALU.mult)
                last.then_inc(S(kind + "_probs"), 1)

            def pair_out(kind, i, dst):
                full(dve, (kind, "o", i))
                emptied(v.tensor_copy(dst, bk((kind, "o", i))[:, 0:256]), (kind, "o", i))

            ada_prev = [("ada1", 7)]

            def ada_folds(key):
                for f in FILL[key]:
                    if ada_prev[0] != ("ada1", 7):
                        ada(*ada_prev[0])
                    ada_prev[0] = f

            def na_scores(h):
                if h >= 4:
                    full(dve, ("na", "t", h - 4, 0))
                full(dve, ("na", "s", h))
                dve.wait_ge(S("bias_made"), 2 * h + 2)
                emptied(v.scalar_tensor_tensor(out=probs("na", h), in0=bk(("na", "s", h))[:, :], scalar=0.125,
                                               in1=bmask[:, h % 2, :], op0=ALU.mult, op1=ALU.add), ("na", "s", h))
                done(dve, ("na", "s", h))
                link(v.tensor_reduce(att[:, h % 4, 0:2], probs("na", h).rearrange("p (a b) -> p a b", a=2), AXX, ALU.max))
                v.tensor_scalar(att[:, h % 4, 2:4], att[:, h % 4, 0:2], -1.0, None, ALU.mult).then_inc(S("na_negmax"), 1)

            na_scores(0)
            na_scores(1)
            for i in range(4):
                if i < 3:
                    na_scores(2 * i + 2)
                    na_scores(2 * i + 3)
                dve.wait_ge(S("na_exp"), 2 * i + 2)
                normalise("na", 2 * i, 256)
                normalise("na", 2 * i + 1, 256)
                ada_folds(("na", i))
                if i >= 1:
                    pair_out("na", i - 1, yT[:, i - 1, :])
            pair_out("na", 3, yT[:, 3, :])

            for gg in range(4):
                full(dve, ("qsw", gg))
                t2 = pT[0:96, gg % 2, 0:512]
                rs = bc(rope_s[0:96, :], [0, 2], [1, 256])
                if gg == 0:
                    dve.wait_ge(S("rope_tab"), 1)
                emptied(v.tensor_tensor(t2.rearrange("p (a b) -> p a b", a=2),
                                        bk(("qsw", gg))[0:96, :].rearrange("p (a b) -> p a b", a=2), rs, ALU.mult), ("qsw", gg))
                done(dve, ("qsw", gg))
                dve.wait_ge(S("q_cos"), gg + 1)
                q = qm[0:96, 2 * gg:2 * gg + 2, :].rearrange("p a b -> p (a b)")
                v.tensor_tensor(q, q, t2, ALU.add).then_inc(S("m_in"), 1)
            full(dve, "ksw")
            t2 = pT[0:96, 0, 512:768]
            emptied(v.tensor_tensor(t2, bk("ksw")[0:96, 0:256], rope_s[0:96, :], ALU.mult), "ksw")
            link(v.tensor_tensor(lat[0:96, 3, :], lat[0:96, 3, :], rope_c[0:96, :], ALU.mult))
            done(dve, "ksw")
            link(v.tensor_tensor(lat[0:96, 3, :], lat[0:96, 3, :], t2, ALU.add))
            for gg in range(4):
                done(dve, ("uk", gg))
                for h in range(2):
                    last = v.tensor_copy(km[64:96, 2 * gg + h, :], lat[64:96, 3, :])
                last.then_inc(S("m_in"), 1)
            for gg in range(8):
                full(dve, ("msum", gg))
                dst = var[0:96, 512 * gg:512 * gg + 512] if gg < 4 else pT[0:96, (gg - 4) // 2, 512 * (gg % 2):512 * (gg % 2) + 512]
                emptied(v.tensor_scalar(dst, bk(("msum", gg))[0:96, :], 1.0 / 96, EPS, ALU.mult, ALU.add), ("msum", gg))
                if gg % 4 == 3:
                    done(dve, ("msum", gg))
                    done(dve, ("msum", gg - 1))
                    signal(("mq" if gg < 4 else "mk") + "_ms")
            pTf = pT[:, :, :].rearrange("p a b -> p (a b)")
            for i, (tag, buf, dst, g) in enumerate((("mq", var, qm, "gmq"), ("mk", pTf, km, "gmk"))):
                dve.wait_ge(S(tag + "_rt"), 1)
                link(v.reciprocal(buf[0:96, 0:2048], buf[0:96, 0:2048]))
                for gg in range(4):
                    o = dst[0:96, 2 * gg:2 * gg + 2, :].rearrange("p a b -> p (a b)")
                    v.scalar_tensor_tensor(out=o, in0=o, scalar=vv(g)[0:96, :], in1=buf[0:96, 512 * gg:512 * gg + 512],
                                           op0=ALU.mult, op1=ALU.mult).then_inc(S("m_ready"), 1)

            def mla_scores(h):
                full(dve, ("mla", "s", h))
                link(v.tensor_reduce(att[:, h % 4, 0:2], bk(("mla", "s", h))[:, :].rearrange("p (a b) -> p a b", a=2), AXX, ALU.max))
                v.tensor_scalar(att[:, h % 4, 2:4], att[:, h % 4, 0:2], -(96 ** -0.5), None, ALU.mult).then_inc(S("mla_negmax"), 1)

            mla_scores(0)
            mla_scores(1)
            for i in range(4):
                for h in (2 * i, 2 * i + 1):
                    done(dve, ("mla", "s", h))
                    normalise("mla", h, 256)
                if i < 3:
                    mla_scores(2 * i + 2)
                    mla_scores(2 * i + 3)
                ada_folds(("mla", i))
                if i >= 1:
                    pair_out("mla", i - 1, yT[:, 4 + i - 1, :])
            ada(*ada_prev[0])
            pair_out("mla", 3, yT[:, 7, :])
            done(dve, ("ada1", 23))
            for d in range(8):
                full(dve, ("pn", d))
                full(dve, ("pm", d))
                t1, t2 = sqt[:, d % 2, 0:256], sqt[:, d % 2, 256:512]
                emptied(v.tensor_tensor(t1, bk(("pn", d))[:, 0:256], sgate[:, d, :], ALU.mult), ("pn", d))
                emptied(v.tensor_tensor(t2, bk(("pm", d))[:, 0:256], sgate[:, 8 + d, :], ALU.mult), ("pm", d))
                done(dve, ("pn", d))
                done(dve, ("pm", d))
                v.tensor_tensor(merged[:, d, :], t1, t2, ALU.add).then_inc(S("merged"), 1)

            def residual(name, d, lo, hi, gate, src=None):
                return v.scalar_tensor_tensor(out=xT[:, d, lo:hi], in0=bk(name)[:, lo:hi] if src is None else src, scalar=gate,
                                              in1=xT[:, d, lo:hi], op0=ALU.mult, op1=ALU.add)

            for d in range(8):
                full(dve, ("wo", d))
                emptied(residual(("wo", d), d, 0, 256, mod1[:, 16 + d:17 + d]), ("wo", d))
            done(dve, ("wo", 6))
            done(dve, ("wo", 7))
            signal("x1")
            link(v.scalar_tensor_tensor(out=gs[:, :, 0], in0=mod1[:, 32:40], scalar=1.0, in1=vv("g2"), op0=ALU.add, op1=ALU.mult))
            rms("n2", "sum2", D, 256, rstd)
            scale_tiles("h2", 256, lambda k, s: gs[:, k, 0:1])
            for t in range(TT):
                done(dve, ("rt", t))
            link(v.tensor_tensor(sel, lg, bc(vv("ebias"), [0, 2], [1, 64]), ALU.add))
            for t in range(TT):
                for g in range(GROUPS):
                    last = v.max(m8[:, t, g, :], sel[:, t, 8 * g:8 * g + 8])
            link(last)
            link(v.tensor_tensor(gsc, m8[:, :, :, 0], m8[:, :, :, 1], ALU.add))
            for t in range(TT):
                a0 = bc(gsc[:, t, :], [0, 8], [1, 8])
                a1 = bc(gsc[:, t, :], [1, 8], [0, 8])
                v.tensor_tensor(cmpa[:, t], a0, a1, ALU.is_gt)
                last = v.tensor_tensor(cmpb[:, t], a0, a1, ALU.is_equal)
            link(last)
            for t in range(TT):
                last = v.tensor_tensor(cmpb[:, t], cmpb[:, t], cc("gtri").rearrange("p (a b) -> p a b", a=8), ALU.mult)
            link(last)
            link(v.tensor_tensor(small[:, 400:528], small[:, 400:528], small[:, 528:656], ALU.add))
            link(v.tensor_reduce(small[:, 656:672], small[:, 400:528].rearrange("p (g b) -> p g b", b=8), AXX, ALU.add))
            link(v.tensor_scalar(small[:, 656:672], small[:, 656:672], float(TOPG) - 0.5, None, ALU.is_lt))
            link(v.tensor_scalar(small[:, 672:688], small[:, 656:672], -1.0, -NEG, ALU.add, ALU.mult))
            selg8 = small[:, 128:256].rearrange("p (g b) -> p g b", b=8)
            link(v.tensor_tensor(selg8, selg8, bc(small[:, 656:672], [1, 16], [0, 8]), ALU.mult))
            link(v.tensor_tensor(selg8, selg8, bc(small[:, 672:688], [1, 16], [0, 8]), ALU.add))
            for t in range(TT):
                last = v.max(top[:, t, :], sel[:, t, :])
            link(last)
            for t in range(TT):
                last = v.match_replace(out=rep[:, t, :], in_to_replace=top[:, t, :], in_values=sel[:, t, :], imm_value=-3e38)
            link(last)
            v.tensor_tensor(mask, rep, sel, ALU.not_equal).then_inc(S("mask"), 1)
            dve.wait_ge(S("mask"), 1)
            link(v.memset(gates, 0.0))
            link(v.tensor_tensor(gates[:, :, 0:64], lg, mask, ALU.mult))
            link(v.tensor_reduce(den[:, 2:4], gates[:, :, 0:64], AXX, ALU.add))
            link(v.reciprocal(den[:, 2:4], den[:, 2:4]))
            for t in range(TT):
                last = v.tensor_scalar(gates[:, t, 0:64], gates[:, t, 0:64], den[:, 2 + t:3 + t], 2.5, ALU.mult, ALU.mult)
            link(last)
            for gg in range(4):
                w0, t = 512 * (gg % 2), gg // 2
                dve.wait_ge(S("part_a"), gg + 1)
                v.tensor_tensor(htok[:, gg % 2, :], bk(("tk", gg))[:, :], hbf[:, 0, t, w0:w0 + 512], ALU.subtract).then_inc(S("rest_a"), 1)
                dve.wait_ge(S("part_b"), gg + 1)
                emptied(v.tensor_tensor(hbf[:, 2, t, w0:w0 + 512], htok[:, gg % 2, :], hbf[:, 1, t, w0:w0 + 512], ALU.subtract), ("tk", gg))
            for t in range(2):
                full(dve, ("shu", t))
                done(dve, ("shg", t))
                emptied(v.tensor_tensor(shu[:, t, :], bk(("shu", t))[:, 0:256], shg[:, t, :], ALU.mult), ("shu", t))
            done(dve, ("shu", 0))
            done(dve, ("shu", 1))
            signal("sh_act")
            for d in range(8):
                full(dve, ("shd", d))
                emptied(residual(("shd", d), d, 0, 256, mod1[:, 40 + d:41 + d]), ("shd", d))
            link(v.memset(posm, -1.0))
            full(dve, "pos")
            link(v.tensor_reduce(flag_f, bk("pos")[:, 128:192], AXX, ALU.max))
            link(v.scalar_tensor_tensor(out=pos1, in0=bk("pos")[:, 0:128].rearrange("p (a b) -> p a b", a=2), scalar=1.0,
                                        in1=mask, op0=ALU.add, op1=ALU.mult))
            emptied(v.tensor_copy(flag, flag_f), "pos")
            link(v.tensor_scalar(posm[:, :, 0:64], pos1, -1.0, None, ALU.add))
            signal("flag")
            link(v.scalar_tensor_tensor(out=near, in0=pos1, scalar=SLOTS + 0.5, in1=mask, op0=ALU.is_lt, op1=ALU.mult))
            link(v.tensor_tensor(rowf, pos1, bc(cc("eoff"), [0, 2], [1, 64]), ALU.add))
            link(v.tensor_tensor(rowf, rowf, near, ALU.mult))
            for t in range(TT):
                last = v.max(rtop[:, t, :], rowf[:, t, :])
            link(last)
            v.tensor_copy(ridx, rtop).then_inc(S("ridx"), 1)

            def moe_full(key, e):
                b = MOE_BANKS[key]
                dve.wait_ge(psum_full[b], e + (moe0[b] + 1))

            def pick(e, u, sem):
                for t in range(TT):
                    v.tensor_scalar(selb[:, u, t, :], cc("iota"), posm[:, t, bass.ds(e, 1)], None, ALU.is_equal)
                    last = v.tensor_scalar(selg[:, u, t, :], cc("iota"), posm[:, t, bass.ds(e, 1)], gates[:, t, bass.ds(e, 1)],
                                           ALU.is_equal, ALU.mult)
                last.then_inc(sem, 1)

            def gathered(e, u):
                moe_full("G1", e)
                v.tensor_copy(xg[:, u, 4 * SLOTS:9 * SLOTS], bank[MOE_BANKS["G1"]][:, 0:5 * SLOTS]).then_inc(psum_done[MOE_BANKS["G1"]], 1)

            def gate_row(u):
                return bc(xg[:, u, 8 * SLOTS:9 * SLOTS], [0, 2], [1, SLOTS])

            def expert(i, u):
                e = UN * i + u
                moe_full("Hu", e)
                b = MOE_BANKS["Hu"]
                v.tensor_tensor(upt[:, u, :].rearrange("p (a b) -> p a b", a=2),
                                bank[b][:, 0:2 * SLOTS].rearrange("p (a b) -> p a b", a=2), gate_row(u), ALU.mult).then_inc(psum_done[b], 1)
                dve.wait_ge(psum_done[b], e + (moe0[b] + 1))
                dve.wait_ge(psum_done[MOE_BANKS["Hg"]], e + (moe0[MOE_BANKS["Hg"]] + 1))
                v.tensor_tensor(aT[:, u, :], sgt[:, u, :], upt[:, u, :], ALU.mult).then_inc(S("act_ready"), 1)
                last = isinstance(i, int) and e == E - 1
                if not last:
                    gathered(e + 1, (u + 1) % UN)
                    pick(e + 2, (u + 2) % UN, S("sel_ready"))
                moe_full("D1", e)
                if not (isinstance(i, int) and i == 0):
                    dve.wait_ge(S(f"stored{u}"), 16 * i)
                b = MOE_BANKS["D1"]
                v.tensor_copy(yo[0:SLOTS, u, 512:1024], bank[b][0:SLOTS, :]).then_inc(psum_done[b], 1)

            pick(0, 0, S("sel_ready"))
            pick(1, 1, S("sel_ready"))
            gathered(0, 0)
            for u in range(UN):
                expert(0, u)
            with dve.Fori(1, TURNS) as i:
                for u in range(UN):
                    expert(i, u)
            for u in range(E - UN * TURNS):
                expert(TURNS, u)

            dve.wait_ge(S("flag"), 1)
            many = dve.value_load(flag[0:1, 0:1])
            with dve.If(many > SLOTS):
                for u in range(UN):
                    dve.wait_ge(S(f"stored{u}"), 16 * (TURNS + (1 if u < E - UN * TURNS else 0)))
                dve.wait_ge(psum_full[MOE_BANKS["D0"]], moe0[MOE_BANKS["D0"]] + E)
                for r in range(1, ROUNDS):
                    v.tensor_scalar(posm[:, :, 0:64], posm[:, :, 0:64], -float(SLOTS), None, ALU.add).then_inc(S("ov_shift"), 1)
                    dve.wait_ge(S("ov_shift"), r)
                    with dve.Fori(0, E) as e:
                        n = e + E * (r - 1)
                        v.tensor_copy(mark[0:1, 31:32], mark[0:1, 0:1]).then_inc(S("ov_go"), 1)
                        pick(e, 0, S("ov_sel"))
                        dve.wait_ge(S("ov_pe"), 3 * n + 1)
                        v.tensor_copy(xg[:, 0, 0:4 * SLOTS], bank[0][:, 0:4 * SLOTS])
                        v.tensor_copy(xg[:, 0, 4 * SLOTS:9 * SLOTS], bank[1][:, 0:5 * SLOTS]).then_inc(S("ov_xg"), 1)
                        dve.wait_ge(S("ov_pe"), 3 * n + 2)
                        dve.wait_ge(S("ov_xg"), n + 1)
                        v.tensor_tensor(upt[:, 0, :].rearrange("p (a b) -> p a b", a=2),
                                        bank[3][:, 0:2 * SLOTS].rearrange("p (a b) -> p a b", a=2), gate_row(0), ALU.mult).then_inc(S("ov_up"), 1)
                        dve.wait_ge(S("ov_up"), n + 1)
                        dve.wait_ge(S("ov_silu"), n + 1)
                        v.tensor_tensor(aT[:, 0, :], sgt[:, 0, :], upt[:, 0, :], ALU.mult).then_inc(S("ov_act"), 1)
                        dve.wait_ge(S("ov_pe"), 3 * n + 3)
                        v.tensor_copy(yo[0:SLOTS, 0, 0:512], bank[4][0:SLOTS, :])
                        v.tensor_copy(yo[0:SLOTS, 0, 512:1024], bank[5][0:SLOTS, :]).then_inc(S("ov_y"), 1)
                        dve.wait_ge(S("ov_stored"), 16 * n + 16)
                over = [0]

                def ov_link(ins):
                    over[0] += 1
                    ins.then_inc(S("ov_step"), 1)
                    dve.wait_ge(S("ov_step"), over[0])

                ov_link(v.scalar_tensor_tensor(out=rowf, in0=bc(cc("eoff"), [0, 2], [1, 64]), scalar=float(ROUNDS - 1), in1=pos1,
                                               op0=ALU.mult, op1=ALU.add))
                ov_link(v.tensor_tensor(near, mask, near, ALU.subtract))
                ov_link(v.scalar_tensor_tensor(out=rowf, in0=rowf, scalar=-float(SLOTS), in1=near, op0=ALU.add, op1=ALU.mult))
                for t in range(TT):
                    ov_link(v.max(rtop[:, t, :], rowf[:, t, :]))
                v.tensor_copy(ridx2, rtop).then_inc(S("ov_ridx"), 1)

            for t in range(TT):
                for k in range(TOPK):
                    n = TOPK * t + k
                    dve.wait_ge(S(f"rows_in{n % 3}"), 16 * (n // 3 + 1))
                    if k:
                        dve.wait_ge(S("acc"), n)
                        ins = v.tensor_tensor(acc[:, t, :], acc[:, t, :], gat[:, n % 3, :], ALU.add)
                    else:
                        ins = v.tensor_copy(acc[:, t, :], gat[:, n % 3, :])
                    ins.then_inc(S("acc"), 1)
            with dve.If(many > SLOTS):
                for n in range(TT * TOPK):
                    dve.wait_ge(S("ov_rows"), 16 * n + 16)
                    v.tensor_tensor(acc[:, n // TOPK, :], acc[:, n // TOPK, :], gat[:, 0, :], ALU.add).then_inc(S("ov_acc"), 1)
                    dve.wait_ge(S("ov_acc"), n + 1)
            signal("acc_final")
            done(dve, ("shd", 7))
            done(dve, ("shd", 6))
            for g in range(4):
                t, hf = g // 2, g % 2
                full(dve, ("ac", g))
                for k in range(4):
                    d = 4 * hf + k
                    last = residual(None, d, P * t, P * t + P, mod1[:, 40 + d:41 + d], src=bk(("ac", g))[:, P * k:P * k + P])
                emptied(last, ("ac", g))
            done(dve, ("ac", 2))
            done(dve, ("ac", 3))
            signal("x2")

            def gains(layer):
                g = vv("ng2", 8 * layer, 8 * layer + 8)
                link(v.scalar_tensor_tensor(out=gs[:, :, :], in0=mod2[:, 24 * layer + 8:24 * layer + 16, :], scalar=1.0,
                                            in1=bc(g, [1, 8], [0, 2]), op0=ALU.add, op1=ALU.mult))

            done(dve, ("ada2", 23))
            dve.wait_ge(S("const2_in"), 32)
            gains(0)
            rms("n3", "sum3", D, 512, rstd)
            scale_tiles("h3", 512, lambda k, s: gs[:, k, s:s + 1])
            for t in range(4):
                for s in range(2):
                    done(dve, (f"vab{s}", t))
                link(v.bn_stats(bn[:, t, 0:6], vtok[:, t, :]))
                link(v.bn_aggr(bn[:, t, 12:14], bn[:, t, 0:6]))
            link(v.tensor_scalar(bn[:, :, 13], bn[:, :, 13], EPS, None, ALU.add))
            signal("v_ms")
            dve.wait_ge(S("v_rt"), 1)
            link(v.reciprocal(bn[:, :, 13], bn[:, :, 13]))
            for t in range(4):
                v.tensor_scalar(vtok[:, t, :], vtok[:, t, :], bn[:, t, 12:13], bn[:, t, 13:14],
                                ALU.subtract, ALU.mult).then_inc(S("v_norm"), 1)
            for n in range(8):
                g, st = n // 2, n % 2
                full(dve, ("fb", n))
                done(dve, (f"z{2 + g // 2}", g % 2))
                z = zT[:, 4 + g, 256 * st:256 * st + 256]
                emptied(v.tensor_tensor(z, z, bk(("fb", n))[:, 0:256], ALU.mult), ("fb", n))
            for h in range(4):
                full(dve, ("sp", h))
                t1 = smt[:, h % 2, :]
                emptied(v.scalar_tensor_tensor(out=t1.rearrange("p (a b) -> p a b", a=4),
                                               in0=bk(("sp", h))[:, :].rearrange("p (a b) -> p a b", a=4), scalar=vv("vg", h, h + 1),
                                               in1=bc(vv("sb", P * h, P * h + P), [0, 4], [1, P]), op0=ALU.mult, op1=ALU.add), ("sp", h))
                done(dve, ("sp", h))
                done(dve, (f"z{4 + h // 2}", h % 2))
                done(dve, (f"z{6 + h // 2}", h % 2))
                link(v.tensor_tensor(t1, t1, zT[:, 8 + h, :], ALU.mult))
                v.tensor_tensor(zT[:, h, :], zT[:, h, :], t1, ALU.mult).then_inc(S("y_a"), 1)
            for d in range(8):
                full(dve, ("oab", d))
                residual(("oab", d), d, 0, 256, mod2[:, 16 + d, 0:1])
                emptied(residual(("oab", d), d, 256, 512, mod2[:, 16 + d, 1:2]), ("oab", d))
            done(dve, ("oab", 6))
            done(dve, ("oab", 7))
            signal("x3")
            gains(1)
            rms("n4", "sum4", D, 512, rstd)
            scale_tiles("h4", 512, lambda k, s: gs[:, k, s:s + 1])
            for j in range(10):
                full(dve, ("sw", j))
                src = k2[:, j, 0:256] if j < 2 else q2[:, j - 2, :]
                t1, t2 = rt1[:, j % 4, :], rt2[:, j % 4, :]
                emptied(v.tensor_tensor(t1, bk(("sw", j))[:, 0:256], cc("sin2"), ALU.mult), ("sw", j))
                link(v.tensor_tensor(t2, src, cc("cos2"), ALU.mult))
                done(dve, ("sw", j))
                v.tensor_tensor(src, t1, t2, ALU.add).then_inc(S("rope2"), 1)

            def c_scores(h):
                if h >= 4:
                    for j in range(2):
                        full(dve, ("c", "t", h - 4, j))
                for t in range(TT):
                    full(dve, ("c", "s", h, t))
                    emptied(v.scalar_tensor_tensor(out=probs("c", h)[:, 512 * t:512 * t + 512], in0=bk(("c", "s", h, t))[:, :], scalar=0.125,
                                                   in1=cc("wmask", 512 * t, 512 * t + 512), op0=ALU.mult, op1=ALU.add), ("c", "s", h, t))
                for t in range(TT):
                    done(dve, ("c", "s", h, t))
                a = att[:, h % 4, :]
                sink = bc(vv("sink", h, h + 1), [0, 2])
                link(v.tensor_reduce(a[:, 0:2], probs("c", h).rearrange("p (a b) -> p a b", a=2), AXX, ALU.max))
                link(v.tensor_tensor(a[:, 0:2], a[:, 0:2], sink, ALU.max))
                link(v.tensor_scalar(a[:, 2:4], a[:, 0:2], -1.0, None, ALU.mult))
                v.tensor_tensor(a[:, 0:2], sink, a[:, 2:4], ALU.add).then_inc(S("c_negmax"), 1)

            def c_out(i):
                full(dve, ("c", "o", i))
                done(dve, (f"g2{i // 2}", i % 2))
                emptied(v.tensor_tensor(o2[:, i, :], bk(("c", "o", i))[:, 0:256], g2s[:, i, :], ALU.mult), ("c", "o", i))

            c_scores(0)
            c_scores(1)
            for i in range(8):
                if i < 7:
                    c_scores(2 * i + 2)
                    c_scores(2 * i + 3)
                for h in (2 * i, 2 * i + 1):
                    dve.wait_ge(S("c_exp"), h + 1)
                    a = att[:, h % 4, :]
                    link(v.tensor_tensor(a[:, 4:6], a[:, 4:6], a[:, 6:8], ALU.add))
                    normalise("c", h, 512)
                if i >= 1:
                    c_out(i - 1)
            c_out(7)
            for d in range(8):
                full(dve, ("oc", d))
                emptied(residual(("oc", d), d, 0, 256, mod2[:, 40 + d, 0:1]), ("oc", d))
            done(dve, ("oc", 6))
            done(dve, ("oc", 7))
            signal("x4")
            rms("n5", "sum5", D, 256, rstd)
            for k in range(KT):
                v.scalar_tensor_tensor(out=outT[:, k, :], in0=xT[:, k, 0:256], scalar=vv("fg", k, k + 1), in1=rstd[:, 0:256],
                                       op0=ALU.mult, op1=ALU.mult).then_inc(S("y_out"), 1)


SLAB_COUNTS = dict(ada1=24, ada2=24, uq=1, ukv=1, pna=2, pmla=2, out=4, shg=1, shu=1, shd=1, ab=10, oab=4, cin=10, oc=4)
SLAB_COUNTS["in"] = 16
slabs_at, _n = {}, 0
for _k, _c in SLAB_COUNTS.items():
    slabs_at[_k] = _n
    _n += _c


def shape_constants():
    c, c2 = np.zeros((P, C_W), np.float64), np.zeros((P, C2_W), np.float64)

    def put(name, a):
        to, (lo, hi) = (c, C_AT[name]) if name in C_AT else (c2, C2_AT[name])
        a = np.asarray(a, np.float64)
        to[:a.shape[0], lo:hi] = a.reshape(a.shape[0], -1)

    i = np.arange(P)
    put("ident", np.eye(P))
    put("fold", np.stack([i % 32 == 0, i % 32 == 1], 1))
    put("bones", (i[:, None] // 64) == (i[None, :] // 64))
    m = np.zeros((96, 96))
    for r in range(16):
        m[80 + r, 64 + r] = -1.0
        m[64 + r, 80 + r] = 1.0
    put("perm96", m)
    m = np.zeros((P, P))
    for blk in range(4):
        for r in range(16):
            m[32 * blk + 16 + r, 32 * blk + r] = -1.0
            m[32 * blk + r, 32 * blk + 16 + r] = 1.0
    put("perm128", m)
    put("tri", i[:, None] < i[None, :])
    put("iota", np.tile(np.arange(SLOTS), (P, 1)))
    ang = TWO_PI * np.outer(i, i) / P
    put("dft_c", np.concatenate([np.cos(ang), -np.sin(ang)], 1))
    t = np.arange(T)
    angl = TWO_PI * (np.outer(t, t) % T) / T
    norm = 1 / np.sqrt(T * P)
    lt = np.stack([np.cos(angl), np.sin(angl)], 1) * norm
    put("dft_l", lt.reshape(2, P, 2, T).transpose(1, 0, 2, 3))
    inv = 10000.0 ** (-np.arange(16) / 16)
    row, col = np.repeat(np.arange(4), 64), np.tile(np.arange(64), 4)
    d = i % 64
    a2 = np.where((d < 32)[:, None], row[None, :], col[None, :]) * inv[d % 16][:, None]
    put("cos2", np.cos(a2))
    put("sin2", np.sin(a2))
    q = (np.arange(2)[None, :, None] * P + i[:, None, None])
    k = np.arange(T)[None, None, :]
    put("wmask", np.concatenate([np.where(np.abs(q - k) <= 128, 0.0, NEG), np.zeros((P, 2, T))], 2))
    cq, ck = (i % 64)[:, None], np.arange(64)[None, :]
    st = np.clip(cq - 8, 0, 48)
    put("namask", np.where((ck >= st) & (ck < st + 16), 0.0, NEG))
    put("invf", np.concatenate([np.zeros(64), inv, inv])[:, None])
    g = np.arange(8)
    put("gtri", np.broadcast_to((g[None, :] < g[:, None]).reshape(1, 64), (P, 64)))
    put("eoff", np.broadcast_to(float(SLOTS) * np.arange(64)[None, :], (P, 64)))
    return c.astype(np.float32), c2.astype(np.float32)


def kernel(**inputs):
    import concourse.bacc as bacc
    from concourse.bass_utils import run_bass_kernel_spmd as run

    x = {k: np.asarray(v) for k, v in inputs.items()}

    def cols(a):
        return a.reshape(-1, P).T

    def rows(a):
        return np.broadcast_to(a.reshape(1, -1), (P, a.size))

    def pad96(a):
        return np.pad(a, (0, P - a.size))[:, None]

    c2 = np.stack([cols(x["c_2"][0]), cols(x["c_ctx_2"])], 2).reshape(P, 16)
    vec = dict(c=cols(x["c"][0]), c2=c2, b_ada=cols(x["b_ada"][0]), g1=cols(x["g_norm1"][0]),
               gq=np.tile(x["g_na_q"][0], 2)[:, None], gk=np.tile(x["g_na_k"][0], 2)[:, None],
               gql=cols(x["g_q_lat"][0]), gkv=cols(x["g_kv_lat"][0]), gmq=pad96(x["g_mla_q"][0]), gmk=pad96(x["g_mla_k"][0]),
               g2=cols(x["g_norm2"][0]), ng2=cols(x["norm_g_2"]), b2=cols(x["ada_b_2"]), vg=cols(x["v_norm_g_2"][0]),
               fg=cols(x["final_g_2"]), ebias=rows(x["e_bias"][0]), sb=rows(x["spatial_b_2"][0]))
    order = np.array([8 * (j // 8) + 4 * (j % 2) + (j % 8) // 2 for j in range(16)])
    vec["sink"] = rows(x["sink_logit_2"][0][order])
    vecs = np.concatenate([vec[k] for k in V_WIDTHS], 1)
    xT = np.concatenate([x["x"][0], x["ctx_2"][0]], 0).reshape(512, 8, P).transpose(2, 1, 0)

    def slab8(w):
        return w.reshape(8, P, -1, 256).transpose(2, 1, 0, 3).reshape(-1, P, SLAB)

    def slabk(w, k):
        w = w.reshape(k, P, -1, SLAB // k).transpose(2, 1, 0, 3)
        return w.reshape(-1, P, SLAB)

    w_in = np.pad(x["w_in"][0], ((0, 0), (0, 96)))
    w_in = np.concatenate([w_in[:, :1952], w_in[:, 4000:], w_in[:, 1952:4000]], 1)
    ukv = x["w_ukv"][0].reshape(P, 8, 2, 64).transpose(0, 2, 1, 3).reshape(P, 1024)
    ab = x["w_in_ab_2"][0]
    ab = np.concatenate([ab[:, 512:1024], ab[:, 1536:2048], ab[:, 2048:2560], ab[:, :512], ab[:, 1024:1536]], 1)
    cin = x["w_in_c_2"][0]
    by_head = lambda w: w.reshape(1024, 16, 64)[:, order].reshape(1024, 1024)
    cin = np.concatenate([cin[:, 1024:1536], by_head(cin[:, :1024]), by_head(cin[:, 1536:])], 1)
    oc = x["w_out_c_2"][0].reshape(16, 64, 1024)[order].reshape(1024, 1024)
    part = dict(ada1=slab8(x["w_ada"][0]), ada2=np.concatenate([slab8(x["ada_w_2"][0]), slab8(x["ada_w_2"][1])]),
                uq=np.pad(x["w_uq"][0].reshape(2, P, 768).transpose(1, 0, 2).reshape(1, P, 1536), ((0, 0), (0, 0), (0, 512))),
                ukv=np.pad(ukv, ((0, 0), (0, 1024)))[None],
                pna=slabk(x["w_proj_na"][0], 4), pmla=slabk(x["w_proj_mla"][0], 4), out=slab8(x["w_out"][0]),
                shg=slab8(x["w_sh_gate"][0]), shu=slab8(x["w_sh_up"][0]), shd=slabk(x["w_sh_down"][0], 2),
                ab=slab8(ab), oab=slab8(x["w_out_ab_2"][0]), cin=slab8(cin), oc=slab8(oc))
    part["in"] = slab8(w_in)
    stream = np.concatenate([part[k] for k in SLAB_COUNTS], 0)

    def per_expert(w, k):
        return w.reshape(E, k, P, SLAB // k).transpose(0, 2, 1, 3).reshape(E, 1, P, SLAB)

    experts = np.concatenate([per_expert(x["w_exp_gate"][0], 8), per_expert(x["w_exp_up"][0], 8), per_expert(x["w_exp_down"][0], 2)], 1)
    consts, consts2 = shape_constants()
    arrays = dict(
        xT=xT, consts=consts, consts2=consts2, vecs=vecs, positions=np.broadcast_to(x["positions"], (96, T)),
        rpb=x["na_rpb"][0][:, :, ::-1],
        spatial=x["spatial_w_2"][0].transpose(2, 0, 1), router=x["w_router"][0].reshape(8, P, E).transpose(1, 0, 2),
        stream=stream, experts=experts)
    arrays = {k: np.ascontiguousarray(v) for k, v in arrays.items()}
    nc = bacc.Bacc("TRN2", target_bir_lowering=False, num_devices=1)
    t = {k: nc.dram_tensor(k, v.shape, mybir.dt.from_np(v.dtype), kind="ExternalInput").ap() for k, v in arrays.items()}
    out = nc.dram_tensor("out", (P, KT, T), F32, kind="ExternalOutput").ap()
    rows_d = nc.dram_tensor("expert_rows", (1 + E * SLOTS, D), F32).ap()
    more_d = nc.dram_tensor("later_rows", (1 + E * SLOTS * (ROUNDS - 1), D), F32).ap()
    build(nc, t["xT"], t["consts"], t["consts2"], t["vecs"], t["positions"], t["rpb"], t["spatial"], t["router"], t["stream"], t["experts"], out, rows_d, more_d)
    r = run(nc, [arrays], core_ids=[0])
    return np.ascontiguousarray(r.results[0]["out"].transpose(2, 1, 0)).reshape(1, T, D)
```

```python
from contextlib import ExitStack

import numpy as np
import concourse.bass as bass
from concourse import mybir

ALU = mybir.AluOpType
ACT = mybir.ActivationFunctionType
F32 = mybir.dt.float32
BF16 = mybir.dt.bfloat16
I32 = mybir.dt.int32
U32 = mybir.dt.uint32
AXX = mybir.AxisListType.X

P = 128
D = 1024
KT = D // P
T = 256
TT = T // P
E = 64
TOPK = 8
GROUPS = 8
TOPG = 4
FF = 256
SLOTS = 64
ROUNDS = T // SLOTS
SLAB = 2048
RING = 9
PER_E = 3
UN = 2
TURNS = E // UN
MORE = 32
NONE = ROUNDS * E
EPS = 1e-6
NEG = -1e30
TWO_PI = 2 * np.pi
RUN = 5 * 31 + 64

C_WIDTHS = dict(fold=2, ident=P, bones=P, perm96=96, tri=P, iota=2 * SLOTS, namask=64, invf=1, gtri=64,
                codes=(ROUNDS - 1) * E)
C2_WIDTHS = dict(perm128=P, dft_c=256, dft_l=4 * 256, cos2=256, sin2=256, wmask=2 * 512)
V_WIDTHS = dict(c=8, c2=16, b_ada=48, g1=8, gq=1, gk=1, gql=2, gkv=1, gmq=1, gmk=1, g2=8, ng2=16,
                b2=48, vg=4, fg=8, ebias=64, sink=16, sb=512)


def offsets(widths):
    at, out = 0, {}
    for k, w in widths.items():
        out[k] = (at, at + w)
        at += w
    return out, at


C_AT, C_W = offsets(C_WIDTHS)
C2_AT, C2_W = offsets(C2_WIDTHS)
V_AT, V_W = offsets(V_WIDTHS)


def build(nc, xT_d, consts_d, consts2_d, vecs_d, pos_d, rpb_d, spat_d, router_d, slabs_d, exp_d, out_d):
    with ExitStack() as ctx:
        def sb(name, shape, dt=F32):
            return ctx.enter_context(nc.sbuf_tensor(name, shape, dt))

        sems = {}

        def S(name):
            if name not in sems:
                sems[name] = ctx.enter_context(nc.semaphore(name))
            return sems[name]

        ring = sb("ring", [P, RING, SLAB])
        xT = sb("resid", [P, KT, 2 * T])
        hT = sb("hT", [P, KT, 2 * T])
        cs = sb("cs", [P, C_W])
        ve = sb("ve", [P, V_W])
        silc = sb("silc", [P, 8, 32])
        silc2 = sb("silc2", [P, 8, 32])
        quarters = sb("quarters", [P, 2, 256])
        mod1 = sb("mod1", [P, 48])
        mod2 = sb("mod2", [P, 48, 2])
        gs = sb("gs", [P, 8, 2])
        ones = sb("ones", [P, P])
        rstd = sb("rstd", [P, 512])
        stat = sb("stat", [P, 512])
        arena = sb("arena", [P, 17632])

        def ar(at, n, *dims, parts=P, lo=0):
            v = arena[lo:lo + parts, at:at + n]
            if len(dims) == 2:
                v = v.rearrange("p (a b) -> p a b", a=dims[0])
            if len(dims) == 3:
                v = v.rearrange("p (a b c) -> p a b c", a=dims[0], b=dims[1])
            return v

        def cc(name, a=0, b=None):
            src, at = (cs, C_AT) if name in C_AT else (cs2, C2_AT)
            lo, hi = at[name]
            return src[:, lo + a:(hi if b is None else lo + b)]

        def vv(name, a=0, b=None):
            lo, hi = V_AT[name]
            return ve[:, lo + a:(hi if b is None else lo + b)]

        qk = ar(0, 2048, 8, 256)
        vna = ar(2048, 1024, 2, 512)
        lat = ar(3072, 1024, 4, 256)
        sgate = ar(4096, 4096, 16, 256)
        qm = ar(8192, 2048, 8, 256)
        km = ar(10240, 2048, 8, 256)
        vm = ar(12288, 1024, 2, 512)
        yT = qk
        merged = qm
        var = hT[:, 4:8, :].rearrange("p a b -> p (a b)")
        sqt = ar(13312, 1024, 2, 512)
        braw = ar(14336, 8 * RUN, 8, RUN)
        bmask = ar(16096, 1024, 2, 512)
        rope_c = ar(17120, 256)
        rope_s = ar(17376, 256)
        pr = sb("pr", [P, 2, 1024])
        pT = sb("pT", [P, 2, 1024])
        att = sb("att", [P, 4, 8])
        small = pT[:, :, :].rearrange("p a b -> p (a b)")
        hbf = arena[:, 0:3072].bitcast(BF16).rearrange("p (q t d) -> p q t d", q=3, t=2)
        htok = ar(3072, 1024, 2, 512)
        xg = ar(4096, 2 * 512, 2, 512)
        selb = ar(5120, 128).bitcast(BF16).rearrange("p (u t s) -> p u t s", u=2, t=2)
        selg = ar(5248, 512, 2, 2, 128)
        sgt = ar(5760, 256, 2, 128)
        hid = ar(6016, 256, 2, 128)
        aT = ar(6272, 256, 2, 128)
        selT = ar(6528, 512, 2, 2, 128)
        yo = ar(7040, 1024, 2, 512)
        acc = ar(8064, 2 * 1024, 2, 1024)
        shg = ar(12352, 512, 2, 256)
        shu = ar(12864, 512, 2, 256)
        small2 = pr[:, :, :].rearrange("p a b -> p (a b)")
        posx = small2[:, 0:2 * NONE + 2].rearrange("p (a b) -> p a b", a=2)
        gatx = small2[:, 514:514 + 2 * NONE + 2].rearrange("p (a b) -> p a b", a=2)
        counts = small2[:, 1028:1092]
        keys = small2[:, 1092:1092 + (ROUNDS - 1) * E]
        klist = small2[:, 1284:1284 + MORE + UN]
        clist = small2[:, 1320:1320 + MORE + UN]
        elist = small2[:, 1356:1356 + MORE + UN]
        lcmp = small2[:, 1392:1392 + MORE + UN]
        codes = small2[:, 1428:1428 + MORE + UN].bitcast(I32)
        whose = small2[:, 1464:1464 + MORE + UN].bitcast(I32)
        nturn_f = small2[:, 1500:1501]
        nturn = small2[:, 1501:1502].bitcast(I32)
        lg = small[:, 0:128].rearrange("p (a b) -> p a b", a=2)
        sel = small[:, 128:256].rearrange("p (a b) -> p a b", a=2)
        m8 = small[:, 256:384].rearrange("p (a g b) -> p a g b", a=2, g=8)
        gsc = small[:, 384:400].rearrange("p (a b) -> p a b", a=2)
        cmpa = small[:, 400:528].rearrange("p (a g b) -> p a g b", a=2, g=8)
        cmpb = small[:, 528:656].rearrange("p (a g b) -> p a g b", a=2, g=8)
        gmk = small[:, 656:672].rearrange("p (a b) -> p a b", a=2)
        gpen = small[:, 672:688].rearrange("p (a b) -> p a b", a=2)
        top = small[:, 688:704].rearrange("p (a b) -> p a b", a=2)
        rep = small[:, 704:832].rearrange("p (a b) -> p a b", a=2)
        mask = small[:, 832:960].rearrange("p (a b) -> p a b", a=2)
        pos1 = small[:, 1224:1352].rearrange("p (a b) -> p a b", a=2)
        den = small[:, 1480:1484]
        wr = sb("wr", [P, 8, 64])
        mark = sb("mark", [1, 32])
        zT = ar(0, 8192, 16, 512)
        vtok = ar(8192, 2048, 4, 512)
        fa = ar(10240, 1024, 2, 512)
        smt = ar(11264, 1024, 2, 512)
        cs2 = ar(13376, C2_W)
        spat = ar(13376 + C2_W, 512, 4, 128)
        bn = ar(12800, 64, 4, 16)
        q2 = ar(0, 2048, 8, 256)
        g2s = ar(2048, 2048, 8, 256)
        k2 = ar(4096, 1024, 2, 512)
        v2 = ar(5120, 1024, 4, 256)
        o2 = ar(6144, 2048, 8, 256)
        rt1 = ar(8192, 1024, 4, 256)
        rt2 = ar(9216, 1024, 4, 256)
        outT = ar(0, 2048, 8, 256)

        bank = [ctx.enter_context(nc.psum_tensor(f"bank{b}", [P, 512], F32)) for b in range(8)]
        psum_full = [S(f"psum_full{b}") for b in range(8)]
        psum_done = [S(f"psum_done{b}") for b in range(8)]
        uses = [0] * 8
        place = {}

        def full(eng, name):
            b, n = place[name]
            eng.wait_ge(psum_full[b], n + 1)

        def done(eng, name):
            b, n = place[name]
            eng.wait_ge(psum_done[b], n + 1)

        def bk(name):
            return bank[place[name][0]]

        def emptied(ins, name):
            ins.then_inc(psum_done[place[name][0]], 1)

        slab_in = [S(f"slab_in{k}") for k in range(RING)]
        slabs = []
        slab_end = []

        def na_head(h):
            b = 64 * (h % 2)
            return dict(q=lambda t: qk[b:b + 64, h // 2, t * P:(t + 1) * P], k=[qk[b:b + 64, 4 + h // 2, :]],
                        v=lambda j: vna[:, j, 64 * h:64 * h + 64], o=b)

        def mla_head(h):
            return dict(q=lambda t: qm[0:96, h, t * P:(t + 1) * P], k=[km[0:96, h, :]],
                        v=lambda j: vm[:, j, 64 * h:64 * h + 64], o=64 * (h % 2))

        def c_head(h):
            b, g = 64 * (h % 2), h // 8
            return dict(q=lambda t: q2[b:b + 64, h // 2, t * P:(t + 1) * P], k=[k2[b:b + 64, g, :]],
                        v=lambda j: v2[:, j, 128 * g + b:128 * g + b + 64], o=b)

        KINDS = dict(na=(8, na_head, 256), mla=(8, mla_head, 256), c=(16, c_head, 512))

        def probs(kind, h):
            if kind == "c":
                return ar(9216 + 1024 * (h % 4), 1024)
            return pr[:, (h % 4) // 2, 512 * (h % 2):512 * (h % 2) + 512]

        fillers = [("ada1", j) for j in range(8, 24)] + [("ada2", j) for j in range(24)]
        FILL = {("na", i): fillers[6 * i:6 * i + 6] for i in range(4)}
        FILL.update({("mla", i): fillers[24 + 4 * i:28 + 4 * i] for i in range(4)})

        B_G, B_GU, B_D, B_X = 4, 5, 6, 7
        ITEM_USE = ("gu_full", "gu_full", "d_full")
        loads = []

        block = ctx.enter_context(nc.Block())

        @block.tensor
        def _(pe):
            mmul = nc.tensor.matmul

            def open_group(name, b):
                if uses[b]:
                    pe.wait_ge(psum_done[b], uses[b])
                place[name] = (b, uses[b])
                uses[b] += 1
                return bank[b]

            def close_group(ins, name):
                ins.then_inc(psum_full[place[name][0]], 1)

            def take_slab(src):
                n = len(slabs)
                slabs.append(src)
                slab_end.append(None)
                loads.append(1 + sum(m % RING == n % RING and slabs[m][0] != "exp" for m in range(n)))
                pe.wait_ge(slab_in[n % RING], 16 * loads[n])
                return ring[:, n % RING, :], n

            def ada_slab(which, j):
                w, n = take_slab((which, j))
                w = w.rearrange("p (k c) -> p k c", k=8)
                name = (which, j, "quarters")
                o = open_group(name, 6)
                for kk in range(2):
                    for g in range(4):
                        mm = mmul(o[32 * g:32 * g + 32, 0:256], (silc if which == "ada1" else silc2)[:, 4 * kk + g, :],
                                  w[:, 4 * kk + g, :], start=(kk == 0), stop=(kk == 1))
                close_group(mm, name)
                slab_end[n] = name
                if ada_prev:
                    ada_fold(*ada_prev.pop())
                ada_prev.append((which, j))

            ada_prev = []

            def ada_fold(which, j):
                done(pe, (which, j, "quarters"))
                o = open_group((which, j), 7)
                width = 1 if which == "ada1" else 2
                for t in range(2):
                    mm = mmul(o[:, t * width:(t + 1) * width], quarters[:, j % 2, t * P:(t + 1) * P], cc("fold", 0, width),
                              start=True, stop=True)
                close_group(mm, (which, j))

            def rms_sums(name, b, n_tok, tiles=KT, src=None):
                o = open_group(name, b)
                for k in range(tiles):
                    mm = mmul(o[:, 0:n_tok], ones[:], hT[:, k, 0:n_tok] if src is None else src(k),
                              start=(k == 0), stop=(k == tiles - 1))
                close_group(mm, name)

            def t_tiles(tag, src, n_tiles, b, n_tok, rows=P, lo=0):
                w, n = take_slab(src)
                w = w.rearrange("p (k c) -> p k c", k=8)
                for t in range(n_tiles):
                    name = (tag, t)
                    o = open_group(name, b[t % len(b)])
                    for k in range(KT):
                        mm = mmul(o[:, 0:n_tok], w[:, k, t * P:(t + 1) * P], hT[:, k, 0:n_tok],
                                  start=(k == 0), stop=(k == KT - 1))
                    close_group(mm, name)
                slab_end[n] = name

            def tok_tiles(tag, src, toks, b):
                w, n = take_slab(src)
                w = w.rearrange("p (k c) -> p k c", k=8)
                for t in range(toks):
                    name = (tag, t)
                    o = open_group(name, b[t % len(b)])
                    for k in range(KT):
                        mm = mmul(o[:, 0:256], hT[:, k, t * P:(t + 1) * P], w[:, k, :],
                                  start=(k == 0), stop=(k == KT - 1))
                    close_group(mm, name)
                slab_end[n] = name

            def attention(kind):
                n_heads, head, nk = KINDS[kind]
                per = nk // 256

                def scores(i):
                    for t in range(TT):
                        for h in (2 * i, 2 * i + 1):
                            hd = head(h)
                            if nk == 256:
                                name = (kind, "s", h)
                                if t == 0:
                                    open_group(name, h % 2)
                                mm = mmul(bk(name)[:, 256 * t:256 * t + 256], hd["q"](t), hd["k"][0], start=True, stop=True)
                                if t == 1:
                                    close_group(mm, name)
                            else:
                                name = (kind, "s", h, t)
                                o = open_group(name, (0 if h % 2 == 0 else 6) + t)
                                close_group(mmul(o[:, :], hd["q"](t), hd["k"][0], start=True, stop=True), name)

                def turn(h):
                    pe.wait_ge(S(kind + "_probs"), h + 1)
                    for j in range(per):
                        name = (kind, "t", h, j)
                        o = open_group(name, 2 + (h % 2 if per == 1 else j))
                        for kt in range(2):
                            for t in range(TT):
                                at = t * nk + (2 * j + kt) * P
                                mm = nc.tensor.transpose(o[:, 256 * kt + P * t:256 * kt + P * t + P],
                                                         probs(kind, h)[:, at:at + P], cc("ident"))
                        close_group(mm, name)

                def values(i):
                    name = (kind, "o", i)
                    o = open_group(name, 4 + i % 2)
                    for h in (2 * i, 2 * i + 1):
                        for j in range(per):
                            done(pe, (kind, "t", h, j))
                    for kt in range(2 * per):
                        for h in (2 * i, 2 * i + 1):
                            hd = head(h)
                            mm = mmul(o[hd["o"]:hd["o"] + 64, 0:256], hd["v"](kt), pT[:, h % 2, 256 * kt:256 * kt + 256],
                                      start=(kt == 0), stop=(kt == 2 * per - 1))
                    close_group(mm, name)

                scores(0)
                for i in range(n_heads // 2):
                    if 2 * i + 2 < n_heads:
                        scores(i + 1)
                    for f in FILL.get((kind, i), []):
                        ada_slab(*f)
                    turn(2 * i)
                    turn(2 * i + 1)
                    values(i)

            pe.wait_ge(S("silu_c"), 1)
            pe.wait_ge(S("const_in"), 48)
            for j in range(8):
                ada_slab("ada1", j)
            ada_fold(*ada_prev.pop())
            pe.wait_ge(S("ones_set"), 1)
            pe.wait_ge(S("const_in"), 48)
            pe.wait_ge(S("sq1"), 1)
            rms_sums("sum1", 0, 256)
            pe.wait_ge(S("h1"), 8)
            for s in range(4):
                t_tiles(f"qk{s}", ("in", s), 2, [1, 2], 256)
                for t in range(2):
                    j = 2 * s + t
                    pe.wait_ge(S("sq_qk"), j + 1)
                    o = open_group(("qkn", j), 3 + j % 2)
                    close_group(mmul(o[:, 0:256], cc("bones"), sqt[:, j % 2, 0:256], start=True, stop=True), ("qkn", j))
            for s in range(2):
                tok_tiles(f"vna{s}", ("in", 4 + s), 2, [1, 2])
            t_tiles("ql", ("in", 6), 2, [1, 2], 256)
            w, n = take_slab(("in", 7))
            w = w.rearrange("p (k c) -> p k c", k=8)
            o = open_group("kvl", 3)
            for k in range(KT):
                mm = mmul(o[:, 0:256], w[:, k, 0:P], hT[:, k, 0:256], start=(k == 0), stop=(k == KT - 1))
            close_group(mm, "kvl")
            o = open_group("krot", 4)
            for k in range(KT):
                mm = mmul(o[64:96, 0:256], w[:, k, P:P + 32], hT[:, k, 0:256], start=(k == 0), stop=(k == KT - 1))
            close_group(mm, "krot")
            slab_end[n] = "krot"
            pe.wait_ge(S("sq_ql"), 2)
            rms_sums("sum_ql", 5, 256, tiles=2, src=lambda k: sqt[:, k, 0:256])
            pe.wait_ge(S("sq_kvl"), 1)
            rms_sums("sum_kvl", 6, 256, tiles=1, src=lambda k: sqt[:, k, 256:512])
            for s in range(8):
                t_tiles(f"gt{s}", ("in", 8 + s), 2, [1, 2], 256)
            pe.wait_ge(S("qln"), 2)
            w, n = take_slab(("uq", 0))
            w = w[:, 0:1536].rearrange("p (k c) -> p k c", k=2)
            for g in range(4):
                o = open_group(("uq", g), 1 + g % 2)
                for h in range(2):
                    for k in range(2):
                        mm = mmul(o[0:96, 256 * h:256 * h + 256], w[:, k, 96 * (2 * g + h):96 * (2 * g + h) + 96],
                                  lat[:, k, :], start=(k == 0), stop=(k == 1))
                close_group(mm, ("uq", g))
            slab_end[n] = ("uq", 3)
            pe.wait_ge(S("kvn"), 1)
            w, n = take_slab(("ukv", 0))
            for g in range(4):
                o = open_group(("uk", g), 1 + g % 2)
                for h in range(2):
                    mm = mmul(o[0:64, 256 * h:256 * h + 256], w[:, 64 * (2 * g + h):64 * (2 * g + h) + 64],
                              lat[:, 2, :], start=True, stop=True)
                close_group(mm, ("uk", g))
            for t in range(2):
                o = open_group(("uv", t), 1 + t % 2)
                close_group(mmul(o[:, :], lat[:, 2, t * P:(t + 1) * P], w[:, 512:1024], start=True, stop=True), ("uv", t))
            slab_end[n] = ("uv", 1)
            pe.wait_ge(S("qk_ready"), 8)
            attention("na")
            for g in range(4):
                done(pe, ("uq", g))
                o = open_group(("qsw", g), 1 + g % 2)
                close_group(mmul(o[0:96, :], cs[0:96, C_AT["perm96"][0]:C_AT["perm96"][1]],
                                 qm[0:96, 2 * g:2 * g + 2, :].rearrange("p a b -> p (a b)"), start=True, stop=True), ("qsw", g))
            pe.wait_ge(S("kr_zero"), 1)
            done(pe, "krot")
            o = open_group("ksw", 3)
            close_group(mmul(o[0:96, 0:256], cs[0:96, C_AT["perm96"][0]:C_AT["perm96"][1]], lat[0:96, 3, :],
                             start=True, stop=True), "ksw")
            for g in range(8):
                pe.wait_ge(S("sq_m"), g + 1)
                o = open_group(("msum", g), 1 + g % 2)
                close_group(mmul(o[0:96, :], ones[0:96, 0:96], sqt[0:96, g % 2, :], start=True, stop=True), ("msum", g))
            pe.wait_ge(S("m_ready"), 8)
            attention("mla")
            ada_fold(*ada_prev.pop())
            done(pe, ("na", "o", 3))
            done(pe, ("mla", "o", 3))
            for half in range(2):
                wa, na = take_slab(("pna", half))
                wb, nb = take_slab(("pmla", half))
                for t in range(4):
                    d = 4 * half + t
                    for tag, w, y0, b in (("pn", wa, 0, 0), ("pm", wb, 4, 1)):
                        o = open_group((tag, d), b + 2 * (d % 2))
                        for k in range(4):
                            mm = mmul(o[:, 0:256], w[:, 512 * k + P * t:512 * k + P * t + P], yT[:, y0 + k, :],
                                      start=(k == 0), stop=(k == 3))
                        close_group(mm, (tag, d))
                slab_end[na] = slab_end[nb] = ("pm", d)
            pe.wait_ge(S("merged"), 8)
            for s in range(4):
                w, n = take_slab(("out", s))
                w = w.rearrange("p (k c) -> p k c", k=8)
                for t in range(2):
                    o = open_group(("wo", 2 * s + t), 4 + t)
                    for k in range(KT):
                        mm = mmul(o[:, 0:256], w[:, k, t * P:(t + 1) * P], merged[:, k, :], start=(k == 0), stop=(k == KT - 1))
                    close_group(mm, ("wo", 2 * s + t))
                slab_end[n] = ("wo", 2 * s + 1)
            pe.wait_ge(S("sq2"), 1)
            rms_sums("sum2", 0, 256)
            pe.wait_ge(S("h2"), 8)
            for t in range(TT):
                o = open_group(("rt", t), 6)
                for k in range(KT):
                    mm = mmul(o[:, 0:64], hT[:, k, t * P:(t + 1) * P], wr[:, k, :], start=(k == 0), stop=(k == KT - 1))
                close_group(mm, ("rt", t))
            for g in range(4):
                o = open_group(("tk", g), 1 + g % 2)
                for k in range(4):
                    mm = nc.tensor.transpose(o[:, P * k:P * k + P],
                                             hT[:, 4 * (g % 2) + k, (g // 2) * P:(g // 2) * P + P], cc("ident"))
                close_group(mm, ("tk", g))
            t_tiles("shg", ("shg", 0), 2, [3, 4], 256)
            t_tiles("shu", ("shu", 0), 2, [3, 4], 256)
            pe.wait_ge(S("mask"), 1)
            o = open_group("pos", 7)
            mmul(o[:, 0:64], cc("tri"), mask[:, 0, :], start=True, stop=True)
            mmul(o[:, 64:128], ones[:], mask[:, 0, :], start=True, stop=False)
            mmul(o[:, 64:128], cc("tri"), mask[:, 1, :], start=False, stop=True)
            mmul(o[:, 128:192], ones[:], mask[:, 0, :], start=True, stop=False)
            mm = mmul(o[:, 128:192], ones[:], mask[:, 1, :], start=False, stop=True)
            close_group(mm, "pos")

            moe_slab0 = len(slabs)
            for e in range(UN):
                for j in range(PER_E):
                    slabs.append(("exp", e, j))
                    slab_end.append(None)
                    loads.append(None)
            for b in (B_G, B_GU, B_D, B_X):
                if uses[b]:
                    pe.wait_ge(psum_done[b], uses[b])
            pe.wait_ge(S("zeros"), 1)
            zero = yo[:, 0, 0:256].bitcast(BF16)
            for b in range(4):
                mmul(open_group(("sums", b), b)[:, :], zero[:, 0:P], zero, start=True, stop=False)

            def gather(n):
                u = n[1]
                pe.wait_ge(S("sel_made"), n[0] + 1)
                for d in range(8):
                    for t in range(TT):
                        for q in range(3):
                            mm = mmul(bank[B_G][:, SLOTS * d:SLOTS * d + SLOTS], hbf[:, q, t, P * d:P * d + P],
                                      selb[:, u, t, :], start=(t == 0 and q == 0), stop=(t == 1 and q == 2))
                mm.then_inc(S("g_full"), 1)

            def scatter(u):
                for t in range(TT):
                    for c in range(2):
                        mmul(bank[2 * t + c][:, :], selT[64 * c:64 * c + 64, u, t, :], yo[64 * c:64 * c + 64, u, :],
                             start=False, stop=False)

            def item(i, u, first=False):
                n = UN * i + u

                def arrived(j):
                    pe.wait_ge(S(f"item_in{u}{j}"), 16 * i + 16)
                    return ring[:, (moe_slab0 + PER_E * u + j) % RING, :]

                pe.wait_ge(S("xg_copied"), n + 1)
                w = [arrived(j).rearrange("p (k c) -> p k c", k=8) for j in range(2)]
                for k in range(KT):
                    for f in range(2):
                        mm = mmul(bank[B_GU][64 * f:64 * f + 64, 0:256], xg[:, u, SLOTS * k:SLOTS * k + SLOTS], w[f][:, k, :],
                                  start=(k == 0), stop=(k == KT - 1))
                mm.then_inc(S("gu_full"), 1)
                gather((n + 1, 1 - u))
                pe.wait_ge(S("hid_made"), n + 1)
                if not first:
                    pe.wait_ge(S("selT_copied"), n)
                nc.tensor.transpose(bank[B_X][:, 0:P], hid[:, u, :], cc("ident"))
                for t in range(TT):
                    mm = nc.tensor.transpose(bank[B_X][:, P + P * t:P + P * t + P], selg[:, u, t, :], cc("ident"))
                mm.then_inc(S("x_full"), 1)
                if not first:
                    pe.wait_ge(S("y_copied"), n)
                    scatter(1 - u)
                pe.wait_ge(S("aT_copied"), n + 1)
                wd = arrived(2)
                for f in range(2):
                    for c in range(2):
                        mm = mmul(bank[B_D][64 * c:64 * c + 64, :], aT[:, u, 64 * f:64 * f + 64],
                                  wd[:, 1024 * f + 512 * c:1024 * f + 512 * c + 512], start=(f == 0), stop=(f == 1))
                mm.then_inc(S("d_full"), 1)

            pe.wait_ge(S("sh_act"), 1)
            gather((0, 0))
            for u in range(UN):
                item(0, u, first=(u == 0))
            with pe.Fori(1, TURNS) as i:
                for u in range(UN):
                    item(i, u)
            pe.wait_ge(S("listed"), 1)
            more = pe.value_load(nturn[0:1, 0:1], min_val=0, max_val=MORE // UN)
            with pe.If(more > 0):
                with pe.Fori(0, more) as i:
                    for u in range(UN):
                        item(i + TURNS, u)
            pe.wait_ge(S("y_copied"), UN * more + E)
            pe.wait_ge(S("selT_copied"), UN * more + E)
            pe.wait_ge(S("xg_copied"), UN * more + (E + 1))
            scatter(UN - 1)
            w, n = take_slab(("shd", 0))
            for b in range(4):
                for f in range(2):
                    mm = mmul(bank[b][:, :], shu[:, f, P * (b // 2):P * (b // 2) + P],
                              w[:, 1024 * f + 512 * (b % 2):1024 * f + 512 * (b % 2) + 512], start=False, stop=(f == 1))
                close_group(mm, ("sums", b))
            slab_end[n] = ("sums", 3)

            for g in range(4):
                done(pe, ("sums", g))
                o = open_group(("ac", g), 4 + g % 4)
                for k in range(4):
                    at = 512 * (g % 2) + P * k
                    mm = nc.tensor.transpose(o[:, P * k:P * k + P], acc[:, g // 2, at:at + P], cc("ident"))
                close_group(mm, ("ac", g))

            pe.wait_ge(S("sq3"), 1)
            rms_sums("sum3", 0, 512)
            pe.wait_ge(S("h3"), 16)
            pe.wait_ge(S("const2_in"), 32)
            for s in range(2):
                tok_tiles(f"vab{s}", ("ab", s), 4, [1, 2])
            for s in range(8):
                t_tiles(f"z{s}", ("ab", 2 + s), 2, [3, 4], 512)
            for g in range(4):
                for st in range(2):
                    n = 2 * g + st
                    done(pe, (f"z{g // 2}", g % 2))
                    o = open_group(("fa", n), 5 + n % 2)
                    for t in range(TT):
                        at = 256 * st + P * t
                        mm = mmul(o[:, 256 * t:256 * t + 256], zT[:, 12 + g, at:at + P], cc("dft_c"), start=True, stop=True)
                    close_group(mm, ("fa", n))
                    done(pe, ("fa", n))
                    o = open_group(("fb", n), 0 if n % 2 else 7)
                    for t in range(TT):
                        for c in range(2):
                            mm = mmul(o[:, 0:256], fa[:, n % 2, 256 * t + P * c:256 * t + P * c + P],
                                      cc("dft_l", 512 * t + 256 * c, 512 * t + 256 * c + 256),
                                      start=(t == 0 and c == 0), stop=(t == 1 and c == 1))
                    close_group(mm, ("fb", n))
            pe.wait_ge(S("v_norm"), 4)
            for h in range(4):
                o = open_group(("sp", h), 1 + h % 2)
                for t in range(4):
                    mm = mmul(o[:, P * t:P * t + P], vtok[:, t, P * h:P * h + P], spat[:, h, :], start=True, stop=True)
                close_group(mm, ("sp", h))
            pe.wait_ge(S("y_a"), 4)
            done(pe, ("fb", 7))
            done(pe, ("fb", 6))
            for s in range(4):
                w, n = take_slab(("oab", s))
                w = w.rearrange("p (k c) -> p k c", k=8)
                for t in range(2):
                    o = open_group(("oab", 2 * s + t), 3 + t)
                    for k in range(KT):
                        mm = mmul(o[:, :], w[:, k, t * P:(t + 1) * P], zT[:, k, :], start=(k == 0), stop=(k == KT - 1))
                    close_group(mm, ("oab", 2 * s + t))
                slab_end[n] = ("oab", 2 * s + 1)
            pe.wait_ge(S("sq4"), 1)
            rms_sums("sum4", 0, 512)
            pe.wait_ge(S("h4"), 16)
            t_tiles("k2", ("cin", 0), 2, [1, 2], 512)
            tok_tiles("v2", ("cin", 1), 4, [1, 2])
            for s in range(4):
                t_tiles(f"q2{s}", ("cin", 2 + s), 2, [3, 4], 256)
            for s in range(4):
                t_tiles(f"g2{s}", ("cin", 6 + s), 2, [3, 4], 256)
            for j in range(10):
                done(pe, ("k2", j) if j < 2 else (f"q2{(j - 2) // 2}", j % 2))
                src = k2[:, j, 0:256] if j < 2 else q2[:, j - 2, :]
                o = open_group(("sw", j), 1 + j % 2)
                close_group(mmul(o[:, 0:256], cc("perm128"), src, start=True, stop=True), ("sw", j))
            pe.wait_ge(S("rope2"), 10)
            done(pe, ("v2", 2))
            done(pe, ("v2", 3))
            attention("c")
            done(pe, ("c", "o", 7))
            done(pe, ("c", "o", 6))
            for s in range(4):
                w, n = take_slab(("oc", s))
                w = w.rearrange("p (k c) -> p k c", k=8)
                for t in range(2):
                    o = open_group(("oc", 2 * s + t), t)
                    for k in range(KT):
                        mm = mmul(o[:, 0:256], w[:, k, t * P:(t + 1) * P], o2[:, k, :], start=(k == 0), stop=(k == KT - 1))
                    close_group(mm, ("oc", 2 * s + t))
                slab_end[n] = ("oc", 2 * s + 1)
            pe.wait_ge(S("sq5"), 1)
            rms_sums("sum5", 2, 256)

        exp0 = next(n for n, s in enumerate(slabs) if s[0] == "exp")

        @block.sync
        def _(sp):
            def load(n):
                slot = n % RING
                src = slabs[n]
                w = slabs_d[slabs_at[src[0]] + src[1]]
                sp.dma_start(ring[:, slot, :], w).then_inc(slab_in[slot], 16)

            def slab_read(n):
                full(sp, slab_end[n])

            for n in range(exp0):
                if n >= RING:
                    slab_read(n - RING)
                load(n)

            def item_slabs(i, u, e):
                for j in range(PER_E):
                    slot = (exp0 + PER_E * u + j) % RING
                    if isinstance(i, int) and i == 0:
                        slab_read(exp0 + PER_E * u + j - RING)
                    else:
                        sp.wait_ge(S(ITEM_USE[j]), UN * i + (u + 1 - UN))
                    sp.dma_start(ring[:, slot, :], exp_d[e, j]).then_inc(S(f"item_in{u}{j}"), 16)

            for u in range(UN):
                item_slabs(0, u, u)
            after = exp0 + UN * PER_E
            for n in range(after, exp0 + RING):
                slab_read(n - RING)
                load(n)
            with sp.Fori(1, TURNS) as i:
                for u in range(UN):
                    item_slabs(i, u, UN * i + u)
            sp.wait_ge(S("listed"), 1)
            more = sp.value_load(nturn[0:1, 0:1], min_val=0, max_val=MORE // UN)
            with sp.If(more > 0):
                with sp.Fori(0, more) as i:
                    for u in range(UN):
                        e = sp.value_load(whose[0:1, bass.ds(UN * i + u, 1)], min_val=0, max_val=E - 1)
                        item_slabs(i + TURNS, u, e)
            for n in range(exp0 + RING, len(slabs)):
                if n < after + RING:
                    u, j = (n - exp0 - RING) // PER_E, (n - exp0) % PER_E
                    sp.wait_ge(S(ITEM_USE[j]), UN * more + (E - UN + 1 + u))
                else:
                    slab_read(n - RING)
                load(n)

        @block.gpsimd
        def _(pool):
            g = nc.gpsimd
            g.memset(silc[:], 0.0).then_inc(S("silc_zero"), 1)
            g.memset(silc2[:], 0.0).then_inc(S("silc_zero"), 1)
            g.memset(ones[:], 1.0).then_inc(S("ones_set"), 1)
            g.memset(lat[0:64, 3, :], 0.0).then_inc(S("kr_zero"), 1)
            pool.wait_ge(S("const_in"), 48)
            pool.wait_ge(S("bias_in"), 32)
            for h in range(8):
                if h >= 2:
                    done(pool, ("na", "s", h - 2))
                for t in range(TT):
                    r = braw[:, h, :]
                    rev = bass.AP(r.tensor, r.offset + 62 * (1 - t) + 63, [list(r.ap[0]), [31, 4], [-1, 64]])
                    m = cc("namask")
                    mb = bass.AP(m.tensor, m.offset, [list(m.ap[0]), [0, 4], [1, 64]])
                    g.tensor_tensor(bmask[:, h % 2, 256 * t:256 * t + 256].rearrange("p (a b) -> p a b", a=4),
                                    rev, mb, ALU.add).then_inc(S("bias_made"), 1)
            pool.wait_ge(S("rope_tab"), 1)
            for gg in range(4):
                full(pool, ("qsw", gg))
                for h in range(2):
                    v = qm[0:96, 2 * gg + h, :]
                    last = g.tensor_tensor(v, v, rope_c[0:96, :], ALU.mult)
                last.then_inc(S("q_cos"), 1)

            pool.wait_ge(S("x1"), 1)
            pool.dma_start(cs2, consts2_d).then_inc(S("const2_in"), 16)
            pool.dma_start(spat, spat_d).then_inc(S("const2_in"), 16)

        @block.scalar
        def _(act):
            a = nc.scalar
            steps = [0]

            def link(ins):
                steps[0] += 1
                ins.then_inc(S("act_step"), 1)
                act.wait_ge(S("act_step"), steps[0])

            act.dma_start(ve[:], vecs_d).then_inc(S("vec_in"), 16)
            act.dma_start(xT[:], xT_d).then_inc(S("x_in"), 16)
            act.dma_start(cs[:], consts_d).then_inc(S("const_in"), 16)
            act.dma_start(stat[0:96, 0:256].bitcast(I32), pos_d).then_inc(S("const_in"), 16)
            act.dma_start(wr[:], router_d).then_inc(S("const_in"), 16)
            for r in range(2):
                src = bass.AP(rpb_d.tensor, (5 - r) * 31 - 48, [[1, 64], [15 * 31, 8], [1, RUN]])
                act.dma_start(braw[64 * r:64 * r + 64, :, :], src).then_inc(S("bias_in"), 16)
            act.wait_ge(S("vec_in"), 16)
            act.wait_ge(S("silc_zero"), 2)
            a.activation(silc[:, :, 0], vv("c"), ACT.Silu)
            a.activation(silc2[:, :, 0:2], vv("c2").rearrange("p (a b) -> p a b", a=8), ACT.Silu).then_inc(S("silu_c"), 1)
            act.wait_ge(S("x_in"), 16)
            for k in range(KT):
                last = a.activation(hT[:, k, 0:256], xT[:, k, 0:256], ACT.Square)
            last.then_inc(S("sq1"), 1)

            def ada_quarters(which, j):
                name = (which, j, "quarters")
                full(act, name)
                emptied(a.copy(quarters[:, j % 2, :], bk(name)[:, 0:256]), name)

            for j in range(8):
                ada_quarters("ada1", j)

            def root(n, src, tag, cols, parts=P):
                act.wait_ge(S(tag + "_ms"), n)
                a.activation(src[0:parts, 0:cols], src[0:parts, 0:cols], ACT.Sqrt).then_inc(S(tag + "_rt"), 1)

            def shifts(tag, cols, shift):
                for k in range(KT):
                    for s in range(cols // 256):
                        n = k * (cols // 256) + s
                        act.wait_ge(S(tag + "_scaled"), n + 1)
                        v = hT[:, k, 256 * s:256 * s + 256]
                        a.activation(v, v, ACT.Identity, bias=shift(k, s)).then_inc(S(tag), 1)

            act.wait_ge(S("angle"), 1)
            a.activation(rope_s[0:96, :], sqt[0:96, 0, 0:256], ACT.Sin)
            a.activation(rope_c[0:96, :], sqt[0:96, 1, 0:256], ACT.Sin).then_inc(S("rope_tab"), 1)
            root(1, rstd, "n1", 256)
            shifts("h1", 256, lambda k, s: mod1[:, k:k + 1])
            for s in range(4):
                for t in range(2):
                    j = 2 * s + t
                    full(act, (f"qk{s}", t))
                    if j >= 2:
                        full(act, ("qkn", j - 2))
                    a.activation(sqt[:, j % 2, 0:256], bk((f"qk{s}", t))[:, 0:256], ACT.Square).then_inc(S("sq_qk"), 1)
                    emptied(a.copy(qk[:, j, :], bk((f"qk{s}", t))[:, 0:256]), (f"qk{s}", t))
            for s in range(2):
                for t in range(2):
                    full(act, (f"vna{s}", t))
                    emptied(a.copy(vna[:, t, 256 * s:256 * s + 256], bk((f"vna{s}", t))[:, 0:256]), (f"vna{s}", t))
            for t in range(2):
                full(act, ("ql", t))
                full(act, ("qkn", 6 + t))
                a.activation(sqt[:, t, 0:256], bk(("ql", t))[:, 0:256], ACT.Square).then_inc(S("sq_ql"), 1)
                emptied(a.copy(lat[:, t, :], bk(("ql", t))[:, 0:256]), ("ql", t))
            full(act, "kvl")
            a.activation(sqt[:, 0, 256:512], bk("kvl")[:, 0:256], ACT.Square).then_inc(S("sq_kvl"), 1)
            emptied(a.copy(lat[:, 2, :], bk("kvl")[:, 0:256]), "kvl")
            full(act, "krot")
            emptied(a.copy(lat[64:96, 3, :], bk("krot")[64:96, 0:256]), "krot")
            root(1, pr[:, :, :].rearrange("p a b -> p (a b)"), "qk", 2048)
            root(1, stat, "lt", 512)
            for s in range(8):
                for t in range(2):
                    full(act, (f"gt{s}", t))
                    emptied(a.activation(sgate[:, 2 * s + t, :], bk((f"gt{s}", t))[:, 0:256], ACT.Sigmoid), (f"gt{s}", t))
            for gg in range(4):
                full(act, ("uq", gg))
                emptied(a.copy(qm[0:96, 2 * gg:2 * gg + 2, :].rearrange("p a b -> p (a b)"), bk(("uq", gg))[0:96, :]), ("uq", gg))
            for gg in range(4):
                full(act, ("uk", gg))
                emptied(a.copy(km[0:64, 2 * gg:2 * gg + 2, :].rearrange("p a b -> p (a b)"), bk(("uk", gg))[0:64, :]), ("uk", gg))
            for t in range(2):
                full(act, ("uv", t))
                emptied(a.copy(vm[:, t, :], bk(("uv", t))[:, :]), ("uv", t))

            def attention(kind):
                n_heads, _, nk = KINDS[kind]
                for i in range(n_heads // 2):
                    for h in (2 * i, 2 * i + 1):
                        act.wait_ge(S(kind + "_negmax"), h + 1)
                        if kind == "c":
                            a.activation(att[:, h % 4, 6:8], att[:, h % 4, 0:2], ACT.Exp)
                        if kind == "mla" and h >= 4:
                            full(act, (kind, "t", h - 4, 0))
                        for t in range(TT):
                            o = probs(kind, h)[:, nk * t:nk * t + nk]
                            src = bk((kind, "s", h))[:, 256 * t:256 * t + 256] if kind == "mla" else o
                            ins = a.activation(o, src, ACT.Exp, bias=att[:, h % 4, 2 + t:3 + t],
                                               scale=96 ** -0.5 if kind == "mla" else 1.0,
                                               accum_out=att[:, h % 4, 4 + t:5 + t])
                        if kind == "mla":
                            emptied(ins, (kind, "s", h))
                        else:
                            ins.then_inc(S(kind + "_exp"), 1)
                    for f in FILL.get((kind, i), []):
                        ada_quarters(*f)
                    for h in (2 * i, 2 * i + 1):
                        for j in range(nk // 256):
                            full(act, (kind, "t", h, j))
                            emptied(a.copy(pT[:, h % 2, 512 * j:512 * j + 512], bk((kind, "t", h, j))[:, :]), (kind, "t", h, j))

            attention("na")
            for gg in range(8):
                act.wait_ge(S("m_in"), gg + 1)
                if gg >= 2:
                    full(act, ("msum", gg - 2))
                v = (qm if gg < 4 else km)[0:96, 2 * (gg % 4):2 * (gg % 4) + 2, :].rearrange("p a b -> p (a b)")
                a.activation(sqt[0:96, gg % 2, :], v, ACT.Square).then_inc(S("sq_m"), 1)
            root(1, var, "mq", 2048, 96)
            root(1, pT[:, :, :].rearrange("p a b -> p (a b)"), "mk", 2048, 96)
            attention("mla")
            act.wait_ge(S("x1"), 1)
            for k in range(KT):
                last = a.activation(hT[:, k, 0:256], xT[:, k, 0:256], ACT.Square)
            last.then_inc(S("sq2"), 1)
            root(1, rstd, "n2", 256)
            shifts("h2", 256, lambda k, s: mod1[:, 24 + k:25 + k])
            for t in range(TT):
                full(act, ("rt", t))
                emptied(a.activation(lg[:, t, :], bk(("rt", t))[:, 0:64], ACT.Sigmoid), ("rt", t))
            for gg in range(4):
                w0, t = 512 * (gg % 2), gg // 2
                full(act, ("tk", gg))
                a.copy(hbf[:, 0, t, w0:w0 + 512], bk(("tk", gg))[:, :]).then_inc(S("part_a"), 1)
                act.wait_ge(S("rest_a"), gg + 1)
                a.copy(hbf[:, 1, t, w0:w0 + 512], htok[:, gg % 2, :]).then_inc(S("part_b"), 1)
            for t in range(2):
                full(act, ("shg", t))
                emptied(a.activation(shg[:, t, :], bk(("shg", t))[:, 0:256], ACT.Silu), ("shg", t))

            def gathered(n, u):
                act.wait_ge(S("g_full"), n + 1)
                a.copy(xg[:, u, :], bank[B_G][:, :]).then_inc(S("xg_copied"), 1)

            def item(i, u):
                n = UN * i + u
                act.wait_ge(S("gu_full"), n + 1)
                a.activation(sgt[:, u, :], bank[B_GU][:, 0:P], ACT.Silu).then_inc(S("silu_made"), 1)
                gathered(n + 1, 1 - u)
                act.wait_ge(S("d_full"), n + 1)
                a.copy(yo[:, u, :], bank[B_D][:, :]).then_inc(S("y_copied"), 1)

            gathered(0, 0)
            with act.Fori(0, TURNS) as i:
                for u in range(UN):
                    item(i, u)
            act.wait_ge(S("listed"), 1)
            more = act.value_load(nturn[0:1, 0:1], min_val=0, max_val=MORE // UN)
            with act.If(more > 0):
                with act.Fori(0, more) as i:
                    for u in range(UN):
                        item(i + TURNS, u)
            for b in (1, 3):
                full(act, ("sums", b))
                emptied(a.copy(acc[:, b // 2, 512 * (b % 2):512 * (b % 2) + 512], bank[b][:, :]), ("sums", b))

            def squares(ready, n, tag, cols):
                act.wait_ge(S(ready), n)
                for k in range(KT):
                    last = a.activation(hT[:, k, 0:cols], xT[:, k, 0:cols], ACT.Square)
                last.then_inc(S(tag), 1)

            squares("x2", 1, "sq3", 512)
            root(1, rstd, "n3", 512)
            shifts("h3", 512, lambda k, s: mod2[:, k, s:s + 1])
            for s in range(2):
                for t in range(4):
                    full(act, (f"vab{s}", t))
                    emptied(a.copy(vtok[:, t, 256 * s:256 * s + 256], bk((f"vab{s}", t))[:, 0:256]), (f"vab{s}", t))
            root(1, bn[:, :, 13], "v", 4)
            for s in range(8):
                for t in range(2):
                    at = (12, 4, 0, 8)[s // 2] + 2 * (s % 2) + t
                    full(act, (f"z{s}", t))
                    f = (ACT.Copy, ACT.Silu, ACT.Copy, ACT.Silu)[s // 2]
                    emptied(a.activation(zT[:, at, :], bk((f"z{s}", t))[:, :], f), (f"z{s}", t))
            for n in range(8):
                full(act, ("fa", n))
                if n >= 2:
                    full(act, ("fb", n - 2))
                emptied(a.copy(fa[:, n % 2, :], bk(("fa", n))[:, :]), ("fa", n))
            squares("x3", 1, "sq4", 512)
            root(1, rstd, "n4", 512)
            shifts("h4", 512, lambda k, s: mod2[:, 24 + k, s:s + 1])
            for t in range(2):
                full(act, ("k2", t))
                emptied(a.copy(k2[:, t, :], bk(("k2", t))[:, :]), ("k2", t))
            for t in range(4):
                full(act, ("v2", t))
                emptied(a.copy(v2[:, t, :], bk(("v2", t))[:, 0:256]), ("v2", t))
            for s in range(4):
                for t in range(2):
                    full(act, (f"q2{s}", t))
                    emptied(a.copy(q2[:, 2 * s + t, :], bk((f"q2{s}", t))[:, 0:256]), (f"q2{s}", t))
            for s in range(4):
                for t in range(2):
                    full(act, (f"g2{s}", t))
                    emptied(a.activation(g2s[:, 2 * s + t, :], bk((f"g2{s}", t))[:, 0:256], ACT.Silu), (f"g2{s}", t))

            attention("c")
            act.wait_ge(S("x4"), 1)
            for k in range(KT):
                last = a.activation(hT[:, k, 0:256], xT[:, k, 0:256], ACT.Square)
            last.then_inc(S("sq5"), 1)
            root(1, rstd, "n5", 256)
            for k in range(KT):
                act.wait_ge(S("y_out"), k + 1)
                act.dma_start(out_d[:, k, :], outT[:, k, :]).then_inc(S("stored_out"), 16)
            act.wait_ge(S("stored_out"), 16 * KT)

        @block.vector
        def _(dve):
            v = nc.vector
            steps = [0]
            signals = [0]

            def link(ins):
                steps[0] += 1
                ins.then_inc(S("dve_step"), 1)
                dve.wait_ge(S("dve_step"), steps[0])

            def signal(name):
                signals[0] += 1
                v.tensor_copy(mark[0:1, signals[0]:signals[0] + 1], mark[0:1, 0:1]).then_inc(S(name), 1)

            def bc(ap, *dims):
                return bass.AP(ap.tensor, ap.offset, [list(ap.ap[0])] + [list(d) for d in dims])

            def ada(which, j):
                full(dve, (which, j))
                o = bk((which, j))
                if which == "ada1":
                    emptied(v.tensor_tensor(mod1[:, 2 * j:2 * j + 2], o[:, 0:2], vv("b_ada", 2 * j, 2 * j + 2), ALU.add), (which, j))
                else:
                    b = vv("b2", 2 * j, 2 * j + 2)
                    emptied(v.tensor_tensor(mod2[:, 2 * j:2 * j + 2, :], o[:, 0:4].rearrange("p (a b) -> p a b", a=2),
                                            bc(b, [1, 2], [0, 2]), ALU.add), (which, j))

            def rms(tag, name, width, cols, dst, parts=P, last=True):
                full(dve, name)
                emptied(v.tensor_scalar(dst[0:parts, 0:cols], bk(name)[0:parts, 0:cols], 1.0 / width, EPS, ALU.mult, ALU.add), name)
                done(dve, name)
                signal(tag + "_ms")
                dve.wait_ge(S(tag + "_rt"), 1)
                link(v.reciprocal(dst[0:parts, 0:cols], dst[0:parts, 0:cols]))

            def scale_tiles(tag, cols, gain):
                for k in range(KT):
                    for s in range(cols // 256):
                        v.scalar_tensor_tensor(out=hT[:, k, 256 * s:256 * s + 256], in0=xT[:, k, 256 * s:256 * s + 256],
                                               scalar=gain(k, s), in1=rstd[:, 256 * s:256 * s + 256],
                                               op0=ALU.mult, op1=ALU.mult).then_inc(S(tag + "_scaled"), 1)

            link(v.memset(mark[:], 0.0))
            dve.wait_ge(S("const_in"), 48)
            pf, an, tn = pr[0:96, 0, 0:256], pr[0:96, 0, 256:512], pr[0:96, 0, 512:768]
            sn, co = sqt[0:96, 0, 0:256], sqt[0:96, 1, 0:256]
            link(v.tensor_copy(pf, stat[0:96, 0:256].bitcast(I32)))
            link(v.tensor_scalar(an, pf, cc("invf")[0:96, :], None, ALU.mult))
            MAGIC = 12582912.0
            link(v.tensor_scalar(tn, an, 1.0 / TWO_PI, MAGIC, ALU.mult, ALU.add))
            link(v.tensor_scalar(tn, tn, -MAGIC, None, ALU.add))
            C1 = 6.28125
            C2 = float(np.float32(np.round((TWO_PI - C1) * 2 ** 20) / 2 ** 20))
            C3 = float(TWO_PI - C1 - C2)
            for c in (C1, C2, C3):
                link(v.scalar_tensor_tensor(out=an, in0=tn, scalar=-c, in1=an, op0=ALU.mult, op1=ALU.add))
            LIM = 3.1415925
            link(v.tensor_scalar(sn, an, LIM, -LIM, ALU.min, ALU.max))
            link(v.tensor_scalar(an, an, float(np.pi / 2), None, ALU.add))
            link(v.tensor_scalar(tn, an, float(np.pi), -TWO_PI, ALU.is_gt, ALU.mult))
            link(v.tensor_tensor(an, an, tn, ALU.add))
            v.tensor_scalar(co, an, LIM, -LIM, ALU.min, ALU.max).then_inc(S("angle"), 1)

            for j in range(8):
                ada("ada1", j)
            done(dve, ("ada1", 6))
            done(dve, ("ada1", 7))
            link(v.scalar_tensor_tensor(out=gs[:, :, 0], in0=mod1[:, 8:16], scalar=1.0, in1=vv("g1"), op0=ALU.add, op1=ALU.mult))
            rms("n1", "sum1", D, 256, rstd)
            scale_tiles("h1", 256, lambda k, s: gs[:, k, 0:1])
            for j in range(8):
                full(dve, ("qkn", j))
                emptied(v.tensor_scalar(pr[:, j // 4, 256 * (j % 4):256 * (j % 4) + 256], bk(("qkn", j))[:, 0:256],
                                        1.0 / 64, EPS, ALU.mult, ALU.add), ("qkn", j))
            full(dve, "sum_ql")
            emptied(v.tensor_scalar(stat[:, 0:256], bk("sum_ql")[:, 0:256], 1.0 / 256, EPS, ALU.mult, ALU.add), "sum_ql")
            full(dve, "sum_kvl")
            emptied(v.tensor_scalar(stat[:, 256:512], bk("sum_kvl")[:, 0:256], 1.0 / 128, EPS, ALU.mult, ALU.add), "sum_kvl")
            done(dve, "sum_kvl")
            done(dve, "sum_ql")
            signal("lt_ms")
            signal("qk_ms")
            dve.wait_ge(S("qk_rt"), 1)
            prf = pr[:, :, :].rearrange("p a b -> p (a b)")
            link(v.reciprocal(prf, prf))
            for j in range(8):
                done(dve, (f"qk{j // 2}", j % 2))
                g = vv("gq") if j < 4 else vv("gk")
                v.scalar_tensor_tensor(out=qk[:, j, :], in0=qk[:, j, :], scalar=g, in1=prf[:, 256 * j:256 * j + 256],
                                       op0=ALU.mult, op1=ALU.mult).then_inc(S("qk_ready"), 1)
            dve.wait_ge(S("lt_rt"), 1)
            link(v.reciprocal(stat[:, :], stat[:, :]))
            for t in range(2):
                done(dve, ("ql", t))
                v.scalar_tensor_tensor(out=lat[:, t, :], in0=lat[:, t, :], scalar=vv("gql", t, t + 1), in1=stat[:, 0:256],
                                       op0=ALU.mult, op1=ALU.mult).then_inc(S("qln"), 1)
            done(dve, "kvl")
            v.scalar_tensor_tensor(out=lat[:, 2, :], in0=lat[:, 2, :], scalar=vv("gkv"), in1=stat[:, 256:512],
                                   op0=ALU.mult, op1=ALU.mult).then_inc(S("kvn"), 1)

            def normalise(kind, h, nk):
                mx = att[:, h % 4, :]
                link(v.reciprocal(mx[:, 4:6], mx[:, 4:6]))
                for t in range(TT):
                    o = probs(kind, h)[:, nk * t:nk * t + nk]
                    last = v.tensor_scalar(o, o, mx[:, 4 + t:5 + t], None, ALU.mult)
                last.then_inc(S(kind + "_probs"), 1)

            def pair_out(kind, i, dst):
                full(dve, (kind, "o", i))
                emptied(v.tensor_copy(dst, bk((kind, "o", i))[:, 0:256]), (kind, "o", i))

            ada_prev = [("ada1", 7)]

            def ada_folds(key):
                for f in FILL[key]:
                    if ada_prev[0] != ("ada1", 7):
                        ada(*ada_prev[0])
                    ada_prev[0] = f

            def na_scores(h):
                if h >= 4:
                    full(dve, ("na", "t", h - 4, 0))
                full(dve, ("na", "s", h))
                dve.wait_ge(S("bias_made"), 2 * h + 2)
                emptied(v.scalar_tensor_tensor(out=probs("na", h), in0=bk(("na", "s", h))[:, :], scalar=0.125,
                                               in1=bmask[:, h % 2, :], op0=ALU.mult, op1=ALU.add), ("na", "s", h))
                done(dve, ("na", "s", h))
                link(v.tensor_reduce(att[:, h % 4, 0:2], probs("na", h).rearrange("p (a b) -> p a b", a=2), AXX, ALU.max))
                v.tensor_scalar(att[:, h % 4, 2:4], att[:, h % 4, 0:2], -1.0, None, ALU.mult).then_inc(S("na_negmax"), 1)

            na_scores(0)
            na_scores(1)
            for i in range(4):
                if i < 3:
                    na_scores(2 * i + 2)
                    na_scores(2 * i + 3)
                dve.wait_ge(S("na_exp"), 2 * i + 2)
                normalise("na", 2 * i, 256)
                normalise("na", 2 * i + 1, 256)
                ada_folds(("na", i))
                if i >= 1:
                    pair_out("na", i - 1, yT[:, i - 1, :])
            pair_out("na", 3, yT[:, 3, :])

            for gg in range(4):
                full(dve, ("qsw", gg))
                t2 = pT[0:96, gg % 2, 0:512]
                rs = bc(rope_s[0:96, :], [0, 2], [1, 256])
                if gg == 0:
                    dve.wait_ge(S("rope_tab"), 1)
                emptied(v.tensor_tensor(t2.rearrange("p (a b) -> p a b", a=2),
                                        bk(("qsw", gg))[0:96, :].rearrange("p (a b) -> p a b", a=2), rs, ALU.mult), ("qsw", gg))
                done(dve, ("qsw", gg))
                dve.wait_ge(S("q_cos"), gg + 1)
                q = qm[0:96, 2 * gg:2 * gg + 2, :].rearrange("p a b -> p (a b)")
                v.tensor_tensor(q, q, t2, ALU.add).then_inc(S("m_in"), 1)
            full(dve, "ksw")
            t2 = pT[0:96, 0, 512:768]
            emptied(v.tensor_tensor(t2, bk("ksw")[0:96, 0:256], rope_s[0:96, :], ALU.mult), "ksw")
            link(v.tensor_tensor(lat[0:96, 3, :], lat[0:96, 3, :], rope_c[0:96, :], ALU.mult))
            done(dve, "ksw")
            link(v.tensor_tensor(lat[0:96, 3, :], lat[0:96, 3, :], t2, ALU.add))
            for gg in range(4):
                done(dve, ("uk", gg))
                for h in range(2):
                    last = v.tensor_copy(km[64:96, 2 * gg + h, :], lat[64:96, 3, :])
                last.then_inc(S("m_in"), 1)
            for gg in range(8):
                full(dve, ("msum", gg))
                dst = var[0:96, 512 * gg:512 * gg + 512] if gg < 4 else pT[0:96, (gg - 4) // 2, 512 * (gg % 2):512 * (gg % 2) + 512]
                emptied(v.tensor_scalar(dst, bk(("msum", gg))[0:96, :], 1.0 / 96, EPS, ALU.mult, ALU.add), ("msum", gg))
                if gg % 4 == 3:
                    done(dve, ("msum", gg))
                    done(dve, ("msum", gg - 1))
                    signal(("mq" if gg < 4 else "mk") + "_ms")
            pTf = pT[:, :, :].rearrange("p a b -> p (a b)")
            for i, (tag, buf, dst, g) in enumerate((("mq", var, qm, "gmq"), ("mk", pTf, km, "gmk"))):
                dve.wait_ge(S(tag + "_rt"), 1)
                link(v.reciprocal(buf[0:96, 0:2048], buf[0:96, 0:2048]))
                for gg in range(4):
                    o = dst[0:96, 2 * gg:2 * gg + 2, :].rearrange("p a b -> p (a b)")
                    v.scalar_tensor_tensor(out=o, in0=o, scalar=vv(g)[0:96, :], in1=buf[0:96, 512 * gg:512 * gg + 512],
                                           op0=ALU.mult, op1=ALU.mult).then_inc(S("m_ready"), 1)

            def mla_scores(h):
                full(dve, ("mla", "s", h))
                link(v.tensor_reduce(att[:, h % 4, 0:2], bk(("mla", "s", h))[:, :].rearrange("p (a b) -> p a b", a=2), AXX, ALU.max))
                v.tensor_scalar(att[:, h % 4, 2:4], att[:, h % 4, 0:2], -(96 ** -0.5), None, ALU.mult).then_inc(S("mla_negmax"), 1)

            mla_scores(0)
            mla_scores(1)
            for i in range(4):
                for h in (2 * i, 2 * i + 1):
                    done(dve, ("mla", "s", h))
                    normalise("mla", h, 256)
                if i < 3:
                    mla_scores(2 * i + 2)
                    mla_scores(2 * i + 3)
                ada_folds(("mla", i))
                if i >= 1:
                    pair_out("mla", i - 1, yT[:, 4 + i - 1, :])
            ada(*ada_prev[0])
            pair_out("mla", 3, yT[:, 7, :])
            done(dve, ("ada1", 23))
            for d in range(8):
                full(dve, ("pn", d))
                full(dve, ("pm", d))
                t1, t2 = sqt[:, d % 2, 0:256], sqt[:, d % 2, 256:512]
                emptied(v.tensor_tensor(t1, bk(("pn", d))[:, 0:256], sgate[:, d, :], ALU.mult), ("pn", d))
                emptied(v.tensor_tensor(t2, bk(("pm", d))[:, 0:256], sgate[:, 8 + d, :], ALU.mult), ("pm", d))
                done(dve, ("pn", d))
                done(dve, ("pm", d))
                v.tensor_tensor(merged[:, d, :], t1, t2, ALU.add).then_inc(S("merged"), 1)

            def residual(name, d, lo, hi, gate, src=None):
                return v.scalar_tensor_tensor(out=xT[:, d, lo:hi], in0=bk(name)[:, lo:hi] if src is None else src, scalar=gate,
                                              in1=xT[:, d, lo:hi], op0=ALU.mult, op1=ALU.add)

            for d in range(8):
                full(dve, ("wo", d))
                emptied(residual(("wo", d), d, 0, 256, mod1[:, 16 + d:17 + d]), ("wo", d))
            done(dve, ("wo", 6))
            done(dve, ("wo", 7))
            signal("x1")
            link(v.scalar_tensor_tensor(out=gs[:, :, 0], in0=mod1[:, 32:40], scalar=1.0, in1=vv("g2"), op0=ALU.add, op1=ALU.mult))
            rms("n2", "sum2", D, 256, rstd)
            scale_tiles("h2", 256, lambda k, s: gs[:, k, 0:1])
            for t in range(TT):
                done(dve, ("rt", t))
            link(v.tensor_tensor(sel, lg, bc(vv("ebias"), [0, 2], [1, 64]), ALU.add))
            for t in range(TT):
                for g in range(GROUPS):
                    last = v.max(m8[:, t, g, :], sel[:, t, 8 * g:8 * g + 8])
            link(last)
            link(v.tensor_tensor(gsc, m8[:, :, :, 0], m8[:, :, :, 1], ALU.add))
            for t in range(TT):
                a0 = bc(gsc[:, t, :], [0, 8], [1, 8])
                a1 = bc(gsc[:, t, :], [1, 8], [0, 8])
                v.tensor_tensor(cmpa[:, t], a0, a1, ALU.is_gt)
                last = v.tensor_tensor(cmpb[:, t], a0, a1, ALU.is_equal)
            link(last)
            for t in range(TT):
                last = v.tensor_tensor(cmpb[:, t], cmpb[:, t], cc("gtri").rearrange("p (a b) -> p a b", a=8), ALU.mult)
            link(last)
            link(v.tensor_tensor(small[:, 400:528], small[:, 400:528], small[:, 528:656], ALU.add))
            link(v.tensor_reduce(small[:, 656:672], small[:, 400:528].rearrange("p (g b) -> p g b", b=8), AXX, ALU.add))
            link(v.tensor_scalar(small[:, 656:672], small[:, 656:672], float(TOPG) - 0.5, None, ALU.is_lt))
            link(v.tensor_scalar(small[:, 672:688], small[:, 656:672], -1.0, -NEG, ALU.add, ALU.mult))
            selg8 = small[:, 128:256].rearrange("p (g b) -> p g b", b=8)
            link(v.tensor_tensor(selg8, selg8, bc(small[:, 656:672], [1, 16], [0, 8]), ALU.mult))
            link(v.tensor_tensor(selg8, selg8, bc(small[:, 672:688], [1, 16], [0, 8]), ALU.add))
            for t in range(TT):
                last = v.max(top[:, t, :], sel[:, t, :])
            link(last)
            for t in range(TT):
                last = v.match_replace(out=rep[:, t, :], in_to_replace=top[:, t, :], in_values=sel[:, t, :], imm_value=-3e38)
            link(last)
            v.tensor_tensor(mask, rep, sel, ALU.not_equal).then_inc(S("mask"), 1)
            dve.wait_ge(S("mask"), 1)
            link(v.memset(gatx, 0.0))
            link(v.tensor_tensor(gatx[:, :, 0:64], lg, mask, ALU.mult))
            link(v.tensor_reduce(den[:, 2:4], gatx[:, :, 0:64], AXX, ALU.add))
            link(v.reciprocal(den[:, 2:4], den[:, 2:4]))
            for t in range(TT):
                last = v.tensor_scalar(gatx[:, t, 0:64], gatx[:, t, 0:64], den[:, 2 + t:3 + t], 2.5, ALU.mult, ALU.mult)
            link(last)
            for t in range(TT):
                v.tensor_copy(gatx[:, t, E:NONE].rearrange("p (a b) -> p a b", a=ROUNDS - 1), bc(gatx[:, t, 0:64], [0, ROUNDS - 1], [1, 64]))
            v.memset(yo[:, 0, :], 0.0).then_inc(S("zeros"), 1)
            for gg in range(4):
                w0, t = 512 * (gg % 2), gg // 2
                dve.wait_ge(S("part_a"), gg + 1)
                v.tensor_tensor(htok[:, gg % 2, :], bk(("tk", gg))[:, :], hbf[:, 0, t, w0:w0 + 512], ALU.subtract).then_inc(S("rest_a"), 1)
                dve.wait_ge(S("part_b"), gg + 1)
                emptied(v.tensor_tensor(hbf[:, 2, t, w0:w0 + 512], htok[:, gg % 2, :], hbf[:, 1, t, w0:w0 + 512], ALU.subtract), ("tk", gg))
            for t in range(2):
                full(dve, ("shu", t))
                done(dve, ("shg", t))
                emptied(v.tensor_tensor(shu[:, t, :], bk(("shu", t))[:, 0:256], shg[:, t, :], ALU.mult), ("shu", t))
            done(dve, ("shu", 0))
            done(dve, ("shu", 1))
            signal("sh_act")
            link(v.memset(posx, -1.0))
            full(dve, "pos")
            v.tensor_copy(counts, bk("pos")[:, 128:192])
            emptied(v.scalar_tensor_tensor(out=pos1, in0=bk("pos")[:, 0:128].rearrange("p (a b) -> p a b", a=2), scalar=1.0,
                                           in1=mask, op0=ALU.add, op1=ALU.mult), "pos")
            done(dve, "pos")
            for r in range(ROUNDS):
                last = v.tensor_scalar(posx[:, :, E * r:E * r + E], pos1, -1.0 - SLOTS * r, None, ALU.add)
            link(last)

            def pick(code, u):
                for t in range(TT):
                    v.tensor_scalar(selb[:, u, t, :], cc("iota")[:, 0:SLOTS], posx[:, t, bass.ds(code, 1)], None, ALU.is_equal)
                    last = v.tensor_scalar(selg[:, u, t, :], cc("iota"), posx[:, t, bass.ds(code, 1)], gatx[:, t, bass.ds(code, 1)],
                                           ALU.is_equal, ALU.mult)
                last.then_inc(S("sel_made"), 1)

            def item(i, u, next_code):
                n = UN * i + u
                dve.wait_ge(S("gu_full"), n + 1)
                dve.wait_ge(S("silu_made"), n + 1)
                v.tensor_tensor(hid[:, u, :], bank[B_GU][:, P:2 * P], sgt[:, u, :], ALU.mult).then_inc(S("hid_made"), 1)
                dve.wait_ge(S("x_full"), n + 1)
                v.tensor_copy(aT[:, u, :], bank[B_X][:, 0:P]).then_inc(S("aT_copied"), 1)
                v.tensor_copy(selT[:, u, :, :].rearrange("p a b -> p (a b)"), bank[B_X][:, P:3 * P]).then_inc(S("selT_copied"), 1)
                pick(next_code(), u)

            pick(0, 0)
            pick(1, 1)
            for r in range(1, ROUNDS):
                last = v.scalar_tensor_tensor(out=keys[:, E * (r - 1):E * r], in0=counts, scalar=SLOTS * r + 0.5,
                                              in1=cc("codes", E * (r - 1), E * r), op0=ALU.is_gt, op1=ALU.mult)
            link(last)
            link(v.memset(klist, 0.0))
            for m in range(MORE // 8):
                link(v.max(klist[:, 8 * m:8 * m + 8], keys))
                if m < MORE // 8 - 1:
                    link(v.match_replace(out=keys, in_to_replace=klist[:, 8 * m:8 * m + 8], in_values=keys, imm_value=0.0))
            link(v.tensor_scalar(clist, klist, -1.0, float(NONE), ALU.mult, ALU.add))
            link(v.tensor_scalar(elist, clist, -float(E), None, ALU.add))
            for r in range(2, ROUNDS + 1):
                link(v.tensor_scalar(lcmp, clist, E * r - 0.5, float(E), ALU.is_gt, ALU.mult))
                link(v.tensor_tensor(elist, elist, lcmp, ALU.subtract))
            link(v.tensor_scalar(lcmp, klist, 0.5, None, ALU.is_gt))
            link(v.tensor_reduce(nturn_f, bc(lcmp, [UN, MORE // UN]), AXX, ALU.add))
            v.tensor_copy(nturn, nturn_f)
            v.tensor_copy(codes, clist)
            link(v.tensor_copy(whose, elist))
            signal("listed")

            with dve.Fori(0, TURNS - 1) as i:
                for u in range(UN):
                    item(i, u, lambda: UN * i + (u + UN))
            dve.wait_ge(S("listed"), 1)

            def later(at):
                return dve.value_load(codes[0:1, bass.ds(at, 1)], min_val=0, max_val=NONE)

            for u in range(UN):
                item(TURNS - 1, u, lambda: later(u))
            more = dve.value_load(nturn[0:1, 0:1], min_val=0, max_val=MORE // UN)
            with dve.If(more > 0):
                with dve.Fori(0, more) as i:
                    for u in range(UN):
                        item(i + TURNS, u, lambda: later(UN * i + (u + UN)))

            for b in (0, 2):
                full(dve, ("sums", b))
                emptied(v.tensor_copy(acc[:, b // 2, 512 * (b % 2):512 * (b % 2) + 512], bank[b][:, :]), ("sums", b))
            for g in range(4):
                t, hf = g // 2, g % 2
                full(dve, ("ac", g))
                for k in range(4):
                    d = 4 * hf + k
                    last = residual(None, d, P * t, P * t + P, mod1[:, 40 + d:41 + d], src=bk(("ac", g))[:, P * k:P * k + P])
                emptied(last, ("ac", g))
            done(dve, ("ac", 2))
            done(dve, ("ac", 3))
            signal("x2")

            def gains(layer):
                g = vv("ng2", 8 * layer, 8 * layer + 8)
                link(v.scalar_tensor_tensor(out=gs[:, :, :], in0=mod2[:, 24 * layer + 8:24 * layer + 16, :], scalar=1.0,
                                            in1=bc(g, [1, 8], [0, 2]), op0=ALU.add, op1=ALU.mult))

            done(dve, ("ada2", 23))
            dve.wait_ge(S("const2_in"), 32)
            gains(0)
            rms("n3", "sum3", D, 512, rstd)
            scale_tiles("h3", 512, lambda k, s: gs[:, k, s:s + 1])
            for t in range(4):
                for s in range(2):
                    done(dve, (f"vab{s}", t))
                link(v.bn_stats(bn[:, t, 0:6], vtok[:, t, :]))
                link(v.bn_aggr(bn[:, t, 12:14], bn[:, t, 0:6]))
            link(v.tensor_scalar(bn[:, :, 13], bn[:, :, 13], EPS, None, ALU.add))
            signal("v_ms")
            dve.wait_ge(S("v_rt"), 1)
            link(v.reciprocal(bn[:, :, 13], bn[:, :, 13]))
            for t in range(4):
                v.tensor_scalar(vtok[:, t, :], vtok[:, t, :], bn[:, t, 12:13], bn[:, t, 13:14],
                                ALU.subtract, ALU.mult).then_inc(S("v_norm"), 1)
            for n in range(8):
                g, st = n // 2, n % 2
                full(dve, ("fb", n))
                done(dve, (f"z{2 + g // 2}", g % 2))
                z = zT[:, 4 + g, 256 * st:256 * st + 256]
                emptied(v.tensor_tensor(z, z, bk(("fb", n))[:, 0:256], ALU.mult), ("fb", n))
            for h in range(4):
                full(dve, ("sp", h))
                t1 = smt[:, h % 2, :]
                emptied(v.scalar_tensor_tensor(out=t1.rearrange("p (a b) -> p a b", a=4),
                                               in0=bk(("sp", h))[:, :].rearrange("p (a b) -> p a b", a=4), scalar=vv("vg", h, h + 1),
                                               in1=bc(vv("sb", P * h, P * h + P), [0, 4], [1, P]), op0=ALU.mult, op1=ALU.add), ("sp", h))
                done(dve, ("sp", h))
                done(dve, (f"z{4 + h // 2}", h % 2))
                done(dve, (f"z{6 + h // 2}", h % 2))
                link(v.tensor_tensor(t1, t1, zT[:, 8 + h, :], ALU.mult))
                v.tensor_tensor(zT[:, h, :], zT[:, h, :], t1, ALU.mult).then_inc(S("y_a"), 1)
            for d in range(8):
                full(dve, ("oab", d))
                residual(("oab", d), d, 0, 256, mod2[:, 16 + d, 0:1])
                emptied(residual(("oab", d), d, 256, 512, mod2[:, 16 + d, 1:2]), ("oab", d))
            done(dve, ("oab", 6))
            done(dve, ("oab", 7))
            signal("x3")
            gains(1)
            rms("n4", "sum4", D, 512, rstd)
            scale_tiles("h4", 512, lambda k, s: gs[:, k, s:s + 1])
            for j in range(10):
                full(dve, ("sw", j))
                src = k2[:, j, 0:256] if j < 2 else q2[:, j - 2, :]
                t1, t2 = rt1[:, j % 4, :], rt2[:, j % 4, :]
                emptied(v.tensor_tensor(t1, bk(("sw", j))[:, 0:256], cc("sin2"), ALU.mult), ("sw", j))
                link(v.tensor_tensor(t2, src, cc("cos2"), ALU.mult))
                done(dve, ("sw", j))
                v.tensor_tensor(src, t1, t2, ALU.add).then_inc(S("rope2"), 1)

            def c_scores(h):
                if h >= 4:
                    for j in range(2):
                        full(dve, ("c", "t", h - 4, j))
                for t in range(TT):
                    full(dve, ("c", "s", h, t))
                    emptied(v.scalar_tensor_tensor(out=probs("c", h)[:, 512 * t:512 * t + 512], in0=bk(("c", "s", h, t))[:, :], scalar=0.125,
                                                   in1=cc("wmask", 512 * t, 512 * t + 512), op0=ALU.mult, op1=ALU.add), ("c", "s", h, t))
                for t in range(TT):
                    done(dve, ("c", "s", h, t))
                a = att[:, h % 4, :]
                sink = bc(vv("sink", h, h + 1), [0, 2])
                link(v.tensor_reduce(a[:, 0:2], probs("c", h).rearrange("p (a b) -> p a b", a=2), AXX, ALU.max))
                link(v.tensor_tensor(a[:, 0:2], a[:, 0:2], sink, ALU.max))
                link(v.tensor_scalar(a[:, 2:4], a[:, 0:2], -1.0, None, ALU.mult))
                v.tensor_tensor(a[:, 0:2], sink, a[:, 2:4], ALU.add).then_inc(S("c_negmax"), 1)

            def c_out(i):
                full(dve, ("c", "o", i))
                done(dve, (f"g2{i // 2}", i % 2))
                emptied(v.tensor_tensor(o2[:, i, :], bk(("c", "o", i))[:, 0:256], g2s[:, i, :], ALU.mult), ("c", "o", i))

            c_scores(0)
            c_scores(1)
            for i in range(8):
                if i < 7:
                    c_scores(2 * i + 2)
                    c_scores(2 * i + 3)
                for h in (2 * i, 2 * i + 1):
                    dve.wait_ge(S("c_exp"), h + 1)
                    a = att[:, h % 4, :]
                    link(v.tensor_tensor(a[:, 4:6], a[:, 4:6], a[:, 6:8], ALU.add))
                    normalise("c", h, 512)
                if i >= 1:
                    c_out(i - 1)
            c_out(7)
            for d in range(8):
                full(dve, ("oc", d))
                emptied(residual(("oc", d), d, 0, 256, mod2[:, 40 + d, 0:1]), ("oc", d))
            done(dve, ("oc", 6))
            done(dve, ("oc", 7))
            signal("x4")
            rms("n5", "sum5", D, 256, rstd)
            for k in range(KT):
                v.scalar_tensor_tensor(out=outT[:, k, :], in0=xT[:, k, 0:256], scalar=vv("fg", k, k + 1), in1=rstd[:, 0:256],
                                       op0=ALU.mult, op1=ALU.mult).then_inc(S("y_out"), 1)


SLAB_COUNTS = dict(ada1=24, ada2=24, uq=1, ukv=1, pna=2, pmla=2, out=4, shg=1, shu=1, shd=1, ab=10, oab=4, cin=10, oc=4)
SLAB_COUNTS["in"] = 16
slabs_at, _n = {}, 0
for _k, _c in SLAB_COUNTS.items():
    slabs_at[_k] = _n
    _n += _c


def shape_constants():
    c, c2 = np.zeros((P, C_W), np.float64), np.zeros((P, C2_W), np.float64)

    def put(name, a):
        to, (lo, hi) = (c, C_AT[name]) if name in C_AT else (c2, C2_AT[name])
        a = np.asarray(a, np.float64)
        to[:a.shape[0], lo:hi] = a.reshape(a.shape[0], -1)

    i = np.arange(P)
    put("ident", np.eye(P))
    put("fold", np.stack([i % 32 == 0, i % 32 == 1], 1))
    put("bones", (i[:, None] // 64) == (i[None, :] // 64))
    m = np.zeros((96, 96))
    for r in range(16):
        m[80 + r, 64 + r] = -1.0
        m[64 + r, 80 + r] = 1.0
    put("perm96", m)
    m = np.zeros((P, P))
    for blk in range(4):
        for r in range(16):
            m[32 * blk + 16 + r, 32 * blk + r] = -1.0
            m[32 * blk + r, 32 * blk + 16 + r] = 1.0
    put("perm128", m)
    put("tri", i[:, None] < i[None, :])
    put("iota", np.tile(np.arange(2 * SLOTS) % SLOTS, (P, 1)))
    ang = TWO_PI * np.outer(i, i) / P
    put("dft_c", np.concatenate([np.cos(ang), -np.sin(ang)], 1))
    t = np.arange(T)
    angl = TWO_PI * (np.outer(t, t) % T) / T
    norm = 1 / np.sqrt(T * P)
    lt = np.stack([np.cos(angl), np.sin(angl)], 1) * norm
    put("dft_l", lt.reshape(2, P, 2, T).transpose(1, 0, 2, 3))
    inv = 10000.0 ** (-np.arange(16) / 16)
    row, col = np.repeat(np.arange(4), 64), np.tile(np.arange(64), 4)
    d = i % 64
    a2 = np.where((d < 32)[:, None], row[None, :], col[None, :]) * inv[d % 16][:, None]
    put("cos2", np.cos(a2))
    put("sin2", np.sin(a2))
    q = (np.arange(2)[None, :, None] * P + i[:, None, None])
    k = np.arange(T)[None, None, :]
    put("wmask", np.concatenate([np.where(np.abs(q - k) <= 128, 0.0, NEG), np.zeros((P, 2, T))], 2))
    cq, ck = (i % 64)[:, None], np.arange(64)[None, :]
    st = np.clip(cq - 8, 0, 48)
    put("namask", np.where((ck >= st) & (ck < st + 16), 0.0, NEG))
    put("invf", np.concatenate([np.zeros(64), inv, inv])[:, None])
    g = np.arange(8)
    put("gtri", np.broadcast_to((g[None, :] < g[:, None]).reshape(1, 64), (P, 64)))
    put("codes", np.broadcast_to(NONE - (E + np.arange((ROUNDS - 1) * E))[None, :], (P, (ROUNDS - 1) * E)))
    return c.astype(np.float32), c2.astype(np.float32)


def kernel(**inputs):
    import concourse.bacc as bacc
    from concourse.bass_utils import run_bass_kernel_spmd as run

    x = {k: np.asarray(v) for k, v in inputs.items()}

    def cols(a):
        return a.reshape(-1, P).T

    def rows(a):
        return np.broadcast_to(a.reshape(1, -1), (P, a.size))

    def pad96(a):
        return np.pad(a, (0, P - a.size))[:, None]

    c2 = np.stack([cols(x["c_2"][0]), cols(x["c_ctx_2"])], 2).reshape(P, 16)
    vec = dict(c=cols(x["c"][0]), c2=c2, b_ada=cols(x["b_ada"][0]), g1=cols(x["g_norm1"][0]),
               gq=np.tile(x["g_na_q"][0], 2)[:, None], gk=np.tile(x["g_na_k"][0], 2)[:, None],
               gql=cols(x["g_q_lat"][0]), gkv=cols(x["g_kv_lat"][0]), gmq=pad96(x["g_mla_q"][0]), gmk=pad96(x["g_mla_k"][0]),
               g2=cols(x["g_norm2"][0]), ng2=cols(x["norm_g_2"]), b2=cols(x["ada_b_2"]), vg=cols(x["v_norm_g_2"][0]),
               fg=cols(x["final_g_2"]), ebias=rows(x["e_bias"][0]), sb=rows(x["spatial_b_2"][0]))
    order = np.array([8 * (j // 8) + 4 * (j % 2) + (j % 8) // 2 for j in range(16)])
    vec["sink"] = rows(x["sink_logit_2"][0][order])
    vecs = np.concatenate([vec[k] for k in V_WIDTHS], 1)
    xT = np.concatenate([x["x"][0], x["ctx_2"][0]], 0).reshape(512, 8, P).transpose(2, 1, 0)

    def slab8(w):
        return w.reshape(8, P, -1, 256).transpose(2, 1, 0, 3).reshape(-1, P, SLAB)

    def slabk(w, k):
        w = w.reshape(k, P, -1, SLAB // k).transpose(2, 1, 0, 3)
        return w.reshape(-1, P, SLAB)

    w_in = np.pad(x["w_in"][0], ((0, 0), (0, 96)))
    w_in = np.concatenate([w_in[:, :1952], w_in[:, 4000:], w_in[:, 1952:4000]], 1)
    ukv = x["w_ukv"][0].reshape(P, 8, 2, 64).transpose(0, 2, 1, 3).reshape(P, 1024)
    ab = x["w_in_ab_2"][0]
    ab = np.concatenate([ab[:, 512:1024], ab[:, 1536:2048], ab[:, 2048:2560], ab[:, :512], ab[:, 1024:1536]], 1)
    cin = x["w_in_c_2"][0]
    by_head = lambda w: w.reshape(1024, 16, 64)[:, order].reshape(1024, 1024)
    cin = np.concatenate([cin[:, 1024:1536], by_head(cin[:, :1024]), by_head(cin[:, 1536:])], 1)
    oc = x["w_out_c_2"][0].reshape(16, 64, 1024)[order].reshape(1024, 1024)
    part = dict(ada1=slab8(x["w_ada"][0]), ada2=np.concatenate([slab8(x["ada_w_2"][0]), slab8(x["ada_w_2"][1])]),
                uq=np.pad(x["w_uq"][0].reshape(2, P, 768).transpose(1, 0, 2).reshape(1, P, 1536), ((0, 0), (0, 0), (0, 512))),
                ukv=np.pad(ukv, ((0, 0), (0, 1024)))[None],
                pna=slabk(x["w_proj_na"][0], 4), pmla=slabk(x["w_proj_mla"][0], 4), out=slab8(x["w_out"][0]),
                shg=slab8(x["w_sh_gate"][0]), shu=slab8(x["w_sh_up"][0]), shd=slabk(x["w_sh_down"][0], 2),
                ab=slab8(ab), oab=slab8(x["w_out_ab_2"][0]), cin=slab8(cin), oc=slab8(oc))
    part["in"] = slab8(w_in)
    stream = np.concatenate([part[k] for k in SLAB_COUNTS], 0)

    gu = np.stack([x["w_exp_gate"][0], x["w_exp_up"][0]], 0).reshape(2, E, 8, P, 2, P)
    gu = gu.transpose(1, 4, 3, 2, 0, 5).reshape(E, 2, P, SLAB)
    dn = x["w_exp_down"][0].reshape(E, 2, P, D).transpose(0, 2, 1, 3).reshape(E, 1, P, SLAB)
    experts = np.concatenate([gu, dn], 1)
    consts, consts2 = shape_constants()
    arrays = dict(
        xT=xT, consts=consts, consts2=consts2, vecs=vecs, positions=np.broadcast_to(x["positions"], (96, T)),
        rpb=x["na_rpb"][0][:, :, ::-1],
        spatial=x["spatial_w_2"][0].transpose(2, 0, 1), router=x["w_router"][0].reshape(8, P, E).transpose(1, 0, 2),
        stream=stream, experts=experts)
    arrays = {k: np.ascontiguousarray(v) for k, v in arrays.items()}
    nc = bacc.Bacc("TRN2", target_bir_lowering=False, num_devices=1)
    t = {k: nc.dram_tensor(k, v.shape, mybir.dt.from_np(v.dtype), kind="ExternalInput").ap() for k, v in arrays.items()}
    out = nc.dram_tensor("out", (P, KT, T), F32, kind="ExternalOutput").ap()
    build(nc, t["xT"], t["consts"], t["consts2"], t["vecs"], t["positions"], t["rpb"], t["spatial"], t["router"], t["stream"], t["experts"], out)
    r = run(nc, [arrays], core_ids=[0])
    return np.ascontiguousarray(r.results[0]["out"].transpose(2, 1, 0)).reshape(1, T, D)
```

```python
from contextlib import ExitStack

import numpy as np
import concourse.bass as bass
from concourse import mybir

ALU = mybir.AluOpType
ACT = mybir.ActivationFunctionType
F32 = mybir.dt.float32
BF16 = mybir.dt.bfloat16
I32 = mybir.dt.int32
AXX = mybir.AxisListType.X

P = 128
D = 1024
KT = D // P
T = 256
TT = T // P
E = 64
TOPK = 8
GROUPS = 8
TOPG = 4
FF = 256
SLOTS = 64
ROUNDS = T // SLOTS
SLAB = 2048
RING = 9
PER_E = 3
UN = 2
PAIRS = E // UN
MORE = 32
NONE = ROUNDS * E
EPS = 1e-6
NEG = -1e30
TWO_PI = 2 * np.pi
RUN = 5 * 31 + 64

C_WIDTHS = dict(fold=2, ident=P, bones=P, perm96=96, tri=P, iota=SLOTS, namask=64, invf=1, gtri=64,
                codes=(ROUNDS - 1) * E)
C2_WIDTHS = dict(perm128=P, dft_c=256, dft_l=4 * 256, cos2=256, sin2=256, wmask=2 * 512)
V_WIDTHS = dict(c=8, c2=16, b_ada=48, g1=8, gq=1, gk=1, gql=2, gkv=1, gmq=1, gmk=1, g2=8, ng2=16,
                b2=48, vg=4, fg=8, ebias=64, sink=16, sb=512)


def offsets(widths):
    at, out = 0, {}
    for k, w in widths.items():
        out[k] = (at, at + w)
        at += w
    return out, at


C_AT, C_W = offsets(C_WIDTHS)
C2_AT, C2_W = offsets(C2_WIDTHS)
V_AT, V_W = offsets(V_WIDTHS)


def build(nc, xT_d, consts_d, consts2_d, vecs_d, pos_d, rpb_d, spat_d, router_d, slabs_d, exp_d, out_d):
    with ExitStack() as ctx:
        def sb(name, shape, dt=F32):
            return ctx.enter_context(nc.sbuf_tensor(name, shape, dt))

        sems = {}

        def S(name):
            if name not in sems:
                sems[name] = ctx.enter_context(nc.semaphore(name))
            return sems[name]

        ring = sb("ring", [P, RING, SLAB])
        xT = sb("resid", [P, KT, 2 * T])
        hT = sb("hT", [P, KT, 2 * T])
        cs = sb("cs", [P, C_W])
        ve = sb("ve", [P, V_W])
        silc = sb("silc", [P, 8, 32])
        silc2 = sb("silc2", [P, 8, 32])
        quarters = sb("quarters", [P, 2, 256])
        mod1 = sb("mod1", [P, 48])
        mod2 = sb("mod2", [P, 48, 2])
        gs = sb("gs", [P, 8, 2])
        ones = sb("ones", [P, P])
        rstd = sb("rstd", [P, 512])
        stat = sb("stat", [P, 512])
        arena = sb("arena", [P, 17632])

        def ar(at, n, *dims, parts=P, lo=0):
            v = arena[lo:lo + parts, at:at + n]
            if len(dims) == 2:
                v = v.rearrange("p (a b) -> p a b", a=dims[0])
            if len(dims) == 3:
                v = v.rearrange("p (a b c) -> p a b c", a=dims[0], b=dims[1])
            return v

        def cc(name, a=0, b=None):
            src, at = (cs, C_AT) if name in C_AT else (cs2, C2_AT)
            lo, hi = at[name]
            return src[:, lo + a:(hi if b is None else lo + b)]

        def vv(name, a=0, b=None):
            lo, hi = V_AT[name]
            return ve[:, lo + a:(hi if b is None else lo + b)]

        qk = ar(0, 2048, 8, 256)
        vna = ar(2048, 1024, 2, 512)
        lat = ar(3072, 1024, 4, 256)
        sgate = ar(4096, 4096, 16, 256)
        qm = ar(8192, 2048, 8, 256)
        km = ar(10240, 2048, 8, 256)
        vm = ar(12288, 1024, 2, 512)
        yT = qk
        merged = qm
        varq = hT[0:96, :, T:2 * T]
        sqt = ar(13312, 1024, 2, 512)
        braw = ar(14336, 8 * RUN, 8, RUN)
        bmask = ar(16096, 1024, 2, 512)
        rope_c = ar(17120, 256)
        rope_s = ar(17376, 256)
        pr = sb("pr", [P, 2, 1024])
        pT = sb("pT", [P, 2, 1024])
        att = sb("att", [P, 4, 8])
        small = pT[:, :, :].rearrange("p a b -> p (a b)")
        hbf = arena[:, 0:3072].bitcast(BF16).rearrange("p (q t d) -> p q t d", q=3, t=2)
        htok = ar(3072, 1024, 2, 512)
        xg = ar(4096, 2 * 512, 2, 512)
        selb = ar(5120, 128).bitcast(BF16).rearrange("p (u t s) -> p u t s", u=2, t=2)
        selg = ar(5248, 256, 2, 128)
        sgt = ar(5504, 256)
        hid = ar(5760, 256)
        aT = ar(6016, 256, 2, 128)
        selT = ar(6272, 256, 2, 128)
        yo = ar(7040, 1024)
        acc = ar(8064, 2 * 1024, 2, 1024)
        shg = ar(12352, 512, 2, 256)
        shu = ar(12864, 512, 2, 256)
        small2 = pr[:, :, :].rearrange("p a b -> p (a b)")
        posx = small2[:, 0:2 * NONE + 2].rearrange("p (a b) -> p a b", a=2)
        gatx = small2[:, 514:514 + 2 * NONE + 2].rearrange("p (a b) -> p a b", a=2)
        counts = small2[:, 1028:1092]
        keys = small2[:, 1092:1092 + (ROUNDS - 1) * E]
        klist = small2[:, 1284:1284 + MORE + 2 * UN]
        clist = small2[:, 1328:1328 + MORE + 2 * UN]
        elist = small2[:, 1372:1372 + MORE + 2 * UN]
        lcmp = small2[:, 1416:1416 + MORE + 2 * UN]
        codes = small2[:, 1460:1460 + MORE + 2 * UN].bitcast(I32)
        whose = small2[:, 1504:1504 + MORE + 2 * UN].bitcast(I32)
        more_f = small2[:, 1548:1549]
        more_i = small2[:, 1549:1550].bitcast(I32)
        lg = small[:, 0:128].rearrange("p (a b) -> p a b", a=2)
        sel = small[:, 128:256].rearrange("p (a b) -> p a b", a=2)
        m8 = small[:, 256:384].rearrange("p (a g b) -> p a g b", a=2, g=8)
        gsc = small[:, 384:400].rearrange("p (a b) -> p a b", a=2)
        cmpa = small[:, 400:528].rearrange("p (a g b) -> p a g b", a=2, g=8)
        cmpb = small[:, 528:656].rearrange("p (a g b) -> p a g b", a=2, g=8)
        gmk = small[:, 656:672].rearrange("p (a b) -> p a b", a=2)
        top = small[:, 688:704].rearrange("p (a b) -> p a b", a=2)
        rep = small[:, 704:832].rearrange("p (a b) -> p a b", a=2)
        mask = small[:, 832:960].rearrange("p (a b) -> p a b", a=2)
        pos1 = small[:, 1224:1352].rearrange("p (a b) -> p a b", a=2)
        den = small[:, 1480:1484]
        wr = sb("wr", [P, 8, 64])
        mark = sb("mark", [1, 32])
        zT = ar(0, 8192, 16, 512)
        vtok = ar(8192, 2048, 4, 512)
        fa = ar(10240, 1024, 2, 512)
        smt = ar(11264, 1024, 2, 512)
        cs2 = ar(13376, C2_W)
        spat = ar(13376 + C2_W, 512, 4, 128)
        bn = ar(12800, 64, 4, 16)
        q2 = ar(0, 2048, 8, 256)
        g2s = ar(2048, 2048, 8, 256)
        k2 = ar(4096, 1024, 2, 512)
        v2 = ar(5120, 1024, 4, 256)
        o2 = ar(6144, 2048, 8, 256)
        rt1 = ar(8192, 1024, 4, 256)
        rt2 = ar(9216, 1024, 4, 256)
        outT = ar(0, 2048, 8, 256)

        bank = [ctx.enter_context(nc.psum_tensor(f"bank{b}", [P, 512], F32)) for b in range(8)]
        psum_full = [S(f"psum_full{b}") for b in range(8)]
        psum_done = [S(f"psum_done{b}") for b in range(8)]
        uses = [0] * 8
        place = {}

        def full(eng, name):
            b, n = place[name]
            eng.wait_ge(psum_full[b], n + 1)

        def done(eng, name):
            b, n = place[name]
            eng.wait_ge(psum_done[b], n + 1)

        def bk(name):
            return bank[place[name][0]]

        def emptied(ins, name):
            ins.then_inc(psum_done[place[name][0]], 1)

        slab_in = [S(f"slab_in{k}") for k in range(RING)]
        slabs = []
        slab_end = []

        def na_head(h):
            b = 64 * (h % 2)
            return dict(q=lambda t: qk[b:b + 64, h // 2, t * P:(t + 1) * P], k=[qk[b:b + 64, 4 + h // 2, :]],
                        v=lambda j: vna[:, j, 64 * h:64 * h + 64], o=b)

        def mla_head(h):
            return dict(q=lambda t: qm[0:96, h, t * P:(t + 1) * P], k=[km[0:96, h, :]],
                        v=lambda j: vm[:, j, 64 * h:64 * h + 64], o=64 * (h % 2))

        def c_head(h):
            b, g = 64 * (h % 2), h // 8
            return dict(q=lambda t: q2[b:b + 64, h // 2, t * P:(t + 1) * P], k=[k2[b:b + 64, g, :]],
                        v=lambda j: v2[:, j, 128 * g + b:128 * g + b + 64], o=b)

        KINDS = dict(na=(8, na_head, 256), mla=(8, mla_head, 256), c=(16, c_head, 512))

        def probs(kind, h):
            if kind == "c":
                return ar(9216 + 1024 * (h % 4), 1024)
            return pr[:, (h % 4) // 2, 512 * (h % 2):512 * (h % 2) + 512]

        GATE_FILL = [("ada1", j) for j in range(8, 24)]
        FILL = {(kind, i): [("ada2", 3 * (4 * n + i) + j) for j in range(3)]
                for n, kind in enumerate(("na", "mla")) for i in range(4)}

        B_G, B_GU, B_D = 4, 5, 6
        PAIR_USE = ("gu_half", "gu_full", "d_full")
        loads = []

        block = ctx.enter_context(nc.Block())

        @block.tensor
        def _(pe):
            mmul = nc.tensor.matmul

            def open_group(name, b):
                if uses[b]:
                    pe.wait_ge(psum_done[b], uses[b])
                place[name] = (b, uses[b])
                uses[b] += 1
                return bank[b]

            def close_group(ins, name):
                ins.then_inc(psum_full[place[name][0]], 1)

            def take_slab(src):
                n = len(slabs)
                slabs.append(src)
                slab_end.append(None)
                loads.append(1 + sum(m % RING == n % RING and slabs[m][0] != "exp" for m in range(n)))
                pe.wait_ge(slab_in[n % RING], 16 * loads[n])
                return ring[:, n % RING, :], n

            def ada_slab(which, j):
                w, n = take_slab((which, j))
                w = w.rearrange("p (k c) -> p k c", k=8)
                name = (which, j, "quarters")
                o = open_group(name, 6)
                for kk in range(2):
                    for g in range(4):
                        mm = mmul(o[32 * g:32 * g + 32, 0:256], (silc if which == "ada1" else silc2)[:, 4 * kk + g, :],
                                  w[:, 4 * kk + g, :], start=(kk == 0), stop=(kk == 1))
                close_group(mm, name)
                slab_end[n] = name
                if ada_prev:
                    ada_fold(*ada_prev.pop())
                ada_prev.append((which, j))

            ada_prev = []

            def ada_fold(which, j):
                done(pe, (which, j, "quarters"))
                o = open_group((which, j), 7)
                width = 1 if which == "ada1" else 2
                for t in range(2):
                    mm = mmul(o[:, t * width:(t + 1) * width], quarters[:, j % 2, t * P:(t + 1) * P], cc("fold", 0, width),
                              start=True, stop=True)
                close_group(mm, (which, j))

            def rms_sums(name, b, n_tok, tiles=KT, src=None, squared=None):
                o = open_group(name, b)
                for k in range(tiles):
                    if squared:
                        pe.wait_ge(S(squared), k + 1)
                    mm = mmul(o[:, 0:n_tok], ones[:], hT[:, k, 0:n_tok] if src is None else src(k),
                              start=(k == 0), stop=(k == tiles - 1))
                close_group(mm, name)

            def h_tile(name, k):
                pe.wait_ge(S(name), (2 if name in ("h3", "h4") else 1) * (k + 1))

            def t_tiles(tag, src, n_tiles, b, n_tok, ready=None):
                w, n = take_slab(src)
                w = w.rearrange("p (k c) -> p k c", k=8)
                for t in range(n_tiles):
                    name = (tag, t)
                    o = open_group(name, b[t % len(b)])
                    for k in range(KT):
                        if ready and t == 0:
                            h_tile(ready, k)
                        mm = mmul(o[:, 0:n_tok], w[:, k, t * P:(t + 1) * P], hT[:, k, 0:n_tok],
                                  start=(k == 0), stop=(k == KT - 1))
                    close_group(mm, name)
                slab_end[n] = name

            def tok_tiles(tag, src, toks, b, ready=None):
                w, n = take_slab(src)
                w = w.rearrange("p (k c) -> p k c", k=8)
                for t in range(toks):
                    name = (tag, t)
                    o = open_group(name, b[t % len(b)])
                    for k in range(KT):
                        if ready and t == 0:
                            h_tile(ready, k)
                        mm = mmul(o[:, 0:256], hT[:, k, t * P:(t + 1) * P], w[:, k, :],
                                  start=(k == 0), stop=(k == KT - 1))
                    close_group(mm, name)
                slab_end[n] = name

            def attention(kind):
                n_heads, head, nk = KINDS[kind]
                per = nk // 256

                def scores(i):
                    if kind == "mla":
                        pe.wait_ge(S("m_ready"), 2 * i + 2)
                    for t in range(TT):
                        for h in (2 * i, 2 * i + 1):
                            hd = head(h)
                            if nk == 256:
                                name = (kind, "s", h)
                                if t == 0:
                                    open_group(name, h % 2)
                                mm = mmul(bk(name)[:, 256 * t:256 * t + 256], hd["q"](t), hd["k"][0], start=True, stop=True)
                                if t == 1:
                                    close_group(mm, name)
                            else:
                                name = (kind, "s", h, t)
                                o = open_group(name, (0 if h % 2 == 0 else 6) + t)
                                close_group(mmul(o[:, :], hd["q"](t), hd["k"][0], start=True, stop=True), name)

                def turn(h):
                    pe.wait_ge(S(kind + "_probs"), h + 1)
                    for j in range(per):
                        name = (kind, "t", h, j)
                        o = open_group(name, 2 + (h % 2 if per == 1 else j))
                        for kt in range(2):
                            for t in range(TT):
                                at = t * nk + (2 * j + kt) * P
                                mm = nc.tensor.transpose(o[:, 256 * kt + P * t:256 * kt + P * t + P],
                                                         probs(kind, h)[:, at:at + P], cc("ident"))
                        close_group(mm, name)

                def values(i):
                    name = (kind, "o", i)
                    o = open_group(name, 4 + i % 2)
                    for h in (2 * i, 2 * i + 1):
                        for j in range(per):
                            done(pe, (kind, "t", h, j))
                    for kt in range(2 * per):
                        for h in (2 * i, 2 * i + 1):
                            hd = head(h)
                            mm = mmul(o[hd["o"]:hd["o"] + 64, 0:256], hd["v"](kt), pT[:, h % 2, 256 * kt:256 * kt + 256],
                                      start=(kt == 0), stop=(kt == 2 * per - 1))
                    close_group(mm, name)

                scores(0)
                for i in range(n_heads // 2):
                    if 2 * i + 2 < n_heads:
                        scores(i + 1)
                    for f in FILL.get((kind, i), []):
                        ada_slab(*f)
                    turn(2 * i)
                    turn(2 * i + 1)
                    values(i)

            pe.wait_ge(S("ones_set"), 1)
            rms_sums("sum1", 0, 256, squared="sq1")
            pe.wait_ge(S("silu_c"), 1)
            pe.wait_ge(S("const_in"), 48)
            for j in range(8):
                ada_slab("ada1", j)
            ada_fold(*ada_prev.pop())
            pe.wait_ge(S("ones_set"), 1)
            pe.wait_ge(S("const_in"), 48)
            for s in range(4):
                t_tiles(f"qk{s}", ("in", s), 2, [1, 2], 256, ready="h1" if s == 0 else None)
                for t in range(2):
                    j = 2 * s + t
                    pe.wait_ge(S("sq_qk"), j + 1)
                    o = open_group(("qkn", j), 3 + j % 2)
                    close_group(mmul(o[:, 0:256], cc("bones"), sqt[:, j % 2, 0:256], start=True, stop=True), ("qkn", j))
            for s in range(2):
                tok_tiles(f"vna{s}", ("in", 4 + s), 2, [1, 2])
            t_tiles("ql", ("in", 6), 2, [1, 2], 256)
            w, n = take_slab(("in", 7))
            w = w.rearrange("p (k c) -> p k c", k=8)
            o = open_group("kvl", 3)
            for k in range(KT):
                mm = mmul(o[:, 0:256], w[:, k, 0:P], hT[:, k, 0:256], start=(k == 0), stop=(k == KT - 1))
            close_group(mm, "kvl")
            o = open_group("krot", 4)
            for k in range(KT):
                mm = mmul(o[64:96, 0:256], w[:, k, P:P + 32], hT[:, k, 0:256], start=(k == 0), stop=(k == KT - 1))
            close_group(mm, "krot")
            slab_end[n] = "krot"
            pe.wait_ge(S("sq_ql"), 2)
            rms_sums("sum_ql", 5, 256, tiles=2, src=lambda k: sqt[:, k, 0:256])
            pe.wait_ge(S("sq_kvl"), 1)
            rms_sums("sum_kvl", 6, 256, tiles=1, src=lambda k: sqt[:, k, 256:512])

            def gate_tiles(s):
                t_tiles(f"gt{s}", ("in", 8 + s), 2, [1, 2], 256)
                for f in GATE_FILL[2 * s:2 * s + 2]:
                    ada_slab(*f)

            gate_tiles(0)
            gate_tiles(1)
            pe.wait_ge(S("qln"), 2)
            w, n = take_slab(("uq", 0))
            w = w[:, 0:1536].rearrange("p (k c) -> p k c", k=2)
            for g in range(4):
                o = open_group(("uq", g), 1 + g % 2)
                for h in range(2):
                    for k in range(2):
                        mm = mmul(o[0:96, 256 * h:256 * h + 256], w[:, k, 96 * (2 * g + h):96 * (2 * g + h) + 96],
                                  lat[:, k, :], start=(k == 0), stop=(k == 1))
                close_group(mm, ("uq", g))
            slab_end[n] = ("uq", 3)
            pe.wait_ge(S("kvn"), 1)
            w, n = take_slab(("ukv", 0))
            for g in range(4):
                o = open_group(("uk", g), 1 + g % 2)
                for h in range(2):
                    mm = mmul(o[0:64, 256 * h:256 * h + 256], w[:, 64 * (2 * g + h):64 * (2 * g + h) + 64],
                              lat[:, 2, :], start=True, stop=True)
                close_group(mm, ("uk", g))
            for t in range(2):
                o = open_group(("uv", t), 1 + t % 2)
                close_group(mmul(o[:, :], lat[:, 2, t * P:(t + 1) * P], w[:, 512:1024], start=True, stop=True), ("uv", t))
            slab_end[n] = ("uv", 1)
            gate_tiles(2)
            for g in range(4):
                done(pe, ("uq", g))
                o = open_group(("qsw", g), 1 + g % 2)
                close_group(mmul(o[0:96, :], cs[0:96, C_AT["perm96"][0]:C_AT["perm96"][1]],
                                 qm[0:96, 2 * g:2 * g + 2, :].rearrange("p a b -> p (a b)"), start=True, stop=True), ("qsw", g))
            pe.wait_ge(S("kr_zero"), 1)
            done(pe, "krot")
            o = open_group("ksw", 3)
            close_group(mmul(o[0:96, 0:256], cs[0:96, C_AT["perm96"][0]:C_AT["perm96"][1]], lat[0:96, 3, :],
                             start=True, stop=True), "ksw")
            gate_tiles(3)
            gate_tiles(4)
            for g in range(8):
                pe.wait_ge(S("sq_m"), g + 1)
                o = open_group(("msum", g), 1 + g % 2)
                close_group(mmul(o[0:96, :], ones[0:96, 0:96], sqt[0:96, g % 2, :], start=True, stop=True), ("msum", g))
            for s in range(5, 8):
                gate_tiles(s)
            ada_fold(*ada_prev.pop())
            pe.wait_ge(S("qk_ready"), 8)
            attention("na")
            attention("mla")
            ada_fold(*ada_prev.pop())
            done(pe, ("na", "o", 3))
            done(pe, ("mla", "o", 3))
            for half in range(2):
                wa, na = take_slab(("pna", half))
                wb, nb = take_slab(("pmla", half))
                for t in range(4):
                    d = 4 * half + t
                    for tag, w, y0, b in (("pn", wa, 0, 0), ("pm", wb, 4, 1)):
                        o = open_group((tag, d), b + 2 * (d % 2))
                        for k in range(4):
                            mm = mmul(o[:, 0:256], w[:, 512 * k + P * t:512 * k + P * t + P], yT[:, y0 + k, :],
                                      start=(k == 0), stop=(k == 3))
                        close_group(mm, (tag, d))
                slab_end[na] = slab_end[nb] = ("pm", d)
            pe.wait_ge(S("merged"), 8)
            for s in range(4):
                w, n = take_slab(("out", s))
                w = w.rearrange("p (k c) -> p k c", k=8)
                for t in range(2):
                    o = open_group(("wo", 2 * s + t), 4 + t)
                    for k in range(KT):
                        mm = mmul(o[:, 0:256], w[:, k, t * P:(t + 1) * P], merged[:, k, :], start=(k == 0), stop=(k == KT - 1))
                    close_group(mm, ("wo", 2 * s + t))
                slab_end[n] = ("wo", 2 * s + 1)
            rms_sums("sum2", 0, 256, squared="sq2")
            for t in range(TT):
                o = open_group(("rt", t), 6)
                for k in range(KT):
                    if t == 0:
                        h_tile("h2", k)
                    mm = mmul(o[:, 0:64], hT[:, k, t * P:(t + 1) * P], wr[:, k, :], start=(k == 0), stop=(k == KT - 1))
                close_group(mm, ("rt", t))
            for g in range(4):
                o = open_group(("tk", g), 1 + g % 2)
                for k in range(4):
                    mm = nc.tensor.transpose(o[:, P * k:P * k + P],
                                             hT[:, 4 * (g % 2) + k, (g // 2) * P:(g // 2) * P + P], cc("ident"))
                close_group(mm, ("tk", g))
            t_tiles("shg", ("shg", 0), 2, [3, 4], 256)
            t_tiles("shu", ("shu", 0), 2, [3, 4], 256)
            pe.wait_ge(S("mask"), 1)
            o = open_group("pos", 7)
            mmul(o[:, 0:64], cc("tri"), mask[:, 0, :], start=True, stop=True)
            mmul(o[:, 64:128], ones[:], mask[:, 0, :], start=True, stop=False)
            mmul(o[:, 64:128], cc("tri"), mask[:, 1, :], start=False, stop=True)
            mmul(o[:, 128:192], ones[:], mask[:, 0, :], start=True, stop=False)
            mm = mmul(o[:, 128:192], ones[:], mask[:, 1, :], start=False, stop=True)
            close_group(mm, "pos")

            moe_slab0 = len(slabs)
            for j in range(PER_E):
                for u in range(UN):
                    slabs.append(("exp", j, u))
                    slab_end.append(None)
                    loads.append(None)
            for b in range(4, 8):
                if uses[b]:
                    pe.wait_ge(psum_done[b], uses[b])
            pe.wait_ge(S("zeros"), 1)
            zero = yo[:, 0:256].bitcast(BF16)
            for b in range(4):
                mmul(open_group(("sums", b), b)[:, :], zero[:, 0:P], zero, start=True, stop=False)

            def gather(n, u):
                pe.wait_ge(S("sel_made"), n + 1)
                for d in range(8):
                    for t in range(TT):
                        for q in range(3):
                            mm = mmul(bank[B_G][:, SLOTS * d:SLOTS * d + SLOTS], hbf[:, q, t, P * d:P * d + P],
                                      selb[:, u, t, :], start=(t == 0 and q == 0), stop=(t == 1 and q == 2))
                mm.then_inc(S("g_full"), 1)

            def scatter():
                for b in range(4):
                    mmul(bank[b][:, :], selT[:, b // 2, :], yo[:, 512 * (b % 2):512 * (b % 2) + 512], start=False, stop=False)

            def pair(m, first=False):
                def arrived(j, u):
                    pe.wait_ge(S(f"item_in{u}{j}"), 16 * m + 16)
                    return ring[:, (moe_slab0 + UN * j + u) % RING, :].rearrange("p (k c) -> p k c", c=512)

                pe.wait_ge(S("xg_copied"), UN * m + 2)
                for half in range(2):
                    w = [arrived(half, u) for u in range(UN)]
                    for k in range(KT // 2):
                        kk = KT // 2 * half + k
                        for u in range(UN):
                            mm = mmul(bank[B_GU][64 * u:64 * u + 64, :], xg[:, u, SLOTS * kk:SLOTS * kk + SLOTS], w[u][:, k, :],
                                      start=(kk == 0), stop=(kk == KT - 1))
                    mm.then_inc(S(("gu_half", "gu_full")[half]), 1)
                gather(UN * m + 2, 0)
                if not first:
                    pe.wait_ge(S("y_copied"), m)
                    scatter()
                pe.wait_ge(S("hid_made"), m + 1)
                pe.wait_ge(S("selg_made"), m + 1)
                for f in range(2):
                    mm = nc.tensor.transpose(bank[B_D][:, P * f:P * f + P], hid[:, P * f:P * f + P], cc("ident"))
                for t in range(TT):
                    mm = nc.tensor.transpose(bank[B_D][:, 2 * P + P * t:3 * P + P * t], selg[:, t, :], cc("ident"))
                mm.then_inc(S("x_full"), 1)
                pe.wait_ge(S("xg_copied"), UN * m + 3)
                gather(UN * m + 3, 1)
                pe.wait_ge(S("selT_copied"), m + 1)
                w = [arrived(2, u) for u in range(UN)]
                for c in range(2):
                    for f in range(2):
                        for u in range(UN):
                            mm = mmul(bank[B_D + c][64 * u:64 * u + 64, :], aT[:, f, 64 * u:64 * u + 64], w[u][:, 2 * f + c, :],
                                      start=(f == 0), stop=(f == 1))
                mm.then_inc(S("d_full"), 1)

            pe.wait_ge(S("sh_act"), 1)
            gather(0, 0)
            pe.wait_ge(S("xg_copied"), 1)
            gather(1, 1)
            pair(0, first=True)
            with pe.Fori(1, PAIRS) as m:
                pair(m)
            pe.wait_ge(S("listed"), 1)
            more = pe.value_load(more_i[0:1, 0:1], min_val=0, max_val=MORE // UN)
            with pe.If(more > 0):
                with pe.Fori(0, more) as m:
                    pair(m + PAIRS)
            pe.wait_ge(S("y_copied"), more + PAIRS)
            pe.wait_ge(S("xg_copied"), UN * more + (E + UN))
            scatter()
            w, n = take_slab(("shd", 0))
            for b in range(4):
                for f in range(2):
                    mm = mmul(bank[b][:, :], shu[:, f, P * (b // 2):P * (b // 2) + P],
                              w[:, 1024 * f + 512 * (b % 2):1024 * f + 512 * (b % 2) + 512], start=False, stop=(f == 1))
                close_group(mm, ("sums", b))
            slab_end[n] = ("sums", 3)

            for g in range(4):
                done(pe, ("sums", g))
                o = open_group(("ac", g), 4 + g % 4)
                for k in range(4):
                    at = 512 * (g % 2) + P * k
                    mm = nc.tensor.transpose(o[:, P * k:P * k + P], acc[:, g // 2, at:at + P], cc("ident"))
                close_group(mm, ("ac", g))

            rms_sums("sum3", 0, 512, squared="sq3")
            pe.wait_ge(S("const2_in"), 32)
            for s in range(2):
                tok_tiles(f"vab{s}", ("ab", s), 4, [1, 2], ready="h3" if s == 0 else None)
            for s in range(8):
                t_tiles(f"z{s}", ("ab", 2 + s), 2, [3, 4], 512)
            for g in range(4):
                for st in range(2):
                    n = 2 * g + st
                    done(pe, (f"z{g // 2}", g % 2))
                    o = open_group(("fa", n), 5 + n % 2)
                    for t in range(TT):
                        at = 256 * st + P * t
                        mm = mmul(o[:, 256 * t:256 * t + 256], zT[:, 12 + g, at:at + P], cc("dft_c"), start=True, stop=True)
                    close_group(mm, ("fa", n))
                    done(pe, ("fa", n))
                    o = open_group(("fb", n), 0 if n % 2 else 7)
                    for t in range(TT):
                        for c in range(2):
                            mm = mmul(o[:, 0:256], fa[:, n % 2, 256 * t + P * c:256 * t + P * c + P],
                                      cc("dft_l", 512 * t + 256 * c, 512 * t + 256 * c + 256),
                                      start=(t == 0 and c == 0), stop=(t == 1 and c == 1))
                    close_group(mm, ("fb", n))
            pe.wait_ge(S("v_norm"), 4)
            for h in range(4):
                o = open_group(("sp", h), 1 + h % 2)
                for t in range(4):
                    mm = mmul(o[:, P * t:P * t + P], vtok[:, t, P * h:P * h + P], spat[:, h, :], start=True, stop=True)
                close_group(mm, ("sp", h))
            pe.wait_ge(S("y_a"), 4)
            done(pe, ("fb", 7))
            done(pe, ("fb", 6))
            for s in range(4):
                w, n = take_slab(("oab", s))
                w = w.rearrange("p (k c) -> p k c", k=8)
                for t in range(2):
                    o = open_group(("oab", 2 * s + t), 3 + t)
                    for k in range(KT):
                        mm = mmul(o[:, :], w[:, k, t * P:(t + 1) * P], zT[:, k, :], start=(k == 0), stop=(k == KT - 1))
                    close_group(mm, ("oab", 2 * s + t))
                slab_end[n] = ("oab", 2 * s + 1)
            rms_sums("sum4", 0, 512, squared="sq4")
            t_tiles("k2", ("cin", 0), 2, [1, 2], 512, ready="h4")
            tok_tiles("v2", ("cin", 1), 4, [1, 2])
            for s in range(4):
                t_tiles(f"q2{s}", ("cin", 2 + s), 2, [3, 4], 256)
            for s in range(4):
                t_tiles(f"g2{s}", ("cin", 6 + s), 2, [3, 4], 256)
            for j in range(10):
                done(pe, ("k2", j) if j < 2 else (f"q2{(j - 2) // 2}", j % 2))
                src = k2[:, j, 0:256] if j < 2 else q2[:, j - 2, :]
                o = open_group(("sw", j), 1 + j % 2)
                close_group(mmul(o[:, 0:256], cc("perm128"), src, start=True, stop=True), ("sw", j))
            pe.wait_ge(S("rope2"), 10)
            done(pe, ("v2", 2))
            done(pe, ("v2", 3))
            attention("c")
            done(pe, ("c", "o", 7))
            done(pe, ("c", "o", 6))
            for s in range(4):
                w, n = take_slab(("oc", s))
                w = w.rearrange("p (k c) -> p k c", k=8)
                for t in range(2):
                    o = open_group(("oc", 2 * s + t), t)
                    for k in range(KT):
                        mm = mmul(o[:, 0:256], w[:, k, t * P:(t + 1) * P], o2[:, k, :], start=(k == 0), stop=(k == KT - 1))
                    close_group(mm, ("oc", 2 * s + t))
                slab_end[n] = ("oc", 2 * s + 1)
            rms_sums("sum5", 2, 256, squared="sq5")

        exp0 = next(n for n, s in enumerate(slabs) if s[0] == "exp")

        @block.sync
        def _(sp):
            def load(n):
                slot = n % RING
                src = slabs[n]
                w = slabs_d[slabs_at[src[0]] + src[1]]
                sp.dma_start(ring[:, slot, :], w).then_inc(slab_in[slot], 16)

            def slab_read(n):
                full(sp, slab_end[n])

            for n in range(exp0):
                if n >= RING:
                    slab_read(n - RING)
                load(n)

            def pair_slabs(m, experts):
                for j in range(PER_E):
                    if isinstance(m, int):
                        for u in range(UN):
                            slab_read(exp0 + UN * j + u - RING)
                    else:
                        sp.wait_ge(S(PAIR_USE[j]), m)
                    for u in range(UN):
                        sp.dma_start(ring[:, (exp0 + UN * j + u) % RING, :], exp_d[experts[u], j]).then_inc(S(f"item_in{u}{j}"), 16)

            pair_slabs(0, range(UN))
            after = exp0 + UN * PER_E
            for n in range(after, exp0 + RING):
                slab_read(n - RING)
                load(n)
            with sp.Fori(1, PAIRS) as m:
                pair_slabs(m, [UN * m + u for u in range(UN)])
            sp.wait_ge(S("listed"), 1)
            more = sp.value_load(more_i[0:1, 0:1], min_val=0, max_val=MORE // UN)
            with sp.If(more > 0):
                with sp.Fori(0, more) as m:
                    pair_slabs(m + PAIRS, [sp.value_load(whose[0:1, bass.ds(UN * m + u, 1)], min_val=0, max_val=E - 1)
                                           for u in range(UN)])
            for n in range(exp0 + RING, len(slabs)):
                if n < after + RING:
                    sp.wait_ge(S(PAIR_USE[(n - exp0 - RING) // UN]), more + PAIRS)
                else:
                    slab_read(n - RING)
                load(n)

        @block.gpsimd
        def _(pool):
            g = nc.gpsimd
            g.memset(silc[:], 0.0).then_inc(S("silc_zero"), 1)
            g.memset(silc2[:], 0.0).then_inc(S("silc_zero"), 1)
            g.memset(ones[:], 1.0).then_inc(S("ones_set"), 1)
            g.memset(lat[0:64, 3, :], 0.0).then_inc(S("kr_zero"), 1)
            pool.wait_ge(S("const_in"), 48)
            pool.wait_ge(S("bias_in"), 32)
            for h in range(8):
                if h == 2:
                    pool.wait_ge(S("rope_tab"), 1)
                    for gg in range(4):
                        full(pool, ("qsw", gg))
                        for hh in range(2):
                            v = qm[0:96, 2 * gg + hh, :]
                            last = g.tensor_tensor(v, v, rope_c[0:96, :], ALU.mult)
                        last.then_inc(S("q_cos"), 1)
                    done(pool, GATE_FILL[-1])
                    g.tensor_tensor(mod1[:, 16:48], mod1[:, 16:48], vv("b_ada", 16, 48), ALU.add).then_inc(S("mod1_made"), 1)
                if h >= 2:
                    done(pool, ("na", "s", h - 2))
                for t in range(TT):
                    r = braw[:, h, :]
                    rev = bass.AP(r.tensor, r.offset + 62 * (1 - t) + 63, [list(r.ap[0]), [31, 4], [-1, 64]])
                    m = cc("namask")
                    mb = bass.AP(m.tensor, m.offset, [list(m.ap[0]), [0, 4], [1, 64]])
                    g.tensor_tensor(bmask[:, h % 2, 256 * t:256 * t + 256].rearrange("p (a b) -> p a b", a=4),
                                    rev, mb, ALU.add).then_inc(S("bias_made"), 1)

            pool.wait_ge(S("x1"), 1)
            pool.dma_start(cs2, consts2_d).then_inc(S("const2_in"), 16)
            pool.dma_start(spat, spat_d).then_inc(S("const2_in"), 16)

        @block.scalar
        def _(act):
            a = nc.scalar
            steps = [0]

            def link(ins):
                steps[0] += 1
                ins.then_inc(S("act_step"), 1)
                act.wait_ge(S("act_step"), steps[0])

            act.dma_start(ve[:], vecs_d).then_inc(S("vec_in"), 16)
            act.dma_start(cs[:], consts_d).then_inc(S("const_in"), 16)
            act.dma_start(xT[:, :, 0:T], xT_d[:, :, 0:T]).then_inc(S("x_in"), 16)
            act.dma_start(stat[0:96, 0:256].bitcast(I32), pos_d).then_inc(S("const_in"), 16)
            act.dma_start(wr[:], router_d).then_inc(S("const_in"), 16)
            for r in range(2):
                src = bass.AP(rpb_d.tensor, (5 - r) * 31 - 48, [[1, 64], [15 * 31, 8], [1, RUN]])
                act.dma_start(braw[64 * r:64 * r + 64, :, :], src).then_inc(S("bias_in"), 16)
            act.wait_ge(S("vec_in"), 16)
            act.wait_ge(S("silc_zero"), 2)
            a.activation(silc[:, :, 0], vv("c"), ACT.Silu)
            a.activation(silc2[:, :, 0:2], vv("c2").rearrange("p (a b) -> p a b", a=8), ACT.Silu).then_inc(S("silu_c"), 1)
            act.wait_ge(S("x_in"), 16)
            for k in range(KT):
                a.activation(hT[:, k, 0:256], xT[:, k, 0:256], ACT.Square).then_inc(S("sq1"), 1)

            def ada_quarters(which, j):
                name = (which, j, "quarters")
                full(act, name)
                emptied(a.copy(quarters[:, j % 2, :], bk(name)[:, 0:256]), name)

            def ada_columns(which, j):
                full(act, (which, j))
                emptied(a.copy(mod1[:, 2 * j:2 * j + 2], bk((which, j))[:, 0:2]), (which, j))

            def root(n, src, tag, cols, parts=P):
                act.wait_ge(S(tag + "_ms"), n)
                a.activation(src[0:parts, 0:cols], src[0:parts, 0:cols], ACT.Sqrt).then_inc(S(tag + "_rt"), 1)

            root(1, rstd, "n1", 256)
            for j in range(8):
                ada_quarters("ada1", j)

            def squares(tag, cols, residual):
                for k in range(KT):
                    done(act, residual(k))
                    a.activation(hT[:, k, 0:cols], xT[:, k, 0:cols], ACT.Square).then_inc(S(tag), 1)

            def shifts(tag, cols, shift):
                for k in range(KT):
                    for s in range(cols // 256):
                        n = k * (cols // 256) + s
                        act.wait_ge(S(tag + "_scaled"), n + 1)
                        v = hT[:, k, 256 * s:256 * s + 256]
                        a.activation(v, v, ACT.Identity, bias=shift(k, s)).then_inc(S(tag), 1)

            act.wait_ge(S("angle"), 1)
            a.activation(rope_s[0:96, :], sqt[0:96, 0, 0:256], ACT.Sin)
            a.activation(rope_c[0:96, :], sqt[0:96, 1, 0:256], ACT.Sin).then_inc(S("rope_tab"), 1)
            shifts("h1", 256, lambda k, s: mod1[:, k:k + 1])
            for s in range(4):
                for t in range(2):
                    j = 2 * s + t
                    full(act, (f"qk{s}", t))
                    if j >= 2:
                        full(act, ("qkn", j - 2))
                    a.activation(sqt[:, j % 2, 0:256], bk((f"qk{s}", t))[:, 0:256], ACT.Square).then_inc(S("sq_qk"), 1)
                    emptied(a.copy(qk[:, j, :], bk((f"qk{s}", t))[:, 0:256]), (f"qk{s}", t))
            for s in range(2):
                for t in range(2):
                    full(act, (f"vna{s}", t))
                    emptied(a.copy(vna[:, t, 256 * s:256 * s + 256], bk((f"vna{s}", t))[:, 0:256]), (f"vna{s}", t))
            for t in range(2):
                full(act, ("ql", t))
                full(act, ("qkn", 6 + t))
                a.activation(sqt[:, t, 0:256], bk(("ql", t))[:, 0:256], ACT.Square).then_inc(S("sq_ql"), 1)
                emptied(a.copy(lat[:, t, :], bk(("ql", t))[:, 0:256]), ("ql", t))
            full(act, "kvl")
            a.activation(sqt[:, 0, 256:512], bk("kvl")[:, 0:256], ACT.Square).then_inc(S("sq_kvl"), 1)
            emptied(a.copy(lat[:, 2, :], bk("kvl")[:, 0:256]), "kvl")
            full(act, "krot")
            emptied(a.copy(lat[64:96, 3, :], bk("krot")[64:96, 0:256]), "krot")
            root(1, stat, "lt", 512)
            root(1, pr[:, :, :].rearrange("p a b -> p (a b)"), "qk", 2048)
            act.dma_start(xT[:, :, T:2 * T], xT_d[:, :, T:2 * T]).then_inc(S("ctx_in"), 16)
            def gate_tiles(s):
                for t in range(2):
                    full(act, (f"gt{s}", t))
                    emptied(a.activation(sgate[:, 2 * s + t, :], bk((f"gt{s}", t))[:, 0:256], ACT.Sigmoid), (f"gt{s}", t))
                for f in (2 * s, 2 * s + 1):
                    ada_quarters(*GATE_FILL[f])
                    if f:
                        ada_columns(*GATE_FILL[f - 1])

            gate_tiles(0)
            gate_tiles(1)
            for gg in range(4):
                full(act, ("uq", gg))
                emptied(a.copy(qm[0:96, 2 * gg:2 * gg + 2, :].rearrange("p a b -> p (a b)"), bk(("uq", gg))[0:96, :]), ("uq", gg))
            for gg in range(4):
                full(act, ("uk", gg))
                emptied(a.copy(km[0:64, 2 * gg:2 * gg + 2, :].rearrange("p a b -> p (a b)"), bk(("uk", gg))[0:64, :]), ("uk", gg))
            for t in range(2):
                full(act, ("uv", t))
                emptied(a.copy(vm[:, t, :], bk(("uv", t))[:, :]), ("uv", t))
            for s in (2, 3, 4):
                gate_tiles(s)
            for gg in range(8):
                act.wait_ge(S("m_in"), gg + 1)
                if gg >= 2:
                    full(act, ("msum", gg - 2))
                v = (qm if gg < 4 else km)[0:96, 2 * (gg % 4):2 * (gg % 4) + 2, :].rearrange("p a b -> p (a b)")
                a.activation(sqt[0:96, gg % 2, :], v, ACT.Square).then_inc(S("sq_m"), 1)
            gate_tiles(5)
            act.wait_ge(S("mq_ms"), 1)
            a.activation(varq, varq, ACT.Sqrt).then_inc(S("mq_rt"), 1)
            root(1, pT[:, :, :].rearrange("p a b -> p (a b)"), "mk", 2048, 96)
            gate_tiles(6)
            gate_tiles(7)
            ada_columns(*GATE_FILL[-1])

            def attention(kind):
                n_heads, _, nk = KINDS[kind]
                for i in range(n_heads // 2):
                    for h in (2 * i, 2 * i + 1):
                        act.wait_ge(S(kind + "_negmax"), h + 1)
                        if kind == "c":
                            a.activation(att[:, h % 4, 6:8], att[:, h % 4, 0:2], ACT.Exp)
                        if kind == "mla" and h >= 4:
                            full(act, (kind, "t", h - 4, 0))
                        for t in range(TT):
                            o = probs(kind, h)[:, nk * t:nk * t + nk]
                            src = bk((kind, "s", h))[:, 256 * t:256 * t + 256] if kind == "mla" else o
                            ins = a.activation(o, src, ACT.Exp, bias=att[:, h % 4, 2 + t:3 + t],
                                               scale=96 ** -0.5 if kind == "mla" else 1.0,
                                               accum_out=att[:, h % 4, 4 + t:5 + t])
                        if kind == "mla":
                            emptied(ins, (kind, "s", h))
                        else:
                            ins.then_inc(S(kind + "_exp"), 1)
                    for f in FILL.get((kind, i), []):
                        ada_quarters(*f)
                    for h in (2 * i, 2 * i + 1):
                        for j in range(nk // 256):
                            full(act, (kind, "t", h, j))
                            emptied(a.copy(pT[:, h % 2, 512 * j:512 * j + 512], bk((kind, "t", h, j))[:, :]), (kind, "t", h, j))

            attention("na")
            attention("mla")
            squares("sq2", 256, lambda k: ("wo", k))
            root(1, rstd, "n2", 256)
            shifts("h2", 256, lambda k, s: mod1[:, 24 + k:25 + k])
            for t in range(TT):
                full(act, ("rt", t))
                emptied(a.activation(lg[:, t, :], bk(("rt", t))[:, 0:64], ACT.Sigmoid), ("rt", t))
            for gg in range(4):
                w0, t = 512 * (gg % 2), gg // 2
                full(act, ("tk", gg))
                a.copy(hbf[:, 0, t, w0:w0 + 512], bk(("tk", gg))[:, :]).then_inc(S("part_a"), 1)
                act.wait_ge(S("rest_a"), gg + 1)
                a.copy(hbf[:, 1, t, w0:w0 + 512], htok[:, gg % 2, :]).then_inc(S("part_b"), 1)
            for t in range(2):
                full(act, ("shg", t))
                emptied(a.activation(shg[:, t, :], bk(("shg", t))[:, 0:256], ACT.Silu), ("shg", t))

            def gathered(n, u):
                act.wait_ge(S("g_full"), n + 1)
                a.copy(xg[:, u, :], bank[B_G][:, :]).then_inc(S("xg_copied"), 1)

            def pair(m):
                act.wait_ge(S("gu_full"), m + 1)
                a.activation(sgt, bank[B_GU][:, 0:FF], ACT.Silu).then_inc(S("silu_made"), 1)
                for u in range(UN):
                    gathered(UN * m + (UN + u), u)
                act.wait_ge(S("d_full"), m + 1)
                a.copy(yo[:, 0:512], bank[B_D][:, :])
                a.copy(yo[:, 512:1024], bank[B_D + 1][:, :]).then_inc(S("y_copied"), 1)

            for u in range(UN):
                gathered(u, u)
            with act.Fori(0, PAIRS) as m:
                pair(m)
            act.wait_ge(S("listed"), 1)
            more = act.value_load(more_i[0:1, 0:1], min_val=0, max_val=MORE // UN)
            with act.If(more > 0):
                with act.Fori(0, more) as m:
                    pair(m + PAIRS)
            for b in (1, 3):
                full(act, ("sums", b))
                emptied(a.copy(acc[:, b // 2, 512 * (b % 2):512 * (b % 2) + 512], bank[b][:, :]), ("sums", b))

            act.wait_ge(S("ctx_in"), 16)
            squares("sq3", 512, lambda k: ("ac", 2 + k // 4))
            root(1, rstd, "n3", 512)
            shifts("h3", 512, lambda k, s: mod2[:, k, s:s + 1])
            for s in range(2):
                for t in range(4):
                    full(act, (f"vab{s}", t))
                    emptied(a.copy(vtok[:, t, 256 * s:256 * s + 256], bk((f"vab{s}", t))[:, 0:256]), (f"vab{s}", t))
            root(1, bn[:, :, 13], "v", 4)
            for s in range(8):
                for t in range(2):
                    at = (12, 4, 0, 8)[s // 2] + 2 * (s % 2) + t
                    full(act, (f"z{s}", t))
                    f = (ACT.Copy, ACT.Silu, ACT.Copy, ACT.Silu)[s // 2]
                    emptied(a.activation(zT[:, at, :], bk((f"z{s}", t))[:, :], f), (f"z{s}", t))
            for n in range(8):
                full(act, ("fa", n))
                if n >= 2:
                    full(act, ("fb", n - 2))
                emptied(a.copy(fa[:, n % 2, :], bk(("fa", n))[:, :]), ("fa", n))
            squares("sq4", 512, lambda k: ("oab", k))
            root(1, rstd, "n4", 512)
            shifts("h4", 512, lambda k, s: mod2[:, 24 + k, s:s + 1])
            for t in range(2):
                full(act, ("k2", t))
                emptied(a.copy(k2[:, t, :], bk(("k2", t))[:, :]), ("k2", t))
            for t in range(4):
                full(act, ("v2", t))
                emptied(a.copy(v2[:, t, :], bk(("v2", t))[:, 0:256]), ("v2", t))
            for s in range(4):
                for t in range(2):
                    full(act, (f"q2{s}", t))
                    emptied(a.copy(q2[:, 2 * s + t, :], bk((f"q2{s}", t))[:, 0:256]), (f"q2{s}", t))
            for s in range(4):
                for t in range(2):
                    full(act, (f"g2{s}", t))
                    emptied(a.activation(g2s[:, 2 * s + t, :], bk((f"g2{s}", t))[:, 0:256], ACT.Silu), (f"g2{s}", t))

            attention("c")
            squares("sq5", 256, lambda k: ("oc", k))
            root(1, rstd, "n5", 256)
            for k in range(KT):
                act.wait_ge(S("y_out"), k + 1)
                act.dma_start(out_d[:, k, :], outT[:, k, :]).then_inc(S("stored_out"), 16)
            act.wait_ge(S("stored_out"), 16 * KT)

        @block.vector
        def _(dve):
            v = nc.vector
            steps = [0]
            signals = [0]

            def link(ins):
                steps[0] += 1
                ins.then_inc(S("dve_step"), 1)
                dve.wait_ge(S("dve_step"), steps[0])

            def signal(name):
                signals[0] += 1
                v.tensor_copy(mark[0:1, signals[0]:signals[0] + 1], mark[0:1, 0:1]).then_inc(S(name), 1)

            def bc(ap, *dims):
                return bass.AP(ap.tensor, ap.offset, [list(ap.ap[0])] + [list(d) for d in dims])

            def ada(which, j):
                full(dve, (which, j))
                o = bk((which, j))
                if which == "ada1":
                    emptied(v.tensor_tensor(mod1[:, 2 * j:2 * j + 2], o[:, 0:2], vv("b_ada", 2 * j, 2 * j + 2), ALU.add), (which, j))
                else:
                    b = vv("b2", 2 * j, 2 * j + 2)
                    emptied(v.tensor_tensor(mod2[:, 2 * j:2 * j + 2, :], o[:, 0:4].rearrange("p (a b) -> p a b", a=2),
                                            bc(b, [1, 2], [0, 2]), ALU.add), (which, j))

            def rms(tag, name, width, cols, dst, parts=P):
                full(dve, name)
                emptied(v.tensor_scalar(dst[0:parts, 0:cols], bk(name)[0:parts, 0:cols], 1.0 / width, EPS, ALU.mult, ALU.add), name)
                done(dve, name)
                signal(tag + "_ms")
                dve.wait_ge(S(tag + "_rt"), 1)
                link(v.reciprocal(dst[0:parts, 0:cols], dst[0:parts, 0:cols]))

            def scale_tiles(tag, cols, gain):
                for k in range(KT):
                    for s in range(cols // 256):
                        v.scalar_tensor_tensor(out=hT[:, k, 256 * s:256 * s + 256], in0=xT[:, k, 256 * s:256 * s + 256],
                                               scalar=gain(k, s), in1=rstd[:, 256 * s:256 * s + 256],
                                               op0=ALU.mult, op1=ALU.mult).then_inc(S(tag + "_scaled"), 1)

            link(v.memset(mark[:], 0.0))
            dve.wait_ge(S("const_in"), 48)
            pf, an, tn = pr[0:96, 0, 0:256], pr[0:96, 0, 256:512], pr[0:96, 0, 512:768]
            sn, co = sqt[0:96, 0, 0:256], sqt[0:96, 1, 0:256]
            link(v.tensor_copy(pf, stat[0:96, 0:256].bitcast(I32)))
            link(v.tensor_scalar(an, pf, cc("invf")[0:96, :], None, ALU.mult))
            MAGIC = 12582912.0
            link(v.tensor_scalar(tn, an, 1.0 / TWO_PI, MAGIC, ALU.mult, ALU.add))
            link(v.tensor_scalar(tn, tn, -MAGIC, None, ALU.add))
            C1 = 6.28125
            C2 = float(np.float32(np.round((TWO_PI - C1) * 2 ** 20) / 2 ** 20))
            C3 = float(TWO_PI - C1 - C2)
            for c in (C1, C2, C3):
                link(v.scalar_tensor_tensor(out=an, in0=tn, scalar=-c, in1=an, op0=ALU.mult, op1=ALU.add))
            LIM = 3.1415925
            link(v.tensor_scalar(sn, an, LIM, -LIM, ALU.min, ALU.max))
            link(v.tensor_scalar(an, an, float(np.pi / 2), None, ALU.add))
            link(v.tensor_scalar(tn, an, float(np.pi), -TWO_PI, ALU.is_gt, ALU.mult))
            link(v.tensor_tensor(an, an, tn, ALU.add))
            v.tensor_scalar(co, an, LIM, -LIM, ALU.min, ALU.max).then_inc(S("angle"), 1)

            rms("n1", "sum1", D, 256, rstd)
            for j in range(8):
                ada("ada1", j)
            done(dve, ("ada1", 6))
            done(dve, ("ada1", 7))
            link(v.scalar_tensor_tensor(out=gs[:, :, 0], in0=mod1[:, 8:16], scalar=1.0, in1=vv("g1"), op0=ALU.add, op1=ALU.mult))
            scale_tiles("h1", 256, lambda k, s: gs[:, k, 0:1])
            for j in range(8):
                full(dve, ("qkn", j))
                emptied(v.tensor_scalar(pr[:, j // 4, 256 * (j % 4):256 * (j % 4) + 256], bk(("qkn", j))[:, 0:256],
                                        1.0 / 64, EPS, ALU.mult, ALU.add), ("qkn", j))
            full(dve, "sum_ql")
            emptied(v.tensor_scalar(stat[:, 0:256], bk("sum_ql")[:, 0:256], 1.0 / 256, EPS, ALU.mult, ALU.add), "sum_ql")
            full(dve, "sum_kvl")
            emptied(v.tensor_scalar(stat[:, 256:512], bk("sum_kvl")[:, 0:256], 1.0 / 128, EPS, ALU.mult, ALU.add), "sum_kvl")
            done(dve, "sum_kvl")
            done(dve, "sum_ql")
            signal("lt_ms")
            signal("qk_ms")
            dve.wait_ge(S("lt_rt"), 1)
            link(v.reciprocal(stat[:, :], stat[:, :]))
            for t in range(2):
                done(dve, ("ql", t))
                v.scalar_tensor_tensor(out=lat[:, t, :], in0=lat[:, t, :], scalar=vv("gql", t, t + 1), in1=stat[:, 0:256],
                                       op0=ALU.mult, op1=ALU.mult).then_inc(S("qln"), 1)
            done(dve, "kvl")
            v.scalar_tensor_tensor(out=lat[:, 2, :], in0=lat[:, 2, :], scalar=vv("gkv"), in1=stat[:, 256:512],
                                   op0=ALU.mult, op1=ALU.mult).then_inc(S("kvn"), 1)
            dve.wait_ge(S("qk_rt"), 1)
            prf = pr[:, :, :].rearrange("p a b -> p (a b)")
            link(v.reciprocal(prf, prf))
            for j in range(8):
                done(dve, (f"qk{j // 2}", j % 2))
                g = vv("gq") if j < 4 else vv("gk")
                v.scalar_tensor_tensor(out=qk[:, j, :], in0=qk[:, j, :], scalar=g, in1=prf[:, 256 * j:256 * j + 256],
                                       op0=ALU.mult, op1=ALU.mult).then_inc(S("qk_ready"), 1)
            def normalise(kind, h, nk):
                mx = att[:, h % 4, :]
                link(v.reciprocal(mx[:, 4:6], mx[:, 4:6]))
                for t in range(TT):
                    o = probs(kind, h)[:, nk * t:nk * t + nk]
                    last = v.tensor_scalar(o, o, mx[:, 4 + t:5 + t], None, ALU.mult)
                last.then_inc(S(kind + "_probs"), 1)

            def pair_out(kind, i, dst):
                full(dve, (kind, "o", i))
                emptied(v.tensor_copy(dst, bk((kind, "o", i))[:, 0:256]), (kind, "o", i))

            ada_prev = [None]

            def ada_folds(key):
                for f in FILL[key]:
                    if ada_prev[0]:
                        ada(*ada_prev[0])
                    ada_prev[0] = f

            for gg in range(4):
                full(dve, ("qsw", gg))
                t2 = pT[0:96, gg % 2, 0:512]
                rs = bc(rope_s[0:96, :], [0, 2], [1, 256])
                if gg == 0:
                    dve.wait_ge(S("rope_tab"), 1)
                emptied(v.tensor_tensor(t2.rearrange("p (a b) -> p a b", a=2),
                                        bk(("qsw", gg))[0:96, :].rearrange("p (a b) -> p a b", a=2), rs, ALU.mult), ("qsw", gg))
                done(dve, ("qsw", gg))
                dve.wait_ge(S("q_cos"), gg + 1)
                q = qm[0:96, 2 * gg:2 * gg + 2, :].rearrange("p a b -> p (a b)")
                v.tensor_tensor(q, q, t2, ALU.add).then_inc(S("m_in"), 1)
            full(dve, "ksw")
            t2 = pT[0:96, 0, 512:768]
            emptied(v.tensor_tensor(t2, bk("ksw")[0:96, 0:256], rope_s[0:96, :], ALU.mult), "ksw")
            link(v.tensor_tensor(lat[0:96, 3, :], lat[0:96, 3, :], rope_c[0:96, :], ALU.mult))
            done(dve, "ksw")
            link(v.tensor_tensor(lat[0:96, 3, :], lat[0:96, 3, :], t2, ALU.add))
            for gg in range(4):
                done(dve, ("uk", gg))
                for h in range(2):
                    last = v.tensor_copy(km[64:96, 2 * gg + h, :], lat[64:96, 3, :])
                last.then_inc(S("m_in"), 1)
            def mean_of(which, gg):
                if which == 0:
                    return varq[:, 2 * gg:2 * gg + 2, :]
                return pT[0:96, gg // 2, 512 * (gg % 2):512 * (gg % 2) + 512].rearrange("p (a b) -> p a b", a=2)

            for gg in range(8):
                full(dve, ("msum", gg))
                dst = mean_of(gg // 4, gg % 4)
                emptied(v.tensor_scalar(dst, bk(("msum", gg))[0:96, :].rearrange("p (a b) -> p a b", a=2), 1.0 / 96, EPS, ALU.mult, ALU.add), ("msum", gg))
                if gg % 4 == 3:
                    done(dve, ("msum", gg))
                    done(dve, ("msum", gg - 1))
                    signal(("mq" if gg < 4 else "mk") + "_ms")

            def latent_norm(gg):
                for n, (tag, dst, g) in enumerate((("mq", qm, "gmq"), ("mk", km, "gmk"))):
                    if gg == 0:
                        dve.wait_ge(S(tag + "_rt"), 1)
                    r = mean_of(n, gg)
                    link(v.reciprocal(r, r))
                    o = dst[0:96, 2 * gg:2 * gg + 2, :]
                    v.scalar_tensor_tensor(out=o, in0=o, scalar=vv(g)[0:96, :], in1=r,
                                           op0=ALU.mult, op1=ALU.mult).then_inc(S("m_ready"), 1)

            for gg in range(4):
                latent_norm(gg)

            def na_scores(h):
                if h >= 4:
                    full(dve, ("na", "t", h - 4, 0))
                full(dve, ("na", "s", h))
                dve.wait_ge(S("bias_made"), 2 * h + 2)
                emptied(v.scalar_tensor_tensor(out=probs("na", h), in0=bk(("na", "s", h))[:, :], scalar=0.125,
                                               in1=bmask[:, h % 2, :], op0=ALU.mult, op1=ALU.add), ("na", "s", h))
                done(dve, ("na", "s", h))
                link(v.tensor_reduce(att[:, h % 4, 0:2], probs("na", h).rearrange("p (a b) -> p a b", a=2), AXX, ALU.max))
                v.tensor_scalar(att[:, h % 4, 2:4], att[:, h % 4, 0:2], -1.0, None, ALU.mult).then_inc(S("na_negmax"), 1)

            na_scores(0)
            na_scores(1)
            for i in range(4):
                for h in (2 * i, 2 * i + 1):
                    dve.wait_ge(S("na_exp"), h + 1)
                    normalise("na", h, 256)
                if i < 3:
                    na_scores(2 * i + 2)
                    na_scores(2 * i + 3)
                ada_folds(("na", i))
                if i >= 1:
                    pair_out("na", i - 1, yT[:, i - 1, :])
            pair_out("na", 3, yT[:, 3, :])

            def mla_scores(h):
                full(dve, ("mla", "s", h))
                link(v.tensor_reduce(att[:, h % 4, 0:2], bk(("mla", "s", h))[:, :].rearrange("p (a b) -> p a b", a=2), AXX, ALU.max))
                v.tensor_scalar(att[:, h % 4, 2:4], att[:, h % 4, 0:2], -(96 ** -0.5), None, ALU.mult).then_inc(S("mla_negmax"), 1)

            mla_scores(0)
            mla_scores(1)
            for i in range(4):
                for h in (2 * i, 2 * i + 1):
                    done(dve, ("mla", "s", h))
                    normalise("mla", h, 256)
                if i < 3:
                    mla_scores(2 * i + 2)
                    mla_scores(2 * i + 3)
                ada_folds(("mla", i))
                if i >= 1:
                    pair_out("mla", i - 1, yT[:, 4 + i - 1, :])
            ada(*ada_prev[0])
            pair_out("mla", 3, yT[:, 7, :])
            dve.wait_ge(S("mod1_made"), 1)
            for d in range(8):
                full(dve, ("pn", d))
                full(dve, ("pm", d))
                t1, t2 = sqt[:, d % 2, 0:256], sqt[:, d % 2, 256:512]
                emptied(v.tensor_tensor(t1, bk(("pn", d))[:, 0:256], sgate[:, d, :], ALU.mult), ("pn", d))
                emptied(v.tensor_tensor(t2, bk(("pm", d))[:, 0:256], sgate[:, 8 + d, :], ALU.mult), ("pm", d))
                done(dve, ("pn", d))
                done(dve, ("pm", d))
                v.tensor_tensor(merged[:, d, :], t1, t2, ALU.add).then_inc(S("merged"), 1)

            def residual(name, d, lo, hi, gate, src=None):
                return v.scalar_tensor_tensor(out=xT[:, d, lo:hi], in0=bk(name)[:, lo:hi] if src is None else src, scalar=gate,
                                              in1=xT[:, d, lo:hi], op0=ALU.mult, op1=ALU.add)

            for d in range(8):
                full(dve, ("wo", d))
                emptied(residual(("wo", d), d, 0, 256, mod1[:, 16 + d:17 + d]), ("wo", d))
            done(dve, ("wo", 6))
            done(dve, ("wo", 7))
            signal("x1")
            link(v.scalar_tensor_tensor(out=gs[:, :, 0], in0=mod1[:, 32:40], scalar=1.0, in1=vv("g2"), op0=ALU.add, op1=ALU.mult))
            rms("n2", "sum2", D, 256, rstd)
            scale_tiles("h2", 256, lambda k, s: gs[:, k, 0:1])
            for t in range(TT):
                done(dve, ("rt", t))
            link(v.tensor_tensor(sel, lg, bc(vv("ebias"), [0, 2], [1, 64]), ALU.add))
            for t in range(TT):
                for g in range(GROUPS):
                    last = v.max(m8[:, t, g, :], sel[:, t, 8 * g:8 * g + 8])
            link(last)
            link(v.tensor_tensor(gsc, m8[:, :, :, 0], m8[:, :, :, 1], ALU.add))
            for t in range(TT):
                a0 = bc(gsc[:, t, :], [0, 8], [1, 8])
                a1 = bc(gsc[:, t, :], [1, 8], [0, 8])
                v.tensor_tensor(cmpa[:, t], a0, a1, ALU.is_gt)
                last = v.tensor_tensor(cmpb[:, t], a0, a1, ALU.is_equal)
            link(last)
            for t in range(TT):
                last = v.tensor_tensor(cmpb[:, t], cmpb[:, t], cc("gtri").rearrange("p (a b) -> p a b", a=8), ALU.mult)
            link(last)
            link(v.tensor_tensor(small[:, 400:528], small[:, 400:528], small[:, 528:656], ALU.add))
            link(v.tensor_reduce(small[:, 656:672], small[:, 400:528].rearrange("p (g b) -> p g b", b=8), AXX, ALU.add))
            link(v.tensor_scalar(small[:, 656:672], small[:, 656:672], float(TOPG) - 0.5, None, ALU.is_lt))
            link(v.tensor_scalar(small[:, 672:688], small[:, 656:672], -1.0, -NEG, ALU.add, ALU.mult))
            selg8 = small[:, 128:256].rearrange("p (g b) -> p g b", b=8)
            link(v.tensor_tensor(selg8, selg8, bc(small[:, 656:672], [1, 16], [0, 8]), ALU.mult))
            link(v.tensor_tensor(selg8, selg8, bc(small[:, 672:688], [1, 16], [0, 8]), ALU.add))
            for t in range(TT):
                last = v.max(top[:, t, :], sel[:, t, :])
            link(last)
            for t in range(TT):
                last = v.match_replace(out=rep[:, t, :], in_to_replace=top[:, t, :], in_values=sel[:, t, :], imm_value=-3e38)
            link(last)
            v.tensor_tensor(mask, rep, sel, ALU.not_equal).then_inc(S("mask"), 1)
            dve.wait_ge(S("mask"), 1)
            link(v.memset(gatx, 0.0))
            link(v.tensor_tensor(gatx[:, :, 0:64], lg, mask, ALU.mult))
            link(v.tensor_reduce(den[:, 2:4], gatx[:, :, 0:64], AXX, ALU.add))
            link(v.reciprocal(den[:, 2:4], den[:, 2:4]))
            for t in range(TT):
                last = v.tensor_scalar(gatx[:, t, 0:64], gatx[:, t, 0:64], den[:, 2 + t:3 + t], 2.5, ALU.mult, ALU.mult)
            link(last)
            for t in range(TT):
                v.tensor_copy(gatx[:, t, E:NONE].rearrange("p (a b) -> p a b", a=ROUNDS - 1), bc(gatx[:, t, 0:64], [0, ROUNDS - 1], [1, 64]))
            v.memset(yo[:, 0:256], 0.0).then_inc(S("zeros"), 1)
            for gg in range(4):
                w0, t = 512 * (gg % 2), gg // 2
                dve.wait_ge(S("part_a"), gg + 1)
                v.tensor_tensor(htok[:, gg % 2, :], bk(("tk", gg))[:, :], hbf[:, 0, t, w0:w0 + 512], ALU.subtract).then_inc(S("rest_a"), 1)
                dve.wait_ge(S("part_b"), gg + 1)
                emptied(v.tensor_tensor(hbf[:, 2, t, w0:w0 + 512], htok[:, gg % 2, :], hbf[:, 1, t, w0:w0 + 512], ALU.subtract), ("tk", gg))
            for t in range(2):
                full(dve, ("shu", t))
                done(dve, ("shg", t))
                emptied(v.tensor_tensor(shu[:, t, :], bk(("shu", t))[:, 0:256], shg[:, t, :], ALU.mult), ("shu", t))
            done(dve, ("shu", 0))
            done(dve, ("shu", 1))
            signal("sh_act")
            link(v.memset(posx, -1.0))
            full(dve, "pos")
            v.tensor_copy(counts, bk("pos")[:, 128:192])
            emptied(v.scalar_tensor_tensor(out=pos1, in0=bk("pos")[:, 0:128].rearrange("p (a b) -> p a b", a=2), scalar=1.0,
                                           in1=mask, op0=ALU.add, op1=ALU.mult), "pos")
            done(dve, "pos")
            for r in range(ROUNDS):
                last = v.tensor_scalar(posx[:, :, E * r:E * r + E], pos1, -1.0 - SLOTS * r, None, ALU.add)
            link(last)

            def pick(code, u):
                for t in range(TT):
                    last = v.tensor_scalar(selb[:, u, t, :], cc("iota"), posx[:, t, bass.ds(code, 1)], None, ALU.is_equal)
                last.then_inc(S("sel_made"), 1)

            def pick_gates(code, u):
                for t in range(TT):
                    last = v.tensor_scalar(selg[:, t, SLOTS * u:SLOTS * u + SLOTS], cc("iota"), posx[:, t, bass.ds(code, 1)],
                                           gatx[:, t, bass.ds(code, 1)], ALU.is_equal, ALU.mult)
                if u == UN - 1:
                    last.then_inc(S("selg_made"), 1)

            def pair(m, code1, code2):
                dve.wait_ge(S("gu_full"), m + 1)
                dve.wait_ge(S("silu_made"), m + 1)
                v.tensor_tensor(hid, bank[B_GU][:, FF:2 * FF], sgt, ALU.mult).then_inc(S("hid_made"), 1)
                dve.wait_ge(S("x_full"), m + 1)
                v.tensor_copy(aT[:, :, :].rearrange("p a b -> p (a b)"), bank[B_D][:, 0:2 * P])
                v.tensor_copy(selT[:, :, :].rearrange("p a b -> p (a b)"), bank[B_D][:, 2 * P:4 * P]).then_inc(S("selT_copied"), 1)
                for u in range(UN):
                    pick_gates(code1(u), u)
                dve.wait_ge(S("g_full"), UN * m + 4)
                for u in range(UN):
                    pick(code2(u), u)

            for u in range(UN):
                pick(u, u)
            for u in range(UN):
                pick_gates(u, u)
            dve.wait_ge(S("g_full"), UN)
            for u in range(UN):
                pick(UN + u, u)
            for r in range(1, ROUNDS):
                last = v.scalar_tensor_tensor(out=keys[:, E * (r - 1):E * r], in0=counts, scalar=SLOTS * r + 0.5,
                                              in1=cc("codes", E * (r - 1), E * r), op0=ALU.is_gt, op1=ALU.mult)
            link(last)
            link(v.memset(klist, 0.0))
            for m in range(MORE // 8):
                link(v.max(klist[:, 8 * m:8 * m + 8], keys))
                if m < MORE // 8 - 1:
                    link(v.match_replace(out=keys, in_to_replace=klist[:, 8 * m:8 * m + 8], in_values=keys, imm_value=0.0))
            link(v.tensor_scalar(clist, klist, -1.0, float(NONE), ALU.mult, ALU.add))
            link(v.tensor_scalar(elist, clist, -float(E), None, ALU.add))
            for r in range(2, ROUNDS + 1):
                link(v.tensor_scalar(lcmp, clist, E * r - 0.5, float(E), ALU.is_gt, ALU.mult))
                link(v.tensor_tensor(elist, elist, lcmp, ALU.subtract))
            link(v.tensor_scalar(lcmp, klist, 0.5, None, ALU.is_gt))
            link(v.tensor_reduce(more_f, bc(lcmp, [UN, MORE // UN]), AXX, ALU.add))
            v.tensor_copy(more_i, more_f)
            v.tensor_copy(codes, clist)
            link(v.tensor_copy(whose, elist))
            signal("listed")

            with dve.Fori(0, PAIRS - 2) as m:
                pair(m, lambda u: UN * m + (UN + u), lambda u: UN * m + (2 * UN + u))
            dve.wait_ge(S("listed"), 1)

            def later(at):
                return dve.value_load(codes[0:1, bass.ds(at, 1)], min_val=0, max_val=NONE)

            pair(PAIRS - 2, lambda u: E - UN + u, lambda u: later(u))
            pair(PAIRS - 1, lambda u: later(u), lambda u: later(UN + u))
            more = dve.value_load(more_i[0:1, 0:1], min_val=0, max_val=MORE // UN)
            with dve.If(more > 0):
                with dve.Fori(0, more) as m:
                    pair(m + PAIRS, lambda u: later(UN * m + (UN + u)), lambda u: later(UN * m + (2 * UN + u)))
            for b in (0, 2):
                full(dve, ("sums", b))
                emptied(v.tensor_copy(acc[:, b // 2, 512 * (b % 2):512 * (b % 2) + 512], bank[b][:, :]), ("sums", b))
            for g in range(4):
                t, hf = g // 2, g % 2
                full(dve, ("ac", g))
                for k in range(4):
                    d = 4 * hf + k
                    last = residual(None, d, P * t, P * t + P, mod1[:, 40 + d:41 + d], src=bk(("ac", g))[:, P * k:P * k + P])
                emptied(last, ("ac", g))
            done(dve, ("ac", 2))
            done(dve, ("ac", 3))

            def gains(layer):
                g = vv("ng2", 8 * layer, 8 * layer + 8)
                link(v.scalar_tensor_tensor(out=gs[:, :, :], in0=mod2[:, 24 * layer + 8:24 * layer + 16, :], scalar=1.0,
                                            in1=bc(g, [1, 8], [0, 2]), op0=ALU.add, op1=ALU.mult))

            done(dve, ("ada2", 23))
            dve.wait_ge(S("const2_in"), 32)
            gains(0)
            rms("n3", "sum3", D, 512, rstd)
            scale_tiles("h3", 512, lambda k, s: gs[:, k, s:s + 1])
            for t in range(4):
                for s in range(2):
                    done(dve, (f"vab{s}", t))
                link(v.bn_stats(bn[:, t, 0:6], vtok[:, t, :]))
                link(v.bn_aggr(bn[:, t, 12:14], bn[:, t, 0:6]))
            link(v.tensor_scalar(bn[:, :, 13], bn[:, :, 13], EPS, None, ALU.add))
            signal("v_ms")
            dve.wait_ge(S("v_rt"), 1)
            link(v.reciprocal(bn[:, :, 13], bn[:, :, 13]))
            for t in range(4):
                v.tensor_scalar(vtok[:, t, :], vtok[:, t, :], bn[:, t, 12:13], bn[:, t, 13:14],
                                ALU.subtract, ALU.mult).then_inc(S("v_norm"), 1)
            for n in range(8):
                g, st = n // 2, n % 2
                full(dve, ("fb", n))
                done(dve, (f"z{2 + g // 2}", g % 2))
                z = zT[:, 4 + g, 256 * st:256 * st + 256]
                emptied(v.tensor_tensor(z, z, bk(("fb", n))[:, 0:256], ALU.mult), ("fb", n))
            for h in range(4):
                full(dve, ("sp", h))
                t1 = smt[:, h % 2, :]
                emptied(v.scalar_tensor_tensor(out=t1.rearrange("p (a b) -> p a b", a=4),
                                               in0=bk(("sp", h))[:, :].rearrange("p (a b) -> p a b", a=4), scalar=vv("vg", h, h + 1),
                                               in1=bc(vv("sb", P * h, P * h + P), [0, 4], [1, P]), op0=ALU.mult, op1=ALU.add), ("sp", h))
                done(dve, ("sp", h))
                done(dve, (f"z{4 + h // 2}", h % 2))
                done(dve, (f"z{6 + h // 2}", h % 2))
                link(v.tensor_tensor(t1, t1, zT[:, 8 + h, :], ALU.mult))
                v.tensor_tensor(zT[:, h, :], zT[:, h, :], t1, ALU.mult).then_inc(S("y_a"), 1)
            for d in range(8):
                full(dve, ("oab", d))
                residual(("oab", d), d, 0, 256, mod2[:, 16 + d, 0:1])
                emptied(residual(("oab", d), d, 256, 512, mod2[:, 16 + d, 1:2]), ("oab", d))
            done(dve, ("oab", 6))
            done(dve, ("oab", 7))
            gains(1)
            rms("n4", "sum4", D, 512, rstd)
            scale_tiles("h4", 512, lambda k, s: gs[:, k, s:s + 1])
            for j in range(10):
                full(dve, ("sw", j))
                src = k2[:, j, 0:256] if j < 2 else q2[:, j - 2, :]
                t1, t2 = rt1[:, j % 4, :], rt2[:, j % 4, :]
                emptied(v.tensor_tensor(t1, bk(("sw", j))[:, 0:256], cc("sin2"), ALU.mult), ("sw", j))
                link(v.tensor_tensor(t2, src, cc("cos2"), ALU.mult))
                done(dve, ("sw", j))
                v.tensor_tensor(src, t1, t2, ALU.add).then_inc(S("rope2"), 1)

            def c_scores(h):
                if h >= 4:
                    for j in range(2):
                        full(dve, ("c", "t", h - 4, j))
                for t in range(TT):
                    full(dve, ("c", "s", h, t))
                    emptied(v.scalar_tensor_tensor(out=probs("c", h)[:, 512 * t:512 * t + 512], in0=bk(("c", "s", h, t))[:, :], scalar=0.125,
                                                   in1=cc("wmask", 512 * t, 512 * t + 512), op0=ALU.mult, op1=ALU.add), ("c", "s", h, t))
                for t in range(TT):
                    done(dve, ("c", "s", h, t))
                a = att[:, h % 4, :]
                sink = bc(vv("sink", h, h + 1), [0, 2])
                link(v.tensor_reduce(a[:, 0:2], probs("c", h).rearrange("p (a b) -> p a b", a=2), AXX, ALU.max))
                link(v.tensor_tensor(a[:, 0:2], a[:, 0:2], sink, ALU.max))
                link(v.tensor_scalar(a[:, 2:4], a[:, 0:2], -1.0, None, ALU.mult))
                v.tensor_tensor(a[:, 0:2], sink, a[:, 2:4], ALU.add).then_inc(S("c_negmax"), 1)

            def c_out(i):
                full(dve, ("c", "o", i))
                done(dve, (f"g2{i // 2}", i % 2))
                emptied(v.tensor_tensor(o2[:, i, :], bk(("c", "o", i))[:, 0:256], g2s[:, i, :], ALU.mult), ("c", "o", i))

            c_scores(0)
            c_scores(1)
            for i in range(8):
                for h in (2 * i, 2 * i + 1):
                    dve.wait_ge(S("c_exp"), h + 1)
                    a = att[:, h % 4, :]
                    link(v.tensor_tensor(a[:, 4:6], a[:, 4:6], a[:, 6:8], ALU.add))
                    normalise("c", h, 512)
                if i < 7:
                    c_scores(2 * i + 2)
                    c_scores(2 * i + 3)
                if i >= 1:
                    c_out(i - 1)
            c_out(7)
            for d in range(8):
                full(dve, ("oc", d))
                emptied(residual(("oc", d), d, 0, 256, mod2[:, 40 + d, 0:1]), ("oc", d))
            done(dve, ("oc", 6))
            done(dve, ("oc", 7))
            rms("n5", "sum5", D, 256, rstd)
            for k in range(KT):
                v.scalar_tensor_tensor(out=outT[:, k, :], in0=xT[:, k, 0:256], scalar=vv("fg", k, k + 1), in1=rstd[:, 0:256],
                                       op0=ALU.mult, op1=ALU.mult).then_inc(S("y_out"), 1)


SLAB_COUNTS = dict(ada1=24, ada2=24, uq=1, ukv=1, pna=2, pmla=2, out=4, shg=1, shu=1, shd=1, ab=10, oab=4, cin=10, oc=4)
SLAB_COUNTS["in"] = 16
slabs_at, _n = {}, 0
for _k, _c in SLAB_COUNTS.items():
    slabs_at[_k] = _n
    _n += _c


def shape_constants():
    c, c2 = np.zeros((P, C_W), np.float64), np.zeros((P, C2_W), np.float64)

    def put(name, a):
        to, (lo, hi) = (c, C_AT[name]) if name in C_AT else (c2, C2_AT[name])
        a = np.asarray(a, np.float64)
        to[:a.shape[0], lo:hi] = a.reshape(a.shape[0], -1)

    i = np.arange(P)
    put("ident", np.eye(P))
    put("fold", np.stack([i % 32 == 0, i % 32 == 1], 1))
    put("bones", (i[:, None] // 64) == (i[None, :] // 64))
    m = np.zeros((96, 96))
    for r in range(16):
        m[80 + r, 64 + r] = -1.0
        m[64 + r, 80 + r] = 1.0
    put("perm96", m)
    m = np.zeros((P, P))
    for blk in range(4):
        for r in range(16):
            m[32 * blk + 16 + r, 32 * blk + r] = -1.0
            m[32 * blk + r, 32 * blk + 16 + r] = 1.0
    put("perm128", m)
    put("tri", i[:, None] < i[None, :])
    put("iota", np.tile(np.arange(SLOTS), (P, 1)))
    ang = TWO_PI * np.outer(i, i) / P
    put("dft_c", np.concatenate([np.cos(ang), -np.sin(ang)], 1))
    t = np.arange(T)
    angl = TWO_PI * (np.outer(t, t) % T) / T
    norm = 1 / np.sqrt(T * P)
    lt = np.stack([np.cos(angl), np.sin(angl)], 1) * norm
    put("dft_l", lt.reshape(2, P, 2, T).transpose(1, 0, 2, 3))
    inv = 10000.0 ** (-np.arange(16) / 16)
    row, col = np.repeat(np.arange(4), 64), np.tile(np.arange(64), 4)
    d = i % 64
    a2 = np.where((d < 32)[:, None], row[None, :], col[None, :]) * inv[d % 16][:, None]
    put("cos2", np.cos(a2))
    put("sin2", np.sin(a2))
    q = (np.arange(2)[None, :, None] * P + i[:, None, None])
    k = np.arange(T)[None, None, :]
    put("wmask", np.concatenate([np.where(np.abs(q - k) <= 128, 0.0, NEG), np.zeros((P, 2, T))], 2))
    cq, ck = (i % 64)[:, None], np.arange(64)[None, :]
    st = np.clip(cq - 8, 0, 48)
    put("namask", np.where((ck >= st) & (ck < st + 16), 0.0, NEG))
    put("invf", np.concatenate([np.zeros(64), inv, inv])[:, None])
    g = np.arange(8)
    put("gtri", np.broadcast_to((g[None, :] < g[:, None]).reshape(1, 64), (P, 64)))
    put("codes", np.broadcast_to(NONE - (E + np.arange((ROUNDS - 1) * E))[None, :], (P, (ROUNDS - 1) * E)))
    return c.astype(np.float32), c2.astype(np.float32)


def kernel(**inputs):
    import concourse.bacc as bacc
    from concourse.bass_utils import run_bass_kernel_spmd as run

    x = {k: np.asarray(v) for k, v in inputs.items()}

    def cols(a):
        return a.reshape(-1, P).T

    def rows(a):
        return np.broadcast_to(a.reshape(1, -1), (P, a.size))

    def pad96(a):
        return np.pad(a, (0, P - a.size))[:, None]

    c2 = np.stack([cols(x["c_2"][0]), cols(x["c_ctx_2"])], 2).reshape(P, 16)
    vec = dict(c=cols(x["c"][0]), c2=c2, b_ada=cols(x["b_ada"][0]), g1=cols(x["g_norm1"][0]),
               gq=np.tile(x["g_na_q"][0], 2)[:, None], gk=np.tile(x["g_na_k"][0], 2)[:, None],
               gql=cols(x["g_q_lat"][0]), gkv=cols(x["g_kv_lat"][0]), gmq=pad96(x["g_mla_q"][0]), gmk=pad96(x["g_mla_k"][0]),
               g2=cols(x["g_norm2"][0]), ng2=cols(x["norm_g_2"]), b2=cols(x["ada_b_2"]), vg=cols(x["v_norm_g_2"][0]),
               fg=cols(x["final_g_2"]), ebias=rows(x["e_bias"][0]), sb=rows(x["spatial_b_2"][0]))
    order = np.array([8 * (j // 8) + 4 * (j % 2) + (j % 8) // 2 for j in range(16)])
    vec["sink"] = rows(x["sink_logit_2"][0][order])
    vecs = np.concatenate([vec[k] for k in V_WIDTHS], 1)
    xT = np.concatenate([x["x"][0], x["ctx_2"][0]], 0).reshape(512, 8, P).transpose(2, 1, 0)

    def slab8(w):
        return w.reshape(8, P, -1, 256).transpose(2, 1, 0, 3).reshape(-1, P, SLAB)

    def slabk(w, k):
        w = w.reshape(k, P, -1, SLAB // k).transpose(2, 1, 0, 3)
        return w.reshape(-1, P, SLAB)

    w_in = np.pad(x["w_in"][0], ((0, 0), (0, 96)))
    w_in = np.concatenate([w_in[:, :1952], w_in[:, 4000:], w_in[:, 1952:4000]], 1)
    ukv = x["w_ukv"][0].reshape(P, 8, 2, 64).transpose(0, 2, 1, 3).reshape(P, 1024)
    ab = x["w_in_ab_2"][0]
    ab = np.concatenate([ab[:, 512:1024], ab[:, 1536:2048], ab[:, 2048:2560], ab[:, :512], ab[:, 1024:1536]], 1)
    cin = x["w_in_c_2"][0]
    by_head = lambda w: w.reshape(1024, 16, 64)[:, order].reshape(1024, 1024)
    cin = np.concatenate([cin[:, 1024:1536], by_head(cin[:, :1024]), by_head(cin[:, 1536:])], 1)
    oc = x["w_out_c_2"][0].reshape(16, 64, 1024)[order].reshape(1024, 1024)
    part = dict(ada1=slab8(x["w_ada"][0]), ada2=np.concatenate([slab8(x["ada_w_2"][0]), slab8(x["ada_w_2"][1])]),
                uq=np.pad(x["w_uq"][0].reshape(2, P, 768).transpose(1, 0, 2).reshape(1, P, 1536), ((0, 0), (0, 0), (0, 512))),
                ukv=np.pad(ukv, ((0, 0), (0, 1024)))[None],
                pna=slabk(x["w_proj_na"][0], 4), pmla=slabk(x["w_proj_mla"][0], 4), out=slab8(x["w_out"][0]),
                shg=slab8(x["w_sh_gate"][0]), shu=slab8(x["w_sh_up"][0]), shd=slabk(x["w_sh_down"][0], 2),
                ab=slab8(ab), oab=slab8(x["w_out_ab_2"][0]), cin=slab8(cin), oc=slab8(oc))
    part["in"] = slab8(w_in)
    stream = np.concatenate([part[k] for k in SLAB_COUNTS], 0)

    gu = np.stack([x["w_exp_gate"][0], x["w_exp_up"][0]], 2).reshape(E, 2, 4, P, 2 * FF)
    gu = gu.transpose(0, 1, 3, 2, 4).reshape(E, 2, P, SLAB)
    dn = x["w_exp_down"][0].reshape(E, 2, P, D).transpose(0, 2, 1, 3).reshape(E, 1, P, SLAB)
    experts = np.concatenate([gu, dn], 1)
    consts, consts2 = shape_constants()
    arrays = dict(
        xT=xT, consts=consts, consts2=consts2, vecs=vecs, positions=np.broadcast_to(x["positions"], (96, T)),
        rpb=x["na_rpb"][0][:, :, ::-1],
        spatial=x["spatial_w_2"][0].transpose(2, 0, 1), router=x["w_router"][0].reshape(8, P, E).transpose(1, 0, 2),
        stream=stream, experts=experts)
    arrays = {k: np.ascontiguousarray(v) for k, v in arrays.items()}
    nc = bacc.Bacc("TRN2", target_bir_lowering=False, num_devices=1)
    t = {k: nc.dram_tensor(k, v.shape, mybir.dt.from_np(v.dtype), kind="ExternalInput").ap() for k, v in arrays.items()}
    out = nc.dram_tensor("out", (P, KT, T), F32, kind="ExternalOutput").ap()
    build(nc, t["xT"], t["consts"], t["consts2"], t["vecs"], t["positions"], t["rpb"], t["spatial"], t["router"], t["stream"], t["experts"], out)
    r = run(nc, [arrays], core_ids=[0])
    return np.ascontiguousarray(r.results[0]["out"].transpose(2, 1, 0)).reshape(1, T, D)
```
